# Optimizing a Trainium2 kernel written in Bass

```python
import math
import jax, jax.numpy as jnp
from jax import lax
import numpy as np

D_MODEL = 1024
BATCH = 1
SEQ = 256
DEPTH = 2

N_META = 16
N_MIXERS = 2
N_A_LAYERS = (DEPTH + 1) // 2
N_B_LAYERS = DEPTH // 2

DA_HEADS = 8
DA_HEAD_DIM = D_MODEL // (2 * DA_HEADS)
DA_V_DIM = 2 * DA_HEAD_DIM
Q_BLOCK = 128
SUBLN_EPS = 1e-5

RW_HEAD_DIM = 64
RW_HEADS = D_MODEL // RW_HEAD_DIM
RW_DECAY_LORA = 64
RW_AAA_LORA = 64
RW_GATE_LORA = 160
RW_N_MIX = 6
RW_LNX_EPS = 64e-5

D_FF = 2816
N_EXPERTS = 8
TOP_K = 2
D_FF_EXPERT = 3584

LN_EPS = 1e-5
DEEPNORM_ALPHA = (2.0 * DEPTH) ** 0.25
DEEPNORM_BETA = (8.0 * DEPTH) ** -0.25


def layer_norm(x, g, b):
    xf = x.astype(jnp.float32)
    mu = jnp.mean(xf, -1, keepdims=True)
    var = jnp.mean(jnp.square(xf - mu), -1, keepdims=True)
    return ((xf - mu) * lax.rsqrt(var + LN_EPS) * g + b).astype(x.dtype)

def diff_attention(x, w_in, w_o, lq1, lk1, lq2, lk2, subln_g, layer_idx):
    B, L, D = x.shape
    H, Dh, Dv = DA_HEADS, DA_HEAD_DIM, DA_V_DIM
    Lp = -(-L // Q_BLOCK) * Q_BLOCK
    nblk = Lp // Q_BLOCK
    qkv = jnp.einsum('bld,de->ble', x, w_in)
    qkv = jnp.pad(qkv, ((0, 0), (0, Lp - L), (0, 0)))
    q, k, v = jnp.split(qkv, 3, axis=-1)
    q = q.reshape(B, Lp, H, 2, Dh)
    k = k.reshape(B, Lp, H, 2, Dh)
    vf = v.reshape(B, Lp, H, Dv).astype(jnp.float32)
    lam_init = 0.8 - 0.6 * math.exp(-0.3 * layer_idx)
    lam = (jnp.exp(jnp.sum(lq1 * lk1).astype(jnp.float32))
           - jnp.exp(jnp.sum(lq2 * lk2).astype(jnp.float32)) + lam_init)
    slopes = 2.0 ** (-(8.0 / H) * jnp.arange(1, H + 1, dtype=jnp.float32))
    kpos = jnp.arange(Lp, dtype=jnp.int32)
    kvalid = kpos < L
    scale = Dh ** -0.5
    qb = q.reshape(B, nblk, Q_BLOCK, H, 2, Dh).transpose(1, 0, 2, 3, 4, 5)
    starts = jnp.arange(nblk, dtype=jnp.int32) * Q_BLOCK

    def block(args):
        qblk, start = args
        s = jnp.einsum('bqhcd,bkhcd->bhcqk', qblk, k).astype(jnp.float32) * scale
        qpos = start + jnp.arange(Q_BLOCK, dtype=jnp.int32)
        dist = jnp.abs(qpos[:, None] - kpos[None, :]).astype(jnp.float32)
        s = s - slopes[None, :, None, None, None] * dist
        s = jnp.where(kvalid, s, -jnp.inf)
        p = jax.nn.softmax(s, axis=-1)
        a = p[:, :, 0] - lam * p[:, :, 1]
        return jnp.einsum('bhqk,bkhe->bqhe', a, vf)

    o = lax.map(block, (qb, starts))
    o = o.transpose(1, 0, 2, 3, 4).reshape(B, Lp, H, Dv)[:, :L]
    o = o * lax.rsqrt(jnp.mean(o * o, -1, keepdims=True) + SUBLN_EPS) * subln_g * (1.0 - lam_init)
    o = o.reshape(B, L, H * Dv).astype(x.dtype)
    return jnp.einsum('ble,ed->bld', o, w_o)

def _wkv7_step(S, inp):
    r, w, k, v, kk, a = inp
    sa = jnp.einsum('bhvk,bhk->bhv', S, kk)
    S = S * w[:, :, None, :] - sa[..., None] * (kk * a)[:, :, None, :] + v[..., None] * k[:, :, None, :]
    y = jnp.einsum('bhvk,bhk->bhv', S, r)
    return S, y

def rwkv7_time_mix(x, mu, w_rkv, w0, w1, w2, a0, a1, a2, g1, g2, k_k, k_a, r_k, lnx_g, lnx_b, w_o):
    B, L, D = x.shape
    H, N = RW_HEADS, RW_HEAD_DIM
    zero = jnp.zeros_like(x[:, :1])
    dx_prev = jnp.concatenate([zero, x[:, :-1]], 1) - x
    dx_next = jnp.concatenate([x[:, 1:], zero], 1) - x
    xs = x[None] + mu[0][:, None, None, :] * dx_prev[None] + mu[1][:, None, None, :] * dx_next[None]
    r, k, v = jnp.einsum('ibld,ide->ible', xs[:3], w_rkv)
    lw = jnp.einsum('nblr,nrd->nbld', jnp.tanh(jnp.einsum('bld,ndr->nblr', xs[3], w1)), w2)
    w_log = -jax.nn.softplus(-(w0[:, None, None, :] + lw).astype(jnp.float32)) - 0.5
    decay = jnp.exp(-jnp.exp(w_log))
    la = jnp.einsum('nblr,nrd->nbld', jnp.einsum('bld,ndr->nblr', xs[4], a1), a2)
    a = jax.nn.sigmoid((a0[:, None, None, :] + la).astype(jnp.float32))
    g = jnp.einsum('blr,rd->bld', jax.nn.sigmoid(jnp.einsum('bld,dr->blr', xs[5], g1)), g2)
    kf = k.astype(jnp.float32)
    kk = (kf * k_k).reshape(B, L, H, N)
    kk = kk / jnp.maximum(jnp.sqrt(jnp.sum(kk * kk, -1, keepdims=True)), 1e-12)
    kd = kf[None] * (1.0 + (a - 1.0) * k_a)

    def tm(t):
        return jnp.swapaxes(t.reshape(B, L, H, N), 0, 1).astype(jnp.float32)

    r_t, v_t, kk_t = tm(r), tm(v), jnp.swapaxes(kk, 0, 1)
    S0 = jnp.zeros((B, H, N, N), jnp.float32)
    _, y_fwd = lax.scan(_wkv7_step, S0, (r_t, tm(decay[0]), tm(kd[0]), v_t, kk_t, tm(a[0])))
    _, y_bwd = lax.scan(_wkv7_step, S0, (r_t, tm(decay[1]), tm(kd[1]), v_t, kk_t, tm(a[1])), reverse=True)
    y = jnp.swapaxes(y_fwd + y_bwd, 0, 1)
    ym = jnp.mean(y, -1, keepdims=True)
    yv = jnp.mean(jnp.square(y - ym), -1, keepdims=True)
    y = ((y - ym) * lax.rsqrt(yv + RW_LNX_EPS)).reshape(B, L, D) * lnx_g + lnx_b
    rh = r.reshape(B, L, H, N).astype(jnp.float32)
    kdh = (kd[0] + kd[1]).reshape(B, L, H, N)
    bonus = jnp.sum(rh * kdh * r_k, -1, keepdims=True) * v.reshape(B, L, H, N).astype(jnp.float32)
    out = ((y + bonus.reshape(B, L, D)) * g).astype(x.dtype)
    return jnp.einsum('bld,de->ble', out, w_o)

def swiglu(x, w_gate, w_up, w_down):
    return (jax.nn.silu(x @ w_gate) * (x @ w_up)) @ w_down

def moe_swiglu(x, w_router, b_router, w_gate, w_up, w_down):
    logits = (jnp.einsum('bld,de->ble', x, w_router) + b_router).astype(jnp.float32)
    probs = jax.nn.softmax(logits, -1)
    top_p, top_i = lax.top_k(probs, TOP_K)
    top_p = top_p / jnp.sum(top_p, -1, keepdims=True)
    gates = jnp.sum(jax.nn.one_hot(top_i, N_EXPERTS, dtype=jnp.float32) * top_p[..., None], -2)
    y = jnp.zeros(x.shape, jnp.float32)
    for e in range(N_EXPERTS):
        y = y + gates[..., e:e + 1] * swiglu(x, w_gate[e], w_up[e], w_down[e]).astype(jnp.float32)
    return y.astype(x.dtype)

def first_inputs(seed: int = 0) -> dict:
    key = jax.random.key(seed)
    ks = iter(jax.random.split(key, 48))
    f32 = jnp.float32
    D, F, FE, E = D_MODEL, D_FF, D_FF_EXPERT, N_EXPERTS
    nA, nB = N_A_LAYERS, N_B_LAYERS

    def nrm(shape, scale):
        return jax.random.normal(next(ks), shape, f32) * scale

    inp = {}
    inp['x'] = nrm((BATCH, SEQ, D), 1.0)
    inp['meta'] = nrm((N_META, D), 1.0)
    inp['ln_g'] = 1.0 + nrm((DEPTH, 2, D), 0.02)
    inp['ln_b'] = nrm((DEPTH, 2, D), 0.02)
    inp['attn_w_in'] = nrm((nA, D, 3 * D), D ** -0.5)
    inp['attn_w_o'] = nrm((nA, D, D), D ** -0.5 * DEEPNORM_BETA)
    inp['attn_lam_q1'] = nrm((nA, DA_HEAD_DIM), 0.1)
    inp['attn_lam_k1'] = nrm((nA, DA_HEAD_DIM), 0.1)
    inp['attn_lam_q2'] = nrm((nA, DA_HEAD_DIM), 0.1)
    inp['attn_lam_k2'] = nrm((nA, DA_HEAD_DIM), 0.1)
    inp['attn_subln_g'] = 1.0 + nrm((nA, DA_V_DIM), 0.02)
    inp['ffn_w_gate'] = nrm((nA, D, F), D ** -0.5)
    inp['ffn_w_up'] = nrm((nA, D, F), D ** -0.5)
    inp['ffn_w_down'] = nrm((nA, F, D), F ** -0.5 * DEEPNORM_BETA)
    inp['rw_mu'] = jax.random.uniform(next(ks), (nB, 2, RW_N_MIX, D), f32, 0.0, 0.5)
    inp['rw_w_rkv'] = nrm((nB, 3, D, D), D ** -0.5)
    inp['rw_w0'] = -1.0 + nrm((nB, 2, D), 0.5)
    inp['rw_w1'] = nrm((nB, 2, D, RW_DECAY_LORA), D ** -0.5)
    inp['rw_w2'] = nrm((nB, 2, RW_DECAY_LORA, D), 0.5 * RW_DECAY_LORA ** -0.5)
    inp['rw_a0'] = nrm((nB, 2, D), 0.1)
    inp['rw_a1'] = nrm((nB, 2, D, RW_AAA_LORA), D ** -0.5)
    inp['rw_a2'] = nrm((nB, 2, RW_AAA_LORA, D), 0.5 * RW_AAA_LORA ** -0.5)
    inp['rw_g1'] = nrm((nB, D, RW_GATE_LORA), D ** -0.5)
    inp['rw_g2'] = nrm((nB, RW_GATE_LORA, D), RW_GATE_LORA ** -0.5)
    inp['rw_k_k'] = 0.85 + nrm((nB, D), 0.05)
    inp['rw_k_a'] = 1.0 + nrm((nB, D), 0.05)
    inp['rw_r_k'] = nrm((nB, RW_HEADS, RW_HEAD_DIM), 0.1)
    inp['rw_lnx_g'] = 1.0 + nrm((nB, D), 0.02)
    inp['rw_lnx_b'] = nrm((nB, D), 0.02)
    inp['rw_w_o'] = nrm((nB, D, D), D ** -0.5 * DEEPNORM_BETA)
    inp['moe_w_router'] = nrm((nB, D, E), D ** -0.5)
    inp['moe_b_router'] = nrm((nB, E), 0.01)
    inp['moe_w_gate'] = nrm((nB, E, D, FE), D ** -0.5)
    inp['moe_w_up'] = nrm((nB, E, D, FE), D ** -0.5)
    inp['moe_w_down'] = nrm((nB, E, FE, D), FE ** -0.5 * DEEPNORM_BETA)
    return inp

def first_block(x, meta, ln_g, ln_b, attn_w_in, attn_w_o, attn_lam_q1, attn_lam_k1, attn_lam_q2,
              attn_lam_k2, attn_subln_g, ffn_w_gate, ffn_w_up, ffn_w_down, rw_mu, rw_w_rkv, rw_w0,
              rw_w1, rw_w2, rw_a0, rw_a1, rw_a2, rw_g1, rw_g2, rw_k_k, rw_k_a, rw_r_k, rw_lnx_g,
              rw_lnx_b, rw_w_o, moe_w_router, moe_b_router, moe_w_gate, moe_w_up, moe_w_down):
    B = x.shape[0]
    h = jnp.concatenate([jnp.broadcast_to(meta[None].astype(x.dtype), (B, N_META, D_MODEL)), x], 1)
    for i in range(DEPTH):
        j = i // N_MIXERS
        if i % N_MIXERS == 0:
            mix = diff_attention(h, attn_w_in[j], attn_w_o[j], attn_lam_q1[j], attn_lam_k1[j],
                                 attn_lam_q2[j], attn_lam_k2[j], attn_subln_g[j], i)
        else:
            mix = rwkv7_time_mix(h, rw_mu[j], rw_w_rkv[j], rw_w0[j], rw_w1[j], rw_w2[j], rw_a0[j],
                                 rw_a1[j], rw_a2[j], rw_g1[j], rw_g2[j], rw_k_k[j], rw_k_a[j],
                                 rw_r_k[j], rw_lnx_g[j], rw_lnx_b[j], rw_w_o[j])
        h = layer_norm(DEEPNORM_ALPHA * h + mix, ln_g[i, 0], ln_b[i, 0])
        if i % 2 == 0:
            ff = swiglu(h, ffn_w_gate[j], ffn_w_up[j], ffn_w_down[j])
        else:
            ff = moe_swiglu(h, moe_w_router[j], moe_b_router[j], moe_w_gate[j], moe_w_up[j], moe_w_down[j])
        h = layer_norm(DEEPNORM_ALPHA * h + ff, ln_g[i, 1], ln_b[i, 1])
    return h[:, N_META:]


N_EVEN = (DEPTH + 1) // 2
N_ODD = DEPTH // 2

MLA_HEADS = 8
MLA_Q_RANK = 384
MLA_KV_RANK = 256
MLA_NOPE = 64
MLA_ROPE = 32
MLA_V = 64
MLA_QK = MLA_NOPE + MLA_ROPE

RET_HEADS = 8
RET_DK = 64
RET_DV = 64
RET_CHUNK = 128
RET_DECAY_BASE = 5.0

GLA_HEADS = 4
GLA_DK = 128
GLA_DV = 256
GLA_GATE_RANK = 16
GLA_TAU = 16.0
GLA_CHUNK = 64

CONV_W = 3

ROPE_THETA = 10000.0
EPS = 1e-6

EVEN_SPLIT = (MLA_Q_RANK, MLA_KV_RANK, MLA_ROPE,
              RET_HEADS * RET_DK, RET_HEADS * RET_DK, RET_HEADS * RET_DV, RET_HEADS * RET_DV)
EVEN_IN = MLA_Q_RANK + MLA_KV_RANK + MLA_ROPE + 2 * RET_HEADS * RET_DK + 2 * RET_HEADS * RET_DV
EVEN_OUT = MLA_HEADS * MLA_V + RET_HEADS * RET_DV
ODD_SPLIT = (GLA_HEADS * GLA_DK, GLA_HEADS * GLA_DK, GLA_HEADS * GLA_DV, GLA_HEADS * GLA_DV,
             GLA_GATE_RANK, GLA_GATE_RANK)
ODD_IN = 2 * GLA_HEADS * GLA_DK + 2 * GLA_HEADS * GLA_DV + 2 * GLA_GATE_RANK
ODD_OUT = GLA_HEADS * GLA_DV


def _split(p, sizes):
    outs, s = [], 0
    for n in sizes:
        outs.append(p[..., s:s + n])
        s += n
    return outs

def _rmsnorm(x, g):
    xf = x.astype(jnp.float32)
    y = xf * lax.rsqrt(jnp.mean(xf * xf, axis=-1, keepdims=True) + EPS)
    return (y * g.astype(jnp.float32)).astype(x.dtype)

def _rope(x, positions):
    half = x.shape[-1] // 2
    inv = ROPE_THETA ** (-jnp.arange(half, dtype=jnp.float32) / half)
    ang = positions.astype(jnp.float32)[:, :, None] * inv
    cos = jnp.cos(ang)[:, :, None, :]
    sin = jnp.sin(ang)[:, :, None, :]
    x1 = x[..., :half].astype(jnp.float32)
    x2 = x[..., half:].astype(jnp.float32)
    return jnp.concatenate([x1 * cos - x2 * sin, x2 * cos + x1 * sin], axis=-1).astype(x.dtype)

def _mla(cq, ckv, k_rope, positions, q_norm, kv_norm, w_uq, w_ukv, q_head_norm, k_head_norm):
    B, S, _ = cq.shape
    H = MLA_HEADS
    q = (_rmsnorm(cq, q_norm) @ w_uq).reshape(B, S, H, MLA_QK)
    kv = (_rmsnorm(ckv, kv_norm) @ w_ukv).reshape(B, S, H, MLA_NOPE + MLA_V)
    k_nope, v = kv[..., :MLA_NOPE], kv[..., MLA_NOPE:]
    k = jnp.concatenate([k_nope, jnp.broadcast_to(k_rope[:, :, None, :], (B, S, H, MLA_ROPE))], axis=-1)
    q = _rmsnorm(q, q_head_norm)
    k = _rmsnorm(k, k_head_norm)
    q = jnp.concatenate([q[..., :MLA_NOPE], _rope(q[..., MLA_NOPE:], positions)], axis=-1)
    k = jnp.concatenate([k[..., :MLA_NOPE], _rope(k[..., MLA_NOPE:], positions)], axis=-1)
    scale = MLA_QK ** -0.5
    nb = S // Q_BLOCK
    qb = q.reshape(B, nb, Q_BLOCK, H, MLA_QK).transpose(1, 0, 2, 3, 4)

    def block(qi):
        s = jnp.einsum('bqhd,bkhd->bhqk', qi, k).astype(jnp.float32) * scale
        p = jax.nn.softmax(s, axis=-1).astype(v.dtype)
        return jnp.einsum('bhqk,bkhe->bqhe', p, v)

    o = lax.map(block, qb)
    return o.transpose(1, 0, 2, 3, 4).reshape(B, S, H * MLA_V)

def _retention_dir(q, k, v, log_gamma, include_diag):
    B, S, H, dk = q.shape
    dv = v.shape[-1]
    C = RET_CHUNK
    n = S // C
    q = q.reshape(B, n, C, H, dk)
    k = k.reshape(B, n, C, H, dk)
    v = v.reshape(B, n, C, H, dv)
    lg = log_gamma.astype(jnp.float32)
    pos = jnp.arange(C, dtype=jnp.float32)
    rel = pos[:, None] - pos[None, :]
    mask = (rel >= 0) if include_diag else (rel > 0)
    decay = jnp.where(mask[None], jnp.exp(lg[:, None, None] * jnp.maximum(rel, 0.0)[None]), 0.0)
    scores = jnp.einsum('bnihd,bnjhd->bnhij', q, k) * decay
    intra = jnp.einsum('bnhij,bnjhe->bnihe', scores, v)
    zeta = jnp.exp(lg[:, None] * (C - 1 - pos)[None])
    chunk_state = jnp.einsum('bnjhd,bnjhe,hj->bnhde', k, v, zeta)
    chunk_decay = jnp.exp(lg * C)[None, :, None, None]

    def step(R, s):
        return chunk_decay * R + s, R

    R0 = jnp.zeros((B, H, dk, dv), chunk_state.dtype)
    _, R_prev = lax.scan(step, R0, jnp.moveaxis(chunk_state, 1, 0))
    R_prev = jnp.moveaxis(R_prev, 0, 1)
    xi = jnp.exp(lg[:, None] * (pos + 1.0)[None]).T
    cross = jnp.einsum('bnihd,bnhde->bnihe', q, R_prev) * xi[None, None, :, :, None]
    return (intra + cross).reshape(B, S, H, dv)

def _retention(rq, rk, rv, rg, positions, theta_fwd, theta_bwd, out_norm):
    B, S, _ = rq.shape
    H = RET_HEADS
    q = _rope(rq.reshape(B, S, H, RET_DK), positions)
    k = _rope(rk.reshape(B, S, H, RET_DK), positions) * (RET_DK ** -0.5)
    v = rv.reshape(B, S, H, RET_DV)
    lg_f = jnp.log1p(-jnp.exp2(-theta_fwd.astype(jnp.float32)))
    lg_b = jnp.log1p(-jnp.exp2(-theta_bwd.astype(jnp.float32)))
    o_f = _retention_dir(q, k, v, lg_f, True)
    o_b = jnp.flip(_retention_dir(jnp.flip(q, 1), jnp.flip(k, 1), jnp.flip(v, 1), lg_b, False), 1)
    o = _rmsnorm(o_f + o_b, out_norm)
    return jax.nn.silu(rg) * o.reshape(B, S, H * RET_DV)

def _gla_dir(q, k, v, log_a, include_diag):
    B, S, H, dk = q.shape
    dv = v.shape[-1]
    C = GLA_CHUNK
    n = S // C
    q = q.reshape(B, n, C, H, dk)
    k = k.reshape(B, n, C, H, dk)
    v = v.reshape(B, n, C, H, dv)
    b = jnp.cumsum(log_a.astype(jnp.float32).reshape(B, n, C, H, dk), axis=2)
    b_mid = b[:, :, C // 2:C // 2 + 1]
    b_last = b[:, :, -1]
    qc = q * jnp.exp(b - b_mid)
    kc = k * jnp.exp(b_mid - b)
    A = jnp.einsum('bnihd,bnjhd->bnhij', qc, kc)
    pos = jnp.arange(C)
    mask = (pos[:, None] >= pos[None, :]) if include_diag else (pos[:, None] > pos[None, :])
    A = jnp.where(mask, A, 0.0)
    intra = jnp.einsum('bnhij,bnjhe->bnihe', A, v)
    k_dec = k * jnp.exp(b_last[:, :, None] - b)
    chunk_state = jnp.einsum('bnjhd,bnjhe->bnhde', k_dec, v)
    chunk_decay = jnp.exp(b_last)

    def step(Sm, xs):
        dcy, st = xs
        return dcy[..., None] * Sm + st, Sm

    S0 = jnp.zeros((B, H, dk, dv), chunk_state.dtype)
    _, S_prev = lax.scan(step, S0, (jnp.moveaxis(chunk_decay, 1, 0), jnp.moveaxis(chunk_state, 1, 0)))
    S_prev = jnp.moveaxis(S_prev, 0, 1)
    inter = jnp.einsum('bnihd,bnhde->bnihe', q * jnp.exp(b), S_prev)
    return (intra + inter).reshape(B, S, H, dv)

def _gla(gq, gk, gv, gr, ga_f, ga_b, w_gate_fwd, b_gate_fwd, w_gate_bwd, b_gate_bwd, out_norm):
    B, S, _ = gq.shape
    H = GLA_HEADS
    q = gq.reshape(B, S, H, GLA_DK) * (GLA_DK ** -0.5)
    k = gk.reshape(B, S, H, GLA_DK)
    v = gv.reshape(B, S, H, GLA_DV)
    la_f = (jax.nn.log_sigmoid((ga_f @ w_gate_fwd + b_gate_fwd).astype(jnp.float32)) / GLA_TAU).reshape(B, S, H, GLA_DK)
    la_b = (jax.nn.log_sigmoid((ga_b @ w_gate_bwd + b_gate_bwd).astype(jnp.float32)) / GLA_TAU).reshape(B, S, H, GLA_DK)
    o_f = _gla_dir(q, k, v, la_f, True)
    o_b = jnp.flip(_gla_dir(jnp.flip(q, 1), jnp.flip(k, 1), jnp.flip(v, 1), jnp.flip(la_b, 1), False), 1)
    o = _rmsnorm(o_f + o_b, out_norm)
    return jax.nn.silu(gr) * o.reshape(B, S, H * GLA_DV)

def _conv_ffn(x, norm_g, w_up, conv_w, conv_b, w_down):
    h = _rmsnorm(x, norm_g)
    up = h @ w_up
    gate, val = up[..., :D_FF], up[..., D_FF:]
    gate = lax.conv_general_dilated(gate, conv_w[:, None, :].astype(gate.dtype), window_strides=(1,),
                                    padding='SAME', dimension_numbers=('NWC', 'WIO', 'NWC'),
                                    feature_group_count=D_FF) + conv_b
    return (jax.nn.silu(gate) * val) @ w_down

def second_inputs(seed: int = 0) -> dict:
    key = jax.random.key(seed)
    ks = iter(jax.random.split(key, 40))

    def dense(shape, fan_in):
        return jax.random.normal(next(ks), shape, jnp.float32) * (fan_in ** -0.5)

    def gain(shape):
        return 1.0 + 0.02 * jax.random.normal(next(ks), shape, jnp.float32)

    def small(shape, s):
        return s * jax.random.normal(next(ks), shape, jnp.float32)

    x = jax.random.normal(next(ks), (BATCH, SEQ, D_MODEL), jnp.float32)
    start = jax.random.randint(next(ks), (BATCH, 1), 0, 4096)
    positions = (start + jnp.arange(SEQ)[None, :]).astype(jnp.int32)
    ret_base = RET_DECAY_BASE + jnp.arange(RET_HEADS, dtype=jnp.float32)
    return {
        "x": x,
        "positions": positions,
        "mix_norm_even": gain((N_EVEN, D_MODEL)),
        "w_in_even": dense((N_EVEN, D_MODEL, EVEN_IN), D_MODEL),
        "mla_q_norm": gain((N_EVEN, MLA_Q_RANK)),
        "mla_kv_norm": gain((N_EVEN, MLA_KV_RANK)),
        "mla_w_uq": dense((N_EVEN, MLA_Q_RANK, MLA_HEADS * MLA_QK), MLA_Q_RANK),
        "mla_w_ukv": dense((N_EVEN, MLA_KV_RANK, MLA_HEADS * (MLA_NOPE + MLA_V)), MLA_KV_RANK),
        "mla_q_head_norm": gain((N_EVEN, MLA_QK)),
        "mla_k_head_norm": gain((N_EVEN, MLA_QK)),
        "ret_theta_fwd": ret_base + small((N_EVEN, RET_HEADS), 0.1),
        "ret_theta_bwd": ret_base + small((N_EVEN, RET_HEADS), 0.1),
        "ret_out_norm": gain((N_EVEN, RET_HEADS, RET_DV)),
        "w_out_even": dense((N_EVEN, EVEN_OUT, D_MODEL), EVEN_OUT),
        "mix_norm_odd": gain((N_ODD, D_MODEL)),
        "w_in_odd": dense((N_ODD, D_MODEL, ODD_IN), D_MODEL),
        "gla_w_gate_fwd": dense((N_ODD, GLA_GATE_RANK, GLA_HEADS * GLA_DK), GLA_GATE_RANK),
        "gla_b_gate_fwd": small((N_ODD, GLA_HEADS * GLA_DK), 0.1),
        "gla_w_gate_bwd": dense((N_ODD, GLA_GATE_RANK, GLA_HEADS * GLA_DK), GLA_GATE_RANK),
        "gla_b_gate_bwd": small((N_ODD, GLA_HEADS * GLA_DK), 0.1),
        "gla_out_norm": gain((N_ODD, GLA_HEADS, GLA_DV)),
        "w_out_odd": dense((N_ODD, ODD_OUT, D_MODEL), ODD_OUT),
        "ffn_norm": gain((DEPTH, D_MODEL)),
        "ffn_w_up": dense((DEPTH, D_MODEL, 2 * D_FF), D_MODEL),
        "ffn_conv_w": dense((DEPTH, CONV_W, D_FF), CONV_W),
        "ffn_conv_b": small((DEPTH, D_FF), 0.02),
        "ffn_w_down": dense((DEPTH, D_FF, D_MODEL), D_FF),
    }

def second_block(x, positions, mix_norm_even, w_in_even, mla_q_norm, mla_kv_norm, mla_w_uq, mla_w_ukv,
              mla_q_head_norm, mla_k_head_norm, ret_theta_fwd, ret_theta_bwd, ret_out_norm, w_out_even,
              mix_norm_odd, w_in_odd, gla_w_gate_fwd, gla_b_gate_fwd, gla_w_gate_bwd, gla_b_gate_bwd,
              gla_out_norm, w_out_odd, ffn_norm, ffn_w_up, ffn_conv_w, ffn_conv_b, ffn_w_down):
    for layer in range(DEPTH):
        i = layer // 2
        if layer % 2 == 0:
            h = _rmsnorm(x, mix_norm_even[i])
            cq, ckv, k_rope, rq, rk, rv, rg = _split(h @ w_in_even[i], EVEN_SPLIT)
            a = _mla(cq, ckv, k_rope, positions, mla_q_norm[i], mla_kv_norm[i], mla_w_uq[i], mla_w_ukv[i],
                     mla_q_head_norm[i], mla_k_head_norm[i])
            r = _retention(rq, rk, rv, rg, positions, ret_theta_fwd[i], ret_theta_bwd[i], ret_out_norm[i])
            x = x + jnp.concatenate([a, r], axis=-1) @ w_out_even[i]
        else:
            h = _rmsnorm(x, mix_norm_odd[i])
            gq, gk, gv, gr, ga_f, ga_b = _split(h @ w_in_odd[i], ODD_SPLIT)
            g = _gla(gq, gk, gv, gr, ga_f, ga_b, gla_w_gate_fwd[i], gla_b_gate_fwd[i],
                     gla_w_gate_bwd[i], gla_b_gate_bwd[i], gla_out_norm[i])
            x = x + g @ w_out_odd[i]
        x = x + _conv_ffn(x, ffn_norm[layer], ffn_w_up[layer], ffn_conv_w[layer], ffn_conv_b[layer],
                          ffn_w_down[layer])
    return x


def setup_inputs(seed=0):
    out = dict(first_inputs(seed))
    for name, value in second_inputs(seed + 1).items():
        if name != "x":
            out[name + "_2"] = value
    return out


def reference(
    x, meta, ln_g, ln_b, attn_w_in, attn_w_o, attn_lam_q1, attn_lam_k1, attn_lam_q2,
    attn_lam_k2, attn_subln_g, ffn_w_gate, ffn_w_up, ffn_w_down, rw_mu, rw_w_rkv, rw_w0, rw_w1,
    rw_w2, rw_a0, rw_a1, rw_a2, rw_g1, rw_g2, rw_k_k, rw_k_a, rw_r_k, rw_lnx_g, rw_lnx_b,
    rw_w_o, moe_w_router, moe_b_router, moe_w_gate, moe_w_up, moe_w_down, positions_2,
    mix_norm_even_2, w_in_even_2, mla_q_norm_2, mla_kv_norm_2, mla_w_uq_2, mla_w_ukv_2,
    mla_q_head_norm_2, mla_k_head_norm_2, ret_theta_fwd_2, ret_theta_bwd_2, ret_out_norm_2,
    w_out_even_2, mix_norm_odd_2, w_in_odd_2, gla_w_gate_fwd_2, gla_b_gate_fwd_2,
    gla_w_gate_bwd_2, gla_b_gate_bwd_2, gla_out_norm_2, w_out_odd_2, ffn_norm_2, ffn_w_up_2,
    ffn_conv_w_2, ffn_conv_b_2, ffn_w_down_2,
):
    x = first_block(
        x, meta, ln_g, ln_b, attn_w_in, attn_w_o, attn_lam_q1, attn_lam_k1, attn_lam_q2,
        attn_lam_k2, attn_subln_g, ffn_w_gate, ffn_w_up, ffn_w_down, rw_mu, rw_w_rkv, rw_w0,
        rw_w1, rw_w2, rw_a0, rw_a1, rw_a2, rw_g1, rw_g2, rw_k_k, rw_k_a, rw_r_k, rw_lnx_g,
        rw_lnx_b, rw_w_o, moe_w_router, moe_b_router, moe_w_gate, moe_w_up, moe_w_down,
    )
    return second_block(
        x, positions_2, mix_norm_even_2, w_in_even_2, mla_q_norm_2, mla_kv_norm_2, mla_w_uq_2,
        mla_w_ukv_2, mla_q_head_norm_2, mla_k_head_norm_2, ret_theta_fwd_2, ret_theta_bwd_2,
        ret_out_norm_2, w_out_even_2, mix_norm_odd_2, w_in_odd_2, gla_w_gate_fwd_2,
        gla_b_gate_fwd_2, gla_w_gate_bwd_2, gla_b_gate_bwd_2, gla_out_norm_2, w_out_odd_2,
        ffn_norm_2, ffn_w_up_2, ffn_conv_w_2, ffn_conv_b_2, ffn_w_down_2,
    )


_drawn_inputs = setup_inputs


def setup_inputs(seed=0):
    import zlib

    import numpy as np

    out = dict(_drawn_inputs(seed))
    spreads = {}
    factors = {'attn_lam_k2': 5.596,
     'attn_subln_g': 2.674,
     'rw_k_k': 3.286,
     'rw_lnx_g': 3.473,
     'rw_lnx_b': 3.015,
     'mla_q_norm_2': 8.0,
     'mla_kv_norm_2': 8.0,
     'mla_q_head_norm_2': 8.0,
     'mla_k_head_norm_2': 8.0,
     'ret_out_norm_2': 18.808,
     'mix_norm_odd_2': 2.926,
     'gla_b_gate_fwd_2': 3.871,
     'gla_b_gate_bwd_2': 3.927,
     'gla_out_norm_2': 19.209,
     'ffn_conv_b_2': 13.97,
     'ffn_norm_2': 8.0}
    for name, (base, spread) in spreads.items():
        noise = np.random.default_rng([zlib.crc32(name.encode()), seed]).standard_normal(out[name].shape)
        drawn = base * np.exp(spread * noise) if base else spread * noise
        out[name] = __import__('jax').numpy.asarray(drawn.astype(out[name].dtype))
    for name, factor in factors.items():
        out[name] = (out[name] * factor).astype(out[name].dtype)
    return out
```

```python
import numpy as np
import concourse.bass as bass
from concourse import mybir
from contextlib import ExitStack

D, T0, T1, C = 1024, 272, 256, 68
FF, FE, NE = 2816, 3584, 8
ALPHA = float(4.0 ** 0.25)
LAM_INIT = 0.8 - 0.6 * float(np.exp(0.0))
BW = 3072
RING = 4


def tiles_of(name, get, nk, cols):
    return [(name, get, nk, c0, cw) for c0, cw in cols]


def cuts(n, w, c0=0):
    return [(c0 + i, min(w, n - i)) for i in range(0, n, w)]


def stream_tiles():
    def g(name, *idx):
        return lambda inp: inp[name][idx] if idx else inp[name]

    def two(name):
        return lambda inp: np.concatenate([inp[name][0, 0], inp[name][0, 1]], axis=1)

    t = []
    t += tiles_of("attn_qk", g("attn_w_in", 0), 8, cuts(2048, 128))
    t += tiles_of("attn_v", g("attn_w_in", 0), 8, [(2048, 384), (2432, 384), (2816, 256)])
    t += tiles_of("attn_o", g("attn_w_o", 0), 8, cuts(D, 128))
    for f in range(22):
        t += tiles_of("ffn_gu", g("ffn_w_gate", 0), 8, [(128 * f, 128)])
        t += tiles_of("ffn_gu", g("ffn_w_up", 0), 8, [(128 * f, 128)])
    t += tiles_of("ffn_d", g("ffn_w_down", 0), 22, cuts(D, 128))
    for i in range(3):
        t += tiles_of(f"rkv{i}", g("rw_w_rkv", 0, i), 8, cuts(D, 128))
    t += tiles_of("lw", two("rw_w1"), 8, [(0, 128)])
    t += tiles_of("la", two("rw_a1"), 8, [(0, 128)])
    t += tiles_of("lg", g("rw_g1", 0), 8, [(0, 128), (128, 32)])
    t += tiles_of("rw_o", g("rw_w_o", 0), 8, cuts(D, 128))
    t += tiles_of("router", g("moe_w_router", 0), 8, [(0, 8)])
    for e in range(NE):
        for f in range(FE // 128):
            t += tiles_of("moe", g("moe_w_gate", 0, e), 8, [(128 * f, 128)])
            t += tiles_of("moe", g("moe_w_up", 0, e), 8, [(128 * f, 128)])
            t += tiles_of("moe", lambda inp, e=e, f=f: inp["moe_w_down"][0, e, 128 * f:128 * f + 128], 1, [(0, D)])
    w = g("w_in_even_2", 0)
    t += tiles_of("e_c", w, 8, cuts(640, 128))
    t += tiles_of("e_kr", w, 8, [(640, 32)])
    t += tiles_of("e_qk", w, 8, [(672, 256), (928, 256), (1184, 256), (1440, 256)])
    t += tiles_of("e_v", w, 8, [(1696, 256), (1952, 256)])
    t += tiles_of("e_g", w, 8, cuts(512, 128, 2208))
    t += tiles_of("uq", g("mla_w_uq_2", 0), 3, [(0, 384), (384, 384)])
    t += tiles_of("ukv", g("mla_w_ukv_2", 0), 2, [(0, 512), (512, 512)])
    t += tiles_of("e_o", g("w_out_even_2", 0), 8, cuts(D, 128))

    def conv(i):
        r = []
        for f in range(22):
            r += tiles_of(f"cu{i}", g("ffn_w_up_2", i), 8, [(128 * f, 128)])
            r += tiles_of(f"cu{i}", g("ffn_w_up_2", i), 8, [(FF + 128 * f, 128)])
        return r + tiles_of(f"cd{i}", g("ffn_w_down_2", i), 22, cuts(D, 128))

    t += conv(0)
    w = g("w_in_odd_2", 0)
    t += tiles_of("o_qk", w, 8, cuts(1024, 128))
    t += tiles_of("o_v", w, 8, [(1024, 384), (1408, 384), (1792, 256)])
    t += tiles_of("o_a", w, 8, [(3072, 16), (3088, 16)])
    t += tiles_of("gg", lambda inp: np.concatenate([inp["gla_w_gate_fwd_2"][0], inp["gla_w_gate_bwd_2"][0]], axis=1),
                  1, [(0, 1024)])
    t += tiles_of("o_g", w, 8, cuts(1024, 128, 2048))
    t += tiles_of("o_o", g("w_out_odd_2", 0), 8, cuts(D, 128))
    t += conv(1)
    return t


def stream_blocks():
    blocks, width = [], BW + 1
    for t in stream_tiles():
        w = t[2] * t[4]
        if width + w > BW or (t[0] == "moe" and blocks[-1][-1][0][0] != "moe"):
            blocks.append([])
            width = 0
        blocks[-1].append((t, width))
        width += w
    return [(b, b[-1][1] + b[-1][0][2] * b[-1][0][4]) for b in blocks]


def pack_stream(inp):
    parts = []
    blocks = stream_blocks()
    out = np.zeros(sum(128 * w for _, w in blocks), np.float32)
    off = 0
    for b, w in blocks:
        dst = out[off:off + 128 * w].reshape(128, w)
        for (name, get, nk, c0, cw), x in b:
            src = get(inp)[:, c0:c0 + cw]
            if nk == 1:
                dst[:src.shape[0], x:x + cw] = src
            else:
                dst[:, x:x + nk * cw].reshape(128, nk, cw)[...] = src.reshape(nk, 128, cw).transpose(1, 0, 2)
        off += 128 * w
    return out


def params():
    def fm(get):
        return lambda inp: np.reshape(get(inp), (-1, 128)).T

    def rep(get):
        return lambda inp: np.broadcast_to(np.reshape(get(inp), (1, -1)), (128, np.size(get(inp))))

    p = []
    for i in range(2):
        for j in range(2):
            p.append((f"ln_g{i}{j}", 8, fm(lambda inp, i=i, j=j: inp["ln_g"][i, j])))
            p.append((f"ln_b{i}{j}", 8, fm(lambda inp, i=i, j=j: inp["ln_b"][i, j])))
    p.append(("subln", 1, fm(lambda inp: inp["attn_subln_g"][0])))
    for n in ("q1", "q2", "k1", "k2"):
        p.append((f"lam_{n}", 64, rep(lambda inp, n=n: inp[f"attn_lam_{n}"][0])))
    for s in range(2):
        for m in range(6):
            p.append((f"mu{s}{m}", 8, fm(lambda inp, s=s, m=m: inp["rw_mu"][0, s, m])))
        p.append((f"w0{s}", 8, fm(lambda inp, s=s: inp["rw_w0"][0, s])))
        p.append((f"a0{s}", 8, fm(lambda inp, s=s: inp["rw_a0"][0, s])))
    for n in ("k_k", "k_a", "r_k", "lnx_g", "lnx_b"):
        p.append((n, 8, fm(lambda inp, n=n: inp[f"rw_{n}"][0])))
    p.append(("b_router", 8, rep(lambda inp: inp["moe_b_router"][0])))
    p.append(("n_even", 8, fm(lambda inp: inp["mix_norm_even_2"][0])))
    p.append(("n_q", 3, fm(lambda inp: inp["mla_q_norm_2"][0])))
    p.append(("n_kv", 2, fm(lambda inp: inp["mla_kv_norm_2"][0])))
    p.append(("n_qh", 96, rep(lambda inp: inp["mla_q_head_norm_2"][0])))
    p.append(("n_kh", 96, rep(lambda inp: inp["mla_k_head_norm_2"][0])))
    p.append(("th_f", 8, rep(lambda inp: inp["ret_theta_fwd_2"][0])))
    p.append(("th_b", 8, rep(lambda inp: inp["ret_theta_bwd_2"][0])))
    p.append(("n_ret", 4, fm(lambda inp: inp["ret_out_norm_2"][0])))
    p.append(("n_odd", 8, fm(lambda inp: inp["mix_norm_odd_2"][0])))
    p.append(("b_gf", 4, fm(lambda inp: inp["gla_b_gate_fwd_2"][0])))
    p.append(("b_gb", 4, fm(lambda inp: inp["gla_b_gate_bwd_2"][0])))
    p.append(("n_gla", 8, fm(lambda inp: inp["gla_out_norm_2"][0])))
    for i in range(2):
        p.append((f"n_ffn{i}", 8, fm(lambda inp, i=i: inp["ffn_norm_2"][i])))
        for j in range(3):
            p.append((f"cw{i}{j}", 22, fm(lambda inp, i=i, j=j: inp["ffn_conv_w_2"][i, j])))
        p.append((f"cb{i}", 22, fm(lambda inp, i=i: inp["ffn_conv_b_2"][i])))
    return p


def columns(items):
    at, out = 0, {}
    for name, n, _ in items:
        out[name] = (at, n)
        at += n
    return out, at


def pack(items, inp):
    at, n = columns(items)
    out = np.zeros((128, n), np.float32)
    for name, w, get in items:
        v = get(inp)
        out[:v.shape[0], at[name][0]:at[name][0] + w] = v
    return out


def consts():
    p = np.arange(128)
    f = np.float32

    def full(n):
        return lambda _: np.full((128, 128), 1.0 / n, f)

    blk = ((p[:, None] // 64) == (p[None, :] // 64)).astype(f)
    s, t = np.arange(C)[:, None], np.arange(C)[None, :]
    q = np.arange(384).reshape(3, 128).T
    j2 = np.arange(256).reshape(2, 128).T
    negd = -np.abs(q[:, :, None] - np.arange(T0)[None, None, :]).astype(f)
    rel = (np.arange(256)[None, None, :] - j2[:, :, None]).astype(f)
    e8 = np.arange(8)
    c = [("ident", 128, lambda _: np.eye(128, dtype=f)),
         ("o1024", 128, full(1024)), ("o128", 128, full(128)), ("o256", 128, full(256)), ("o384", 128, full(384)),
         ("blk", 128, lambda _: blk), ("blk64", 128, lambda _: blk / f(64)),
         ("up", C, lambda _: (s < t).astype(f)), ("upi", C, lambda _: (s <= t).astype(f)),
         ("dn", C, lambda _: (s > t).astype(f)), ("dni", C, lambda _: (s >= t).astype(f)),
         ("nup", C, lambda _: -(s < t).astype(f)), ("ndn", C, lambda _: -(s > t).astype(f))]
    for lv in range(7):
        m = ((s >> (lv + 1)) == (t >> (lv + 1))) & (((s >> lv) & 1) == 0) & (((t >> lv) & 1) == 1)
        c.append((f"lu{lv}", C, lambda _, m=m: m.astype(f)))
        c.append((f"ld{lv}", C, lambda _, m=m: m.T.astype(f)))
    c.append(("negd", 3 * T0, lambda _: negd.reshape(128, -1)))
    c.append(("relp", 512, lambda _: np.maximum(rel, 0).reshape(128, -1)))
    c.append(("reln", 512, lambda _: np.maximum(-rel, 0).reshape(128, -1)))
    i64, j64 = np.arange(64)[None, :], (p % 64)[:, None]
    c.append(("gm0", 64, lambda _: (j64 <= i64).astype(f)))
    c.append(("gm1", 64, lambda _: (j64 > i64).astype(f)))
    for h in (16, 32):
        inv = (f(10000.0) ** (-np.arange(h, dtype=f) / f(h))).astype(f)
        c.append((f"inv{h}", h, lambda _, inv=inv: np.broadcast_to(inv[None], (128, len(inv)))))
    c.append(("before", 64, lambda _: np.broadcast_to((e8[None, :] < e8[:, None]).astype(f).reshape(1, 64), (128, 64))))
    return c


def resident():
    return [("w2", D, lambda inp: np.reshape(inp["rw_w2"][0], (128, D))),
            ("a2", D, lambda inp: np.reshape(inp["rw_a2"][0], (128, D))),
            ("g2", D, lambda inp: inp["rw_g2"][0, 0:128]),
            ("g2b", D, lambda inp: inp["rw_g2"][0, 128:160])]


class Eng:

    def __init__(self, sem):
        self.sem, self.n, self.queue = sem, 0, []

    def __call__(self, fn, *waits, inc=True, chain=True):
        w = [x for x in waits if x is not None]
        if chain and self.n:
            w.append((self.sem, self.n))
        self.n += 1 if inc else 0
        self.queue.append((fn, w, inc))
        return (self.sem, self.n)

    def last(self):
        return (self.sem, self.n) if self.n else None

    def emit(self, eng):
        seen = {}
        for fn, waits, inc in self.queue:
            for sem, v in waits:
                if seen.get(id(sem), 0) < v:
                    eng.wait_ge(sem, v)
                    seen[id(sem)] = v
            if fn is None:
                continue
            ins = fn(eng)
            if inc:
                ins.then_inc(self.sem, 1)


def build(nc, x_d, ws_d, par_d, con_d, res_d, pos_d, out_d, stop=99):
    fp32, i32, u32 = mybir.dt.float32, mybir.dt.int32, mybir.dt.uint32
    ALU, ACT, AX = mybir.AluOpType, mybir.ActivationFunctionType, mybir.AxisListType
    MUL, ADD, SUB, MAXO = ALU.mult, ALU.add, ALU.subtract, ALU.max
    ctx = ExitStack()
    with ctx:
        def sb(name, shape, dt=fp32):
            return ctx.enter_context(nc.sbuf_tensor(name, shape, dt))

        def sem(name):
            return ctx.enter_context(nc.semaphore(name))

        pc, np_ = columns(params())
        cc, nc_ = columns(consts())
        rc, nr_ = columns(resident())
        ring = sb("ring", [128, RING, BW])
        par_t, con_t, res_t = sb("par", [128, np_]), sb("con", [128, nc_]), sb("res", [128, nr_])
        pos_t = sb("pos", [128, 2], i32)
        NA = (208 * 1024 - 1024 - 4 * (RING * BW + np_ + nc_ + nr_)) // 4 // 64 * 64
        arena = sb("arena", [128, NA])
        ps_t = ctx.enter_context(nc.psum_tensor("ps", [128, 8, 512], fp32))
        ar, PS = arena[:, :], ps_t[:, :, :]

        def par(n):
            return par_t[:, pc[n][0]:pc[n][0] + pc[n][1]]

        def con(n):
            return con_t[:, cc[n][0]:cc[n][0] + cc[n][1]]

        def res(n):
            return res_t[:, rc[n][0]:rc[n][0] + rc[n][1]]

        def at(off, *shape):
            n = int(np.prod(shape))
            assert off + n <= NA, (off, shape, NA)
            v = ar[:, off:off + n]
            if len(shape) == 2:
                v = v.rearrange("p (a b) -> p a b", a=shape[0])
            if len(shape) == 3:
                v = v.rearrange("p (a b c) -> p a b c", a=shape[0], b=shape[1])
            return v

        def bc(v, *shape):
            return v.broadcast_to([v.shape[0], *shape])

        PE, DV, AC, PO, SP = (Eng(sem(n)) for n in ("s_pe", "s_dve", "s_act", "s_pool", "s_sp"))
        s_in = [sem(f"s_in{i}") for i in range(5)]
        s_w = [sem(f"s_w{i}") for i in range(RING)]
        s_out = sem("s_out")
        IN_X, IN_PAR, IN_CON, IN_RES, IN_POS = ((s, 16) for s in s_in)

        def everything():
            return [t for t in (PE.last(), DV.last(), AC.last(), PO.last()) if t]

        blocks = stream_blocks()
        flat = [(t, bi, x) for bi, (b, _) in enumerate(blocks) for t, x in b]
        state = {"tile": 0, "freed": {}}

        def weight(name):
            t, bi, x = flat[state["tile"]]
            assert t[0] == name, (t[0], name)
            state["tile"] += 1
            n = state["tile"]
            w = t[2] * t[4]
            v = ring[:, bi % RING, x:x + w].rearrange("p (k c) -> p k c", k=t[2])
            closes = n == len(flat) or flat[n][1] != bi
            return v, (s_w[bi % RING], 16 * (bi // RING + 1)), (bi if closes else None)

        def used(bi, tok):
            if bi is not None:
                state["freed"][bi] = tok

        free = [[] for _ in range(8)]
        turn = [0]

        def bank(n=1):
            b = turn[0]
            if b % n or b + n > 8:
                b = -(-b // n) * n % 8
            turn[0] = (b + n) % 8
            w = [t for i in range(n) for t in free[b + i]]
            return b, w

        def release(b, *toks, n=1):
            for i in range(n):
                free[b + i] = list(toks)

        def mm(out, lhsT, rhs, start, stop, *waits, inc=False):
            return PE(lambda e: e.matmul(out, lhsT, rhs, start=start, stop=stop), *waits, inc=inc, chain=False)

        def tr(out, in_, *waits, inc=False):
            k = in_.shape[0]
            return PE(lambda e: e.transpose(out, in_, con("ident")[0:k, 0:k]), *waits, IN_CON, inc=inc, chain=False)

        def tt(E, out, a, b, op, *w, chain=True):
            return E(lambda e: e.tensor_tensor(out, a, b, op), *w, chain=chain)

        def ts(E, out, a, s1, s2, o0, o1, *w, chain=True):
            return E(lambda e: e.tensor_scalar(out, a, s1, s2, o0, o1) if o1 is not None
                     else e.tensor_scalar(out, a, s1, None, o0), *w, chain=chain)

        def stt(E, out, a, s, b, o0, o1, *w, chain=True):
            return E(lambda e: e.scalar_tensor_tensor(out=out, in0=a, scalar=s, in1=b, op0=o0, op1=o1), *w, chain=chain)

        def cp(E, out, a, *w, chain=True):
            if E is AC:
                return E(lambda e: e.activation(out, a, ACT.Copy), *w, chain=chain)
            return E(lambda e: e.tensor_copy(out, a), *w, chain=chain)

        def act(out, a, f, *w, bias=0.0, scale=1.0, accum=None, chain=True):
            return AC(lambda e: e.activation(out, a, f, bias=bias, scale=scale, accum_out=accum), *w, chain=chain)

        def mset(E, out, v, *w):
            return E(lambda e: e.memset(out, v), *w)

        def red(out, a, op, *w):
            return DV(lambda e: e.tensor_reduce(out, a, AX.X, op), *w)

        def rec(out, a, *w):
            return DV(lambda e: e.reciprocal(out, a), *w)

        def rsq(out, a, eps, *w):
            t = ts(DV, out, a, eps, None, ADD, None, *w)
            t = act(out, out, ACT.Sqrt, t)
            return rec(out, out, t)

        def linear(name, n, x, T, evac, *waits):
            toks = []
            for e in range(n):
                wv, wt, closes = weight(name)
                nk, cw = wv.shape[1], wv.shape[2]
                b, fr = bank()
                out = PS[0:cw, b, 0:T]
                for k in range(nk):
                    tok = mm(out, wv[:, k, :], x[:, k, :], k == 0, k == nk - 1, *(fr + [wt] + list(waits) if k == 0 else []),
                             inc=k == nk - 1)
                used(closes, tok)
                tk = evac(e, out, tok)
                release(b, tk)
                toks.append(tk)
            return toks

        def linear_t(name, n, x, spans, evac, *waits):
            out_t = []
            for i in range(n):
                wv, wt, closes = weight(name)
                nk, cw = wv.shape[1], wv.shape[2]
                for j, (t0, tn) in enumerate(spans):
                    b, fr = bank()
                    out = PS[0:tn, b, 0:cw]
                    for k in range(nk):
                        tok = mm(out, x[:, k, t0:t0 + tn], wv[:, k, :], k == 0, k == nk - 1,
                                 *(fr + [wt] + list(waits) if k == 0 else []), inc=k == nk - 1)
                    tk = evac(i, j, out, tok)
                    release(b, tk)
                    out_t.append(tk)
                used(closes, tok)
            return out_t

        def colsum(mat, src, n, T, *waits):
            b, fr = bank()
            for k in range(n):
                tok = mm(PS[:, b, 0:T], con(mat), src[:, k, :], k == 0, k == n - 1, *(fr + [IN_CON] + list(waits) if k == 0 else []),
                         inc=k == n - 1)
            return b, tok

        def layer_norm(src, dst, tmp, small, T, g, bb, *waits):
            b, tok = colsum("o1024", src, 8, T, *waits)
            t = tt(DV, src, src, bc(PS[:, b, None, 0:T], 8, T), SUB, tok)
            release(b, t)
            t = act(tmp, src, ACT.Square, t)
            b, tok = colsum("o1024", tmp, 8, T, t)
            t = rsq(small, PS[:, b, 0:T], 1e-5, tok)
            release(b, t)
            t = tt(DV, src, src, bc(small[:, None, :], 8, T), MUL)
            for k in range(8):
                o = act(dst[:, k, :], src[:, k, :], ACT.Identity, t, IN_PAR, bias=par(bb)[:, k:k + 1],
                        scale=par(g)[:, k:k + 1], chain=False)
            return o

        def rms_norm(src, dst, tmp, small, n, T, g, mat, *waits):
            t = act(tmp, src, ACT.Square, *waits)
            b, tok = colsum(mat, tmp, n, T, t)
            t = rsq(small, PS[:, b, 0:T], 1e-6, tok)
            release(b, t)
            for k in range(n):
                o = stt(DV, dst[:, k, :], src[:, k, :], par(g)[:, k:k + 1], small, MUL, MUL, t, IN_PAR, *waits)
            return o

        def done():
            return everything()

        AB = 8 * T0
        phases = []

        X = at(0, 8, T0)
        Q, K = at(AB, 8, T0), at(2 * AB, 8, T0)
        O, H = at(3 * AB, 8, T0), at(4 * AB, 8, T0)
        VT = at(5 * AB, 4, 1024)
        base = 5 * AB + 4096
        QT = [(0, 128), (128, 128), (256, 16)]

        def attention():
            linear("attn_qk", 16, X, T0, lambda e, ps, tok: cp(AC if e % 2 else DV, (Q if e < 8 else K)[:, e % 8, :], ps, tok), IN_X)
            c0 = [0, 384, 768]
            linear_t("attn_v", 3, X, QT, lambda i, j, ps, tok: cp(AC if j else DV, VT[0:ps.shape[0], j, c0[i]:c0[i] + ps.shape[1]], ps, tok))
            lam = at(base, 8)
            pr = at(base + 8, 64)
            for i in (1, 2):
                t = tt(DV, pr, par(f"lam_q{i}"), par(f"lam_k{i}"), MUL, IN_PAR)
                red(lam[:, i - 1:i], pr, ADD)
            t = act(lam[:, 2:4], lam[:, 0:2], ACT.Exp, DV.last())
            t = tt(DV, lam[:, 4:5], lam[:, 3:4], lam[:, 2:3], SUB, t)
            t = ts(DV, lam[:, 5:6], lam[:, 4:5], -LAM_INIT, None, ADD, None)
            nlam = lam[:, 5:6]
            o = base + 128
            NB = 2
            st = [at(o + i * 2 * T0, 2, T0) for i in range(NB)]
            o += NB * 2 * T0
            ex = [at(o + i * 2 * T0, 2, T0) for i in range(NB)]
            o += NB * 2 * T0
            sm = [at(o + i * 16, 16) for i in range(NB)]
            o += NB * 16
            aT = [at(o + i * 3 * T0, 3, T0) for i in range(2)]
            barrier = done()
            scale = 64.0 ** -0.5
            ready, freeS = {}, [[], []]
            freeT = [[], []]

            def scores(u):
                h, qi = u // 3, u % 3
                q0, qn = QT[qi]
                i = u % NB
                b, fr = bank(2)
                for c in range(2):
                    tok = mm(PS[0:qn, b + c, 0:T0], Q[64 * c:64 * c + 64, h, q0:q0 + qn], K[64 * c:64 * c + 64, h, :],
                             True, True, *(fr + barrier), inc=c == 1)
                slope = 2.0 ** -(h + 1)
                S, E, m = st[i][0:qn], ex[i][0:qn], sm[i][0:qn]
                t = stt(DV, S, bc(con("negd")[0:qn, None, T0 * qi:T0 * qi + T0], 2, T0), slope / scale, PS[0:qn, b:b + 2, 0:T0],
                        MUL, ADD, tok, IN_CON, *freeS[i])
                release(b, t, n=2)
                red(m[:, 0:2], S, MAXO)
                t = ts(DV, m[:, 2:4], m[:, 0:2], -scale, None, MUL, None)
                for c in range(2):
                    t = act(E[:, c, :], S[:, c, :], ACT.Exp, DV.last() if c == 0 else None, bias=m[:, 2 + c:3 + c], scale=scale, accum=m[:, 4 + c:5 + c])
                rec(m[:, 6:8], m[:, 4:6], t)
                tt(DV, m[:, 8:9], m[:, 7:8], nlam[0:qn], MUL)
                ts(DV, S[:, 0, :], E[:, 0, :], m[:, 6:7], None, MUL, None)
                ready[u] = stt(DV, S[:, 1, :], E[:, 1, :], m[:, 8:9], S[:, 0, :], MUL, ADD)

            def rest(u):
                h, qi = u // 3, u % 3
                q0, qn = QT[qi]
                i = u % NB
                b, fr = bank()
                pt = PS[:, b, 0:384].rearrange("p (k q) -> p k q", k=3)
                for kt, (k0, kn) in enumerate(QT):
                    tok = tr(pt[0:kn, kt, 0:qn], st[i][0:qn, 1, k0:k0 + kn], ready[u], *fr, inc=kt == 2)
                freeS[i] = [tok]
                w = freeT[h % 2] if qi == 0 else []
                cp(AC, aT[h % 2][:, 0:2, q0:q0 + qn], pt[:, 0:2, 0:qn], tok, *w)
                t = cp(AC, aT[h % 2][0:16, 2, q0:q0 + qn], pt[0:16, 2, 0:qn])
                release(b, t)
                if qi == 2:
                    b, fr = bank()
                    for kt, (k0, kn) in enumerate(QT):
                        tok = mm(PS[:, b, 0:T0], VT[0:kn, kt, 128 * h:128 * h + 128], aT[h % 2][0:kn, kt, :], kt == 0, kt == 2,
                                 t, *fr, inc=kt == 2)
                    freeT[h % 2] = [tok]
                    release(b, cp(AC, O[:, h, :], PS[:, b, 0:T0], tok))

            for u in range(25):
                if u < 24:
                    scores(u)
                if u:
                    rest(u - 1)
            t = act(H, O, ACT.Square)
            for h in range(8):
                b, tok = colsum("o128", H[:, h:h + 1, :], 1, T0, t)
                t2 = rsq(Q[:, h, :], PS[:, b, 0:T0], 1e-5, tok)
                release(b, t2)
            ts(DV, lam[:, 6:7], par("subln"), 1.0 - LAM_INIT, None, MUL, None)
            t = stt(DV, O, O, lam[:, 6:7], Q, MUL, MUL, t)
            linear("attn_o", 8, O, T0, lambda e, ps, tok: stt(DV, H[:, e, :], X[:, e, :], ALPHA, ps, MUL, ADD, tok), *done())
            layer_norm(H, X, O, at(base, T0), T0, "ln_g00", "ln_b00", *done())

        phases.append(attention)

        HF = at(2 * AB, 22, T0)

        def glu(name, hf, T, tmpo, x, *waits):
            sg = [at(tmpo + 512 * i, 2, 256) if T == 256 else at(tmpo + 2 * T0 * i, 2, T0) for i in range(2)]
            hold = {}

            def evac(e, ps, tok):
                f = e // 2
                if e % 2 == 0:
                    t = act(sg[f % 2][:, 0, :], ps, ACT.Sigmoid, tok, hold.get(f - 2))
                    return tt(DV, sg[f % 2][:, 1, :], ps, sg[f % 2][:, 0, :], MUL, t)
                t = tt(DV, hf[:, f, :], sg[f % 2][:, 1, :], ps, MUL, tok)
                hold[f] = t
                return t

            return linear(name, 44, x, T, evac, *waits)

        def ffn():
            R = at(AB, 8, T0)
            glu("ffn_gu", HF, T0, 5 * AB, X, *done())
            linear("ffn_d", 8, HF, T0, lambda e, ps, tok: stt(DV, R[:, e, :], X[:, e, :], ALPHA, ps, MUL, ADD, tok), *done())
            layer_norm(R, X, at(2 * AB, 8, T0), at(3 * AB, T0), T0, "ln_g01", "ln_b01", *done())

        phases.append(ffn)

        Rr, Kr, Vr = at(AB, 8, T0), at(2 * AB, 8, T0), at(3 * AB, 8, T0)
        KK, KD, Yb = at(3 * AB, 8, T0), at(4 * AB, 8, T0), at(8 * AB // 2 + AB, 8, T0)
        vt_o = 6 * AB
        VC = at(vt_o, 4, 1024)
        hid_o = vt_o + 4096
        HW, HA, HG, HG2 = (at(hid_o + i * T0, T0) for i in range(4))
        grp_o = hid_o + 4 * T0

        def rwkv_project():
            DP, DN, XS = at(grp_o, 8, T0), at(4 * AB, 8, T0), at(5 * AB, 8, T0)
            bar = done()
            ts(DV, DP[:, :, 0:1], X[:, :, 0:1], -1.0, None, MUL, None, *bar)
            tt(DV, DP[:, :, 1:T0], X[:, :, 0:T0 - 1], X[:, :, 1:T0], SUB)
            ts(DV, DN[:, :, T0 - 1:T0], X[:, :, T0 - 1:T0], -1.0, None, MUL, None)
            tt(DV, DN[:, :, 0:T0 - 1], X[:, :, 1:T0], X[:, :, 0:T0 - 1], SUB)

            def mix(m):
                bar = done()
                for k in range(8):
                    stt(DV, XS[:, k, :], DP[:, k, :], par(f"mu0{m}")[:, k:k + 1], X[:, k, :], MUL, ADD, *bar)
                    t = stt(DV, XS[:, k, :], DN[:, k, :], par(f"mu1{m}")[:, k:k + 1], XS[:, k, :], MUL, ADD)
                return t

            for m, dst in enumerate((Rr, Kr, Vr)):
                t = mix(m)
                linear(f"rkv{m}", 8, XS, T0, lambda e, ps, tok: cp(AC, dst[:, e, :], ps, tok), t)
            t = mix(3)
            linear("lw", 1, XS, T0, lambda e, ps, tok: act(HW, ps, ACT.Tanh, tok), t)
            t = mix(4)
            linear("la", 1, XS, T0, lambda e, ps, tok: cp(AC, HA, ps, tok), t)
            t = mix(5)
            linear("lg", 2, XS, T0, lambda e, ps, tok: act((HG, HG2[0:32])[e], ps, ACT.Sigmoid, tok), t)
            bar = done()
            for c in range(4):
                for hf in range(2):
                    b, fr = bank()
                    for d in range(4):
                        tok = tr(PS[0:C, b, 128 * d:128 * d + 128], Vr[:, 4 * hf + d, C * c:C * c + C], *(fr + bar), inc=d == 3)
                    release(b, cp(AC, VC[0:C, c, 512 * hf:512 * hf + 512], PS[0:C, b, :], tok))
            bar = done()
            sq = at(grp_o, 8, T0)
            for k in range(8):
                t = ts(DV, KK[:, k, :], Kr[:, k, :], par("k_k")[:, k:k + 1], None, MUL, None, *bar)
            t = act(sq, KK, ACT.Square, t)
            nrm = at(grp_o + AB, T0)
            for k in range(8):
                b, tok = colsum("blk", sq[:, k:k + 1, :], 1, T0, t)
                t1 = act(nrm, PS[:, b, 0:T0], ACT.Sqrt, tok, DV.last())
                release(b, t1)
                ts(DV, nrm, nrm, 1e-12, None, MAXO, None, t1)
                rec(nrm, nrm)
                tt(DV, KK[:, k, :], KK[:, k, :], nrm, MUL)

        phases.append(rwkv_project)

        def rwkv_scan():
            o = grp_o
            ARb = at(o, 2, 4, T0)
            o += 8 * T0
            Bb, Kb, t1b, t2b = (at(o + i * 4 * T0, 4, T0) for i in range(4))
            o += 16 * T0
            W = 8 * C
            U, Xi, Yi, TT, GKA, GKR, GBR = (at(o + i * W, 2, 4, C) for i in range(7))
            o += 7 * W
            Kt, Bt = (at(o + i * 512, 4, 128) for i in range(2))
            o += 1024
            Z, NS = (at(o + i * 512, 2, 4, 64) for i in range(2))
            o += 1024
            S = at(o, 4, 64)
            o += 256
            PCt = at(o, 4, 4)
            o += 16
            one = at(o, T0)
            o += T0
            bar = done()
            mset(DV, one, 1.0, *bar)
            mset(DV, one.rearrange("p (c t) -> p c t", c=4)[:, :, 0:1], 0.0)

            def group(n, hf):
                d0 = 4 * hf
                bar = done()
                for d in range(4):
                    b, fr = bank()
                    tok = mm(PS[:, b, 0:T0], res("w2")[64 * n:64 * n + 64, 128 * (d0 + d):128 * (d0 + d) + 128],
                             HW[64 * n:64 * n + 64, :], True, True, *(fr + bar + [IN_RES]), inc=True)
                    release(b, act(t1b[:, d, :], PS[:, b, 0:T0], ACT.Sigmoid, tok, *bar, bias=par(f"w0{n}")[:, d0 + d:d0 + d + 1]))
                    b, fr = bank()
                    tok = mm(PS[:, b, 0:T0], res("a2")[64 * n:64 * n + 64, 128 * (d0 + d):128 * (d0 + d) + 128],
                             HA[64 * n:64 * n + 64, :], True, True, *fr, inc=True)
                    t = act(t2b[:, d, :], PS[:, b, 0:T0], ACT.Sigmoid, tok, bias=par(f"a0{n}")[:, d0 + d:d0 + d + 1])
                    release(b, t)
                kk, r, k = KK[:, d0:d0 + 4, :], Rr[:, d0:d0 + 4, :], Kr[:, d0:d0 + 4, :]
                kds = KD[:, d0:d0 + 4, :]
                Ab, Rb = ARb[:, 0], ARb[:, 1]
                tt(DV, Bb, kk, t2b, MUL, t, *bar)
                for d in range(4):
                    ka = par("k_a")[:, d0 + d:d0 + d + 1]
                    ts(DV, t2b[:, d, :], t2b[:, d, :], -1.0, ka, ADD, MUL)
                stt(DV, Kb, t2b, 1.0, k, ADD, MUL)
                if n == 0:
                    cp(DV, kds, Kb)
                else:
                    tt(DV, kds, kds, Kb, ADD)
                ts(DV, t1b, t1b, -float(np.exp(-0.5)), None, MUL, None)
                for d in range(4):
                    cum, ld = Ab[:, d, :], t1b[:, d, :]
                    if n == 1:
                        cum, ld = cum[:, ::-1], ld[:, ::-1]
                    t = DV(lambda e, cum=cum, ld=ld: e.tensor_tensor_scan(cum, one, ld, 0.0, MUL, ADD))
                t2 = act(t2b, Ab, ACT.Exp, t)
                tt(DV, Rb, r, t2b, MUL, t2)
                last = C - 1 if n == 0 else 0
                t = cp(DV, PCt, t2b.rearrange("p a (c t) -> p a c t", c=4)[:, :, :, last])
                t2 = act(t2b, Ab, ACT.Exp, t, scale=-1.0)
                tt(DV, Bb, Bb, t2b, MUL, t2)
                t = tt(DV, Kb, Kb, t2b, MUL)
                t = tt(DV, t1b, Ab, t1b, SUB)
                t2 = act(t1b, t1b, ACT.Exp, t)
                t = tt(DV, Ab, kk, t1b, MUL, t2)
                mset(DV, S, 0.0)
                order = range(4) if n == 0 else range(3, -1, -1)
                strict, nstrict, incl = ("up", "nup", "upi") if n == 0 else ("dn", "ndn", "dni")
                lx, ly = ("lu", "ld") if n == 0 else ("ld", "lu")
                for ci, c in enumerate(order):
                    chunk(n, hf, c, ci, strict, nstrict, incl, lx, ly)

            def chunk(n, hf, c, ci, strict, nstrict, incl, lx, ly):
                bar = done()
                cs = slice(C * c, C * c + C)
                m = {}
                for name, lh, rh, dst, mask in (("u", Bb, 0, U, nstrict), ("gbr", Bb, 1, GBR, incl),
                                                ("gka", Kb, 0, GKA, strict), ("gkr", Kb, 1, GKR, incl)):
                    b, fr = bank(2)
                    for p in range(2):
                        for i in range(4):
                            rows = slice(64 * p, 64 * p + 64)
                            tok = mm(PS[0:C, b + p, C * i:C * i + C], lh[rows, i, cs], ARb[rows, rh, i, cs], True, True,
                                     *(fr + bar if p + i == 0 else []), inc=p * i == 3)
                    for p in range(2):
                        t = tt(DV, dst[0:C, p], PS[0:C, b + p, 0:4 * C].rearrange("s (i t) -> s i t", i=4),
                               bc(con(mask)[0:C, None, :], 4, C), MUL, tok)
                    release(b, t, n=2)
                for src, dst in ((Kb, Kt), (Bb, Bt)):
                    b, fr = bank()
                    for d in range(4):
                        tok = tr(PS[0:C, b, 128 * d:128 * d + 128], src[:, d, cs], *fr, inc=d == 3)
                    tkb = cp(AC, dst[0:C], PS[0:C, b, :].rearrange("s (d k) -> s d k", d=4), tok)
                    release(b, tkb)
                idb = bc(con("ident")[0:C, None, 0:C], 4, C)
                for p in range(2):
                    cp(DV, Xi[0:C, p], idb)
                    t = cp(DV, Yi[0:C, p], idb)
                for lv in range(7):
                    b, fr = bank(2)
                    for p in range(2):
                        for i in range(4):
                            tok = mm(PS[0:C, b + p, C * i:C * i + C], U[0:C, p, i, :], Yi[0:C, p, i, :], True, True,
                                     *(fr + [t] if p + i == 0 else []), inc=p * i == 3)
                    t = cp(AC, TT[0:C].rearrange("s p i t -> s p (i t)"), PS[0:C, b:b + 2, 0:4 * C], tok)
                    release(b, t, n=2)
                    for dst, msk, swap in ((Xi, f"{lx}{lv}", False), (Yi, f"{ly}{lv}", True)):
                        if swap and lv == 6:
                            continue
                        b, fr = bank(2)
                        for p in range(2):
                            for i in range(4):
                                a_, b_ = (Xi, TT) if swap else (TT, Xi)
                                tok = mm(PS[0:C, b + p, C * i:C * i + C], a_[0:C, p, i, :], b_[0:C, p, i, :], True, True,
                                         *(fr + [t] if p + i == 0 else []), inc=p * i == 3)
                        m[swap] = (dst, msk, b, tok)
                    ptok = PE.last()
                    for swap in ((False, True) if lv < 6 else (False,)):
                        dst, msk, b, _ = m[swap]
                        for p in range(2):
                            def pred(e, dst=dst, msk=msk, b=b, p=p):
                                return e.copy_predicated(dst[0:C, p], bc(con(msk)[0:C, None, :], 4, C).bitcast(u32),
                                                         PS[0:C, b + p, 0:4 * C].rearrange("s (i t) -> s i t", i=4))
                            t = DV(pred, ptok)
                        release(b, t, n=2)
                zt = t
                b, fr = bank(2)
                for p in range(2):
                    rows = slice(64 * p, 64 * p + 64)
                    for i in range(4):
                        hh = 2 * (4 * hf + i) + p
                        out = PS[0:C, b + p, 64 * i:64 * i + 64]
                        if ci:
                            mm(out, ARb[rows, 0, i, cs], S[rows, i, :], True, False, *(fr + done()))
                        tok = mm(out, GKA[0:C, p, i, :], VC[0:C, c, 64 * hh:64 * hh + 64], not ci, True, *(fr + done()), inc=p * i == 3)
                t = cp(AC, Z[0:C].rearrange("s p i v -> s p (i v)"), PS[0:C, b:b + 2, 0:256], tok)
                release(b, t, n=2)
                b, fr = bank(2)
                for p in range(2):
                    for i in range(4):
                        tok = mm(PS[0:C, b + p, 64 * i:64 * i + 64], Xi[0:C, p, i, :], Z[0:C, p, i, :], True, True, t, zt, *fr, inc=p * i == 3)
                t = act(NS[0:C].rearrange("s p i v -> s p (i v)"), PS[0:C, b:b + 2, 0:256], ACT.Copy, tok, scale=-1.0)
                release(b, t, n=2)
                b, fr = bank(2)
                for p in range(2):
                    rows = slice(64 * p, 64 * p + 64)
                    for i in range(4):
                        hh = 2 * (4 * hf + i) + p
                        out = PS[rows, b + p, C * i:C * i + C]
                        if ci:
                            mm(out, S[rows, i, :], ARb[rows, 1, i, cs], True, False, t, *fr)
                        mm(out, VC[0:C, c, 64 * hh:64 * hh + 64], GKR[0:C, p, i, :], not ci, False, t, *fr)
                        tok = mm(out, NS[0:C, p, i, :], GBR[0:C, p, i, :], False, True, t, inc=p * i == 3)
                for p in range(2):
                    rows = slice(64 * p, 64 * p + 64)
                    y = Yb[rows, 4 * hf:4 * hf + 4, cs]
                    src = PS[rows, b + p, 0:4 * C].rearrange("v (i t) -> v i t", i=4)
                    ty = cp(DV, y, src, tok) if n == 0 else tt(DV, y, y, src, ADD, tok)
                release(b, ty, n=2)
                b, fr = bank()
                for p in range(2):
                    rows = slice(64 * p, 64 * p + 64)
                    for i in range(4):
                        hh = 2 * (4 * hf + i) + p
                        out = PS[rows, b, 64 * i:64 * i + 64]
                        mm(out, Kt[0:C, i, 64 * p:64 * p + 64], VC[0:C, c, 64 * hh:64 * hh + 64], True, False, tkb, *fr)
                        tok = mm(out, Bt[0:C, i, 64 * p:64 * p + 64], NS[0:C, p, i, :], False, True, inc=p * i == 3)
                t = tt(DV, S, S, PS[:, b, 0:256].rearrange("k (i v) -> k i v", i=4), ADD, tok)
                release(b, t)
                tt(DV, S, S, bc(PCt[:, :, c:c + 1], 4, 64), MUL)

            for hf in range(2):
                for n in range(2):
                    group(n, hf)

        phases.append(rwkv_scan)

        def rwkv_out():
            bar = done()
            sq = at(grp_o, 8, T0)
            sm = at(grp_o + AB, T0)
            sm2 = at(grp_o + AB + T0, T0)
            for k in range(8):
                b, tok = colsum("blk64", Yb[:, k:k + 1, :], 1, T0, *bar)
                t = tt(DV, Yb[:, k, :], Yb[:, k, :], PS[:, b, 0:T0], SUB, tok)
                release(b, t)
            t = act(sq, Yb, ACT.Square, t)
            for k in range(8):
                b, tok = colsum("blk64", sq[:, k:k + 1, :], 1, T0, t)
                t1 = rsq(sm, PS[:, b, 0:T0], 64e-5, tok)
                release(b, t1)
                tt(DV, Yb[:, k, :], Yb[:, k, :], sm, MUL)
                t2 = ts(DV, Yb[:, k, :], Yb[:, k, :], par("lnx_g")[:, k:k + 1], par("lnx_b")[:, k:k + 1], MUL, ADD)
            for k in range(8):
                t = stt(DV, KD[:, k, :], KD[:, k, :], par("r_k")[:, k:k + 1], Rr[:, k, :], MUL, MUL)
            vf = at(grp_o, 8, T0)
            bar = done()
            for c in range(4):
                for hf in range(2):
                    b, fr = bank()
                    for d in range(4):
                        tok = tr(PS[:, b, C * d:C * d + C], VC[0:C, c, 512 * hf + 128 * d:512 * hf + 128 * d + 128], *(fr + bar), inc=d == 3)
                    tv = cp(AC, vf[:, 4 * hf:4 * hf + 4, C * c:C * c + C], PS[:, b, 0:4 * C].rearrange("p (d t) -> p d t", d=4), tok)
                    release(b, tv)
            for k in range(8):
                b, tok = colsum("blk", KD[:, k:k + 1, :], 1, T0, t)
                t1 = tt(DV, sm, PS[:, b, 0:T0], vf[:, k, :], MUL, tok, tv)
                release(b, t1)
                tt(DV, Yb[:, k, :], Yb[:, k, :], sm, ADD)
                b, fr = bank()
                mm(PS[:, b, 0:T0], res("g2")[:, 128 * k:128 * k + 128], HG, True, False, *fr)
                tok = mm(PS[:, b, 0:T0], res("g2b")[0:32, 128 * k:128 * k + 128], HG2[0:32, :], False, True, inc=True)
                t2 = tt(DV, Yb[:, k, :], Yb[:, k, :], PS[:, b, 0:T0], MUL, tok)
                release(b, t2)
            R = at(AB, 8, T0)
            linear("rw_o", 8, Yb, T0, lambda e, ps, tok: stt(DV, R[:, e, :], X[:, e, :], ALPHA, ps, MUL, ADD, tok), *done())
            layer_norm(R, X, at(2 * AB, 8, T0), at(3 * AB, T0), T0, "ln_g10", "ln_b10", *done())

        phases.append(rwkv_out)

        T = T1
        XA = 8 * T
        Xm = X[:, :, 16:T0]

        def moe():
            bar = done()
            o = AB
            YA = at(o, 2, 1024)
            o += 2048
            lg, gt = at(o, 2, 8), at(o + 16, 2, 8)
            gq = at(o + 32, 2, 8, 8)
            g2 = at(o + 160, 2, 8, 8)
            s8 = at(o + 288, 2, 8)
            s1 = at(o + 304, 4)
            o += 320
            evs = linear_t("router", 1, Xm, [(0, 128), (128, 128)],
                           lambda i, j, ps, tok: tt(DV, lg[:, j, :], ps, par("b_router"), ADD, tok), *bar)
            red(s1[:, 0:2], lg, MAXO)
            tt(DV, lg, lg, bc(s1[:, 0:2, None], 2, 8), SUB)
            t = act(lg, lg, ACT.Exp, DV.last())
            red(s1[:, 0:2], lg, ADD, t)
            rec(s1[:, 2:4], s1[:, 0:2])
            tt(DV, lg, lg, bc(s1[:, 2:4, None], 2, 8), MUL)
            for j in range(2):
                pe_ = bc(lg[:, j, :, None], 8, 8)
                pj = bc(lg[:, j, None, :], 8, 8)
                tt(DV, gq[:, j], pj, pe_, ALU.is_gt)
                tt(DV, g2[:, j], pj, pe_, ALU.is_equal)
                tt(DV, g2[:, j], g2[:, j], con("before").rearrange("p (e j) -> p e j", e=8), MUL)
                tt(DV, gq[:, j], gq[:, j], g2[:, j], ADD)
            red(s8, gq, ADD)
            ts(DV, s8, s8, 2.0, None, ALU.is_lt, None)
            tt(DV, gt, s8, lg, MUL)
            red(s1[:, 0:2], gt, ADD)
            rec(s1[:, 2:4], s1[:, 0:2])
            tt(DV, gt, gt, bc(s1[:, 2:4, None], 2, 8), MUL)
            bar = done()
            NH = 3
            hh = [at(o + i * T, T) for i in range(NH)]
            o += NH * T
            sg = [at(o + i * 2 * T, 2, T) for i in range(2)]
            gfree = [list(free[i]) for i in range(4)]
            dfree = [t for i in range(4, 8) for t in free[i]]
            NF = FE // 128
            hold, wd, hfree = {}, {}, {}

            def up(u):
                b = u % 4
                for g in range(2):
                    wv, wt, _ = weight("moe")
                    for k in range(8):
                        tok = mm(PS[:, b, T * g:T * g + T], wv[:, k, :], Xm[:, k, :], k == 0, k == 7,
                                 *(gfree[b] + [wt] + bar if k == 0 else []), inc=k == 7)
                    if g == 0:
                        t = None
                wv, wt, bi = weight("moe")
                wd[u] = (wv, bi)
                s = sg[u % 2]
                t = act(s[:, 0, :], PS[:, b, 0:T], ACT.Sigmoid, tok, hold.get(u - 2), chain=False)
                t = tt(DV, s[:, 1, :], PS[:, b, 0:T], s[:, 0, :], MUL, t)
                t = tt(DV, hh[u % NH], PS[:, b, T:2 * T], s[:, 1, :], MUL, hfree.get(u - NH))
                gfree[b] = [t]
                hold[u] = t

            def down(u):
                nonlocal dfree
                e, f = divmod(u, NF)
                wv, bi = wd.pop(u)
                for j in range(2):
                    for n in range(2):
                        tok = mm(PS[:, 4 + 2 * j + n, :], hh[u % NH][:, 128 * j:128 * j + 128], wv[:, 0, 512 * n:512 * n + 512],
                                 f == 0, f == NF - 1, hold[u], *(dfree if f == 0 else []), inc=j + n == 2)
                used(bi, tok)
                hfree[u] = tok
                if f == NF - 1:
                    for j in range(2):
                        y = YA[:, j, :].rearrange("p (n c) -> p n c", n=2)
                        src = PS[:, 4 + 2 * j:6 + 2 * j, :]
                        g = gt[:, j, e:e + 1]
                        if e == 0:
                            t = ts(DV, y, src, g, None, MUL, None, tok)
                        else:
                            t = stt(DV, y, src, g, y, MUL, ADD, tok)
                    dfree = [t]

            NU = NE * NF
            for u in range(NU + 1):
                if u < NU:
                    up(u)
                if u:
                    down(u - 1)
            for i in range(4):
                release(i, *gfree[i])
                release(4 + i, *dfree)
            R = at(AB + 4096, 8, T)
            bar = done()
            for d in range(8):
                b, fr = bank()
                for j in range(2):
                    tok = tr(PS[:, b, 128 * j:128 * j + 128], YA[:, j, 128 * d:128 * d + 128], *(fr + bar), inc=j == 1)
                t = stt(DV, R[:, d, :], Xm[:, d, :], ALPHA, PS[:, b, 0:T], MUL, ADD, tok, *bar)
                release(b, t)
            layer_norm(R, at(0, 8, T), at(AB + 4096 + XA, 8, T), at(AB + 4096 + 2 * XA, T), T, "ln_g11", "ln_b11", *done())

        phases.append(moe)

        X2 = at(0, 8, T)
        SP2 = [(0, 128), (128, 128)]

        def even():
            o = XA
            HN, TMP = at(o, 8, T), at(o + XA, 8, T)
            CAT = at(o + 2 * XA, 8, T)
            o += 3 * XA
            small = at(o, T)
            o += T
            tabs, posf = {}, at(o, 2)
            o += 8
            bar = done()
            cp(DV, posf, pos_t[:, :], IN_POS, *bar)
            tw = [at(o + 64 * i, 2, 32) for i in range(3)]
            o += 192
            for hlf in (16, 32):
                for fn, ph in (("sin", 0.0), ("cos", 0.25)):
                    tab = at(o, 2, hlf)
                    o += 2 * hlf
                    a, n_, r = (x[:, :, 0:hlf] for x in tw)
                    for j in range(2):
                        ts(DV, a[:, j, :], con(f"inv{hlf}"), posf[:, j:j + 1], None, MUL, None, IN_CON, *(AC.last(),))
                    ts(DV, n_, a, 1.0 / (2 * np.pi), ph, MUL, ADD)
                    ts(DV, n_, n_, 12582912.0, None, ADD, None)
                    ts(DV, n_, n_, 12582912.0, None, SUB, None)
                    stt(DV, r, n_, -6.28125, a, MUL, ADD)
                    stt(DV, r, n_, -float(np.float32(2 * np.pi - 6.28125)), r, MUL, ADD)
                    ts(DV, r, r, 2 * np.pi * ph, None, ADD, None)
                    ts(DV, r, r, 3.1415925, -3.1415925, ALU.min, ALU.max)
                    act(tab, r, ACT.Sin, DV.last())
                    tabs[fn, hlf] = tab
            lgm = at(o, 8, 8)
            o += 64
            for i, n in enumerate(("th_f", "th_b")):
                y, u, d, l = (lgm[:, 4 * i + k, :] for k in range(4))
                t = act(y, par(n), ACT.Exp, IN_PAR, *bar, scale=-float(np.log(2.0)))
                ts(DV, u, y, -1.0, 1.0, MUL, ADD, t)
                t = stt(DV, d, u, -1.0, y, ADD, ADD)
                t = act(l, u, ACT.Ln, t)
                rec(u, u, t)
                tt(DV, d, d, u, MUL)
                tt(DV, l, l, d, SUB)
            lgf, lgb = lgm[:, 3, :], lgm[:, 7, :]
            rms_norm(X2, HN, TMP, small, 8, T, "n_even", "o1024", *done())
            bar = done()
            CQ = at(o, 5, T)
            o += 5 * T
            linear("e_c", 5, HN, T, lambda e, ps, tok: cp(AC, CQ[:, e, :], ps, tok), *bar)
            KRO = at(o, 2, 32)
            o += 64
            linear_t("e_kr", 1, HN, SP2, lambda i, j, ps, tok: cp(AC, KRO[:, j, :], ps, tok))
            RQK = at(o, 2, 1024)
            o += 2048
            linear_t("e_qk", 4, HN, SP2, lambda i, j, ps, tok: cp(AC, RQK[:, j, 256 * i:256 * i + 256], ps, tok))
            RV = at(o, 2, 512)
            o += 1024
            linear_t("e_v", 2, HN, SP2, lambda i, j, ps, tok: cp(AC, RV[:, j, 256 * i:256 * i + 256], ps, tok))
            RG = at(o, 4, T)
            o += 4 * T
            GS = TMP

            def rg(e, ps, tok):
                t = act(GS[:, e, :], ps, ACT.Sigmoid, tok)
                return tt(DV, RG[:, e, :], ps, GS[:, e, :], MUL, t)

            linear("e_g", 4, HN, T, rg, *done())
            bar = done()
            CN = at(o, 5, T)
            o += 5 * T
            rms_norm(CQ[:, 0:3, :], CN[:, 0:3, :], TMP[:, 0:3, :], small, 3, T, "n_q", "o384", *bar)
            rms_norm(CQ[:, 3:5, :], CN[:, 3:5, :], TMP[:, 3:5, :], small, 2, T, "n_kv", "o256", *done())
            bar = done()
            QM, KM = at(o, 2, 8, 96), at(o + 1536, 2, 8, 96)
            o += 3072
            VM = at(o, 2, 8, 64)
            o += 1024
            linear_t("uq", 2, CN[:, 0:3, :], SP2,
                     lambda i, j, ps, tok: cp(AC, QM[:, j, 4 * i:4 * i + 4, :], ps.rearrange("p (h c) -> p h c", h=4), tok), *bar)

            def kv(i, j, ps, tok):
                v = ps.rearrange("p (h c) -> p h c", h=4)
                cp(AC, KM[:, j, 4 * i:4 * i + 4, 0:64], v[:, :, 0:64], tok)
                return cp(AC, VM[:, j, 4 * i:4 * i + 4, :], v[:, :, 64:128])

            linear_t("ukv", 2, CN[:, 3:5, :], SP2, kv)
            bar = done()
            for j in range(2):
                cp(DV, KM[:, j, :, 64:96], bc(KRO[:, j, None, :], 8, 32), *bar)

            rt = at(o, 4, 8, 32)
            o += 1024

            def rope(v, h, hlf, j):
                c = bc(tabs["cos", hlf][:, j, None, :], h, hlf)
                s = bc(tabs["sin", hlf][:, j, None, :], h, hlf)
                x1, x2 = v[:, :, 0:hlf], v[:, :, hlf:2 * hlf]
                w = [rt[:, i, 0:h, 0:hlf] for i in range(4)]
                tt(DV, w[0], x1, c, MUL, AC.last())
                tt(DV, w[1], x2, s, MUL)
                tt(DV, w[2], x2, c, MUL)
                tt(DV, w[3], x1, s, MUL)
                tt(DV, x1, w[0], w[1], SUB)
                return tt(DV, x2, w[2], w[3], ADD)

            sq = TMP.rearrange("p a t -> p (a t)")[:, 0:768].rearrange("p (h c) -> p h c", h=8)
            ss = at(o, 16)
            o += 16
            for M, g in ((QM, "n_qh"), (KM, "n_kh")):
                for j in range(2):
                    v = M[:, j]
                    tt(DV, sq, v, v, MUL, *bar)
                    red(ss[:, 0:8], sq, ADD)
                    t = ts(DV, ss[:, 0:8], ss[:, 0:8], 1.0 / 96, 1e-6, MUL, ADD)
                    t = act(ss[:, 8:16], ss[:, 0:8], ACT.Sqrt, t)
                    rec(ss[:, 8:16], ss[:, 8:16], t)
                    tt(DV, v, v, bc(ss[:, 8:16, None], 8, 96), MUL)
                    tt(DV, v, v, bc(par(g)[:, None, :], 8, 96), MUL)
                    rope(v[:, :, 64:96], 8, 16, j)
            for half in range(2):
                for j in range(2):
                    v = RQK[:, j, 512 * half:512 * half + 512].rearrange("p (h c) -> p h c", h=8)
                    rope(v, 8, 32, j)
            ts(DV, RQK[:, :, 512:1024], RQK[:, :, 512:1024], 64.0 ** -0.5, None, MUL, None)
            bar = done()
            QF, KF = at(o, 8, T), at(o + XA, 8, T)
            o += 2 * XA
            RF = HN
            for M, F in ((QM, QF), (KM, KF)):
                for j in range(2):
                    for q in range(2):
                        b, fr = bank()
                        for h in range(4):
                            tok = tr(PS[0:96, b, 128 * h:128 * h + 128], M[:, j, 4 * q + h, :], *(fr + bar), inc=h == 3)
                        release(b, cp(AC, F[0:96, 4 * q:4 * q + 4, 128 * j:128 * j + 128],
                                      PS[0:96, b, :].rearrange("p (h t) -> p h t", h=4), tok))
            for j in range(2):
                for q in range(2):
                    b, fr = bank()
                    for h in range(4):
                        tok = tr(PS[:, b, 128 * h:128 * h + 128], RQK[:, j, 512 * q + 128 * h:512 * q + 128 * h + 128], *(fr + bar), inc=h == 3)
                    tF = cp(AC, RF[:, 4 * q:4 * q + 4, 128 * j:128 * j + 128], PS[:, b, :].rearrange("p (h t) -> p h t", h=4), tok)
                    release(b, tF)
            bar = done()
            P = [at(o + 512 * i, 2, T) for i in range(2)]
            o += 1024
            PT = [at(o + 512 * i, 2, T) for i in range(2)]
            o += 1024
            sm = [at(o + 16 * i, 16) for i in range(2)]
            o += 32
            scale = 96.0 ** -0.5
            freeP, freePT, ready = [[], []], [[], []], {}

            def mscore(h):
                i = h % 2
                b, fr = bank()
                for j in range(2):
                    tok = mm(PS[:, b, T * j:T * j + T], QF[0:96, h, 128 * j:128 * j + 128], KF[0:96, h, :], True, True, *(fr + bar), inc=j == 1)
                v = PS[:, b, :].rearrange("p (j t) -> p j t", j=2)
                m = sm[i]
                red(m[:, 0:2], v, MAXO, tok)
                t = ts(DV, m[:, 2:4], m[:, 0:2], -scale, None, MUL, None)
                for j in range(2):
                    t = act(P[i][:, j, :], v[:, j, :], ACT.Exp, t if j == 0 else None, *freeP[i], bias=m[:, 2 + j:3 + j], scale=scale, accum=m[:, 4 + j:5 + j])
                release(b, t)
                rec(m[:, 6:8], m[:, 4:6], t)
                ready[h] = tt(DV, P[i], P[i], bc(m[:, 6:8, None], 2, T), MUL)

            def mrest(h):
                i = h % 2
                b, fr = bank()
                v = PS[:, b, :].rearrange("p (k t) -> p k t", k=2)
                for j in range(2):
                    for k in range(2):
                        tok = tr(v[:, k, 128 * j:128 * j + 128], P[i][:, j, 128 * k:128 * k + 128], ready[h], *fr, inc=j + k == 2)
                freeP[i] = [tok]
                t = cp(AC, PT[i], v, tok, *freePT[i])
                release(b, t)
                rows = slice(64 * (h % 2), 64 * (h % 2) + 64)
                b, fr = bank()
                for k in range(2):
                    tok = mm(PS[rows, b, 0:T], VM[:, k, h, :], PT[i][:, k, :], k == 0, k == 1, t, *fr, inc=k == 1)
                freePT[i] = [tok]
                release(b, cp(AC, CAT[rows, h // 2, :], PS[rows, b, 0:T], tok))

            for h in range(9):
                if h < 8:
                    mscore(h)
                if h:
                    mrest(h - 1)
            bar = done()
            Dt = [at(o + 512 * i, 2, T) for i in range(2)]
            o += 1024
            OR = at(o, 4, T)
            o += 4 * T
            relp, reln = (con(n).rearrange("p (j t) -> p j t", j=2) for n in ("relp", "reln"))
            fin = {}
            for h in range(8):
                i = h % 2
                rows = slice(64 * (h % 2), 64 * (h % 2) + 64)
                ts(DV, Dt[i], reln, lgb[:, h:h + 1], None, MUL, None, fin.get(h - 2), *bar)
                t = stt(DV, Dt[i], relp, lgf[:, h:h + 1], Dt[i], MUL, ADD)
                td = act(Dt[i], Dt[i], ACT.Exp, t)
                b, fr = bank()
                for j in range(2):
                    tok = mm(PS[:, b, T * j:T * j + T], RF[rows, 4 + h // 2, 128 * j:128 * j + 128], RF[rows, h // 2, :], True, True, *(fr + bar), inc=j == 1)
                t = tt(DV, Dt[i], Dt[i], PS[:, b, :].rearrange("p (j t) -> p j t", j=2), MUL, tok, td)
                release(b, t)
                b, fr = bank()
                for j in range(2):
                    tok = mm(PS[rows, b, 0:T], RV[:, j, 64 * h:64 * h + 64], Dt[i][:, j, :], j == 0, j == 1, t, *fr, inc=j == 1)
                fin[h] = tok
                release(b, cp(AC, OR[rows, h // 2, :], PS[rows, b, 0:T], tok))
            t = act(TMP[:, 0:4, :], OR, ACT.Square, *done())
            for k in range(4):
                b, tok = colsum("blk64", TMP[:, k:k + 1, :], 1, T, t)
                t1 = rsq(small, PS[:, b, 0:T], 1e-6, tok)
                release(b, t1)
                stt(DV, OR[:, k, :], OR[:, k, :], par("n_ret")[:, k:k + 1], small, MUL, MUL)
                tt(DV, CAT[:, 4 + k, :], OR[:, k, :], RG[:, k, :], MUL)
            linear("e_o", 8, CAT, T, lambda e, ps, tok: tt(DV, X2[:, e, :], X2[:, e, :], ps, ADD, tok), *done())

        phases.append(even)

        def conv_ffn(i):
            o = XA
            HN = at(o, 8, T)
            o += XA
            HF2 = at(o, 22, T)
            o += 22 * T
            small = at(o, T)
            o += T
            rms_norm(X2, HN, HF2[:, 0:8, :], small, 8, T, f"n_ffn{i}", "o1024", *done())
            bar = done()
            gp = [at(o + 258 * j, 258) for j in range(2)]
            o += 516
            cv = [at(o + 256 * j, 256) for j in range(2)]
            o += 512
            sg = [at(o + 256 * j, 256) for j in range(2)]
            for j in range(2):
                mset(DV, gp[j][:, 0:1], 0.0, *bar)
                mset(DV, gp[j][:, 257:258], 0.0)
            bar = done()
            hold, cvt = {}, {}

            def evac(e, ps, tok):
                f = e // 2
                s = f % 2
                if e % 2 == 0:
                    t = cp(AC, gp[s][:, 1:257], ps, tok, cvt.get(f - 2), *bar)
                    ts(DV, cv[s], gp[s][:, 0:256], par(f"cw{i}0")[:, f:f + 1], None, MUL, None, t)
                    stt(DV, cv[s], gp[s][:, 1:257], par(f"cw{i}1")[:, f:f + 1], cv[s], MUL, ADD)
                    t2 = stt(DV, cv[s], gp[s][:, 2:258], par(f"cw{i}2")[:, f:f + 1], cv[s], MUL, ADD)
                    t3 = act(sg[s], cv[s], ACT.Sigmoid, t2, bias=par(f"cb{i}")[:, f:f + 1])
                    cvt[f] = stt(DV, cv[s], cv[s], par(f"cb{i}")[:, f:f + 1], sg[s], ADD, MUL, t3)
                    return t
                return tt(DV, HF2[:, f, :], cv[s], ps, MUL, tok)

            linear(f"cu{i}", 44, HN, T, evac, *bar)
            linear(f"cd{i}", 8, HF2, T, lambda e, ps, tok: tt(DV, X2[:, e, :], X2[:, e, :], ps, ADD, tok), *done())

        phases.append(lambda: conv_ffn(0))

        def odd():
            o = XA
            HN, TMP = at(o, 8, T), at(o + XA, 8, T)
            o += 2 * XA
            small = at(o, T)
            o += T
            rms_norm(X2, HN, TMP, small, 8, T, "n_odd", "o1024", *done())
            bar = done()
            GQ, GK = at(o, 4, T), at(o + 4 * T, 4, T)
            o += 8 * T
            GV = at(o, 2, 1024)
            o += 2048
            GA = [at(o + T * i, T) for i in range(2)]
            o += 2 * T

            def qk(e, ps, tok):
                if e < 4:
                    return act(GQ[:, e, :], ps, ACT.Copy, tok, scale=128.0 ** -0.5)
                return cp(AC, GK[:, e - 4, :], ps, tok)

            linear("o_qk", 8, HN, T, qk, *bar)
            c0 = [0, 384, 768]
            linear_t("o_v", 3, HN, SP2, lambda i, j, ps, tok: cp(AC, GV[:, j, c0[i]:c0[i] + ps.shape[1]], ps, tok))
            linear("o_a", 2, HN, T, lambda e, ps, tok: cp(AC, GA[e][0:16, :], ps, tok))
            LA = [at(o + 4 * T * i, 4, T) for i in range(2)]
            o += 8 * T
            bar = done()
            wv, wt, closes = weight("gg")
            tmp = TMP[:, 0:4, :]
            ab = TMP[:, 4:8, :]
            for n in range(2):
                for h in range(4):
                    b, fr = bank()
                    tok = mm(PS[:, b, 0:T], wv[0:16, 0, 512 * n + 128 * h:512 * n + 128 * h + 128], GA[n][0:16, :], True, True,
                             wt, *(fr + bar), inc=True)
                    t = ts(DV, LA[n][:, h, :], PS[:, b, 0:T], par(("b_gf", "b_gb")[n])[:, h:h + 1], None, ADD, None, tok, *bar)
                    release(b, t)
                t = act(ab, LA[n], ACT.Abs, t)
                t = act(ab, ab, ACT.Exp, scale=-1.0)
                t = act(ab, ab, ACT.Ln, bias=1.0)
                t = stt(DV, LA[n], LA[n], 0.0, ab, ALU.min, SUB, t)
                t = ts(DV, LA[n], LA[n], 1.0 / 16, None, MUL, None)
            used(closes, tok)
            RGo = at(o, 8, T)
            o += 8 * T
            bar = done()

            def rg(e, ps, tok):
                t = act(TMP[:, e, :], ps, ACT.Sigmoid, tok)
                return tt(DV, RGo[:, e, :], ps, TMP[:, e, :], MUL, t)

            linear("o_g", 8, HN, T, rg, *bar)
            one = HN[:, 0:4, :]
            bar = done()
            mset(DV, one, 1.0, *bar)
            mset(DV, one.rearrange("p a (c t) -> p (a c) t", c=4)[:, :, 0:1], 0.0)
            Bc = TMP[:, 0:4, :]
            Ex = TMP[:, 4:8, :]
            QC, KC = at(o, 4, T), at(o + 4 * T, 4, T)
            QB, KE = at(o + 8 * T, 4, T), at(o + 12 * T, 4, T)
            o += 16 * T
            AT = at(o, 2, 4, 64)
            o += 512
            KDT = at(o, 2, 512)
            o += 1024
            S = at(o, 4, 256)
            o += 1024
            OG = HN
            mid = at(o, 16)
            lst = at(o + 16, 4, 4)
            o += 32

            def c4(v):
                return v.rearrange("p a (c t) -> p (a c) t", c=4)

            onef = at(o, 4, T)
            o += 4 * T
            cp(DV, onef, one)
            for n in range(2):
                bar = done()
                cumf, laf = Bc.rearrange("p a t -> p (a t)"), LA[n].rearrange("p a t -> p (a t)")
                if n == 1:
                    cumf, laf = cumf[:, ::-1], laf[:, ::-1]
                DV(lambda e, a=cumf, l=laf: e.tensor_tensor_scan(a, onef.rearrange("p a t -> p (a t)"), l, 0.0, MUL, ADD), *bar)
                mi, la = (32, 63) if n == 0 else (31, 0)
                bm = c4(Bc)[:, :, mi:mi + 1]
                bl = c4(Bc)[:, :, la:la + 1]
                t = act(Ex, Bc, ACT.Exp, DV.last())
                tt(DV, QB, GQ, Ex, MUL, t)
                t = act(lst.rearrange("p a c -> p (a c)"), bl[:, :, 0], ACT.Exp, DV.last())
                t = tt(DV, c4(Ex), bc(bl, 16, 64), c4(Bc), SUB, t)
                t = act(Ex, Ex, ACT.Exp, t)
                t = tt(DV, KE, GK, Ex, MUL, t)
                t = cp(DV, mid, bm[:, :, 0])
                t = tt(DV, c4(Bc), c4(Bc), bc(mid[:, :, None], 16, 64), SUB)
                t = act(Ex, Bc, ACT.Exp, t)
                tt(DV, QC, GQ, Ex, MUL, t)
                t = act(Ex, Bc, ACT.Exp, DV.last(), scale=-1.0)
                tt(DV, KC, GK, Ex, MUL, t)
                mset(DV, AT, 0.0)
                bar = done()
                b, fr = bank()
                for c in range(4):
                    rows = slice(64 * (c % 2), 64 * (c % 2) + 64)
                    for h in range(4):
                        k = 256 * (c // 2) + 64 * h
                        tok = mm(PS[rows, b, k:k + 64], KC[:, h, 64 * c:64 * c + 64], QC[:, h, 64 * c:64 * c + 64], True, True,
                                 *(fr + bar), inc=c * h == 9)
                ATf = AT.rearrange("p c h t -> p (c h) t")
                tA = DV(lambda e, b=b, n=n: e.copy_predicated(ATf, bc(con(f"gm{n}")[:, None, :], 8, 64).bitcast(u32),
                                                              PS[:, b, :].rearrange("p (k t) -> p k t", k=8)), tok)
                release(b, tA)
                for j in range(2):
                    b, fr = bank()
                    for h in range(4):
                        tok = tr(PS[:, b, 128 * h:128 * h + 128], KE[:, h, 128 * j:128 * j + 128], *(fr + bar), inc=h == 3)
                    tK = cp(AC, KDT[:, j, :], PS[:, b, :], tok)
                    release(b, tK)
                order = range(4) if n == 0 else range(3, -1, -1)
                tS = None
                for ci, c in enumerate(order):
                    rows = slice(64 * (c % 2), 64 * (c % 2) + 64)
                    j = c // 2
                    b, fr = bank()
                    for h in range(4):
                        for v in range(2):
                            out = PS[:, b, 128 * h + 64 * v:128 * h + 64 * v + 64]
                            mm(out, GV[rows, j, 256 * h + 128 * v:256 * h + 128 * v + 128], AT[rows, j, h, :], True, ci == 0, tA, *fr)
                            if ci:
                                mm(out, S[:, h, 128 * v:128 * v + 128], QB[:, h, 64 * c:64 * c + 64], False, True, tS)
                    bs, fs = bank(2)
                    for h in range(4):
                        tok = mm(PS[:, bs + h // 2, 256 * (h % 2):256 * (h % 2) + 256], KDT[rows, j, 128 * h:128 * h + 128],
                                 GV[rows, j, 256 * h:256 * h + 256], True, True, tK, *fs, inc=h == 3)
                    src = PS[:, b, :].rearrange("p (k t) -> p k t", k=8)
                    dst = OG[:, :, 64 * c:64 * c + 64]
                    t = cp(DV, dst, src, tok) if n == 0 else tt(DV, dst, dst, src, ADD, tok)
                    release(b, t)
                    for h in range(4):
                        st = PS[:, bs + h // 2, 256 * (h % 2):256 * (h % 2) + 256]
                        if ci == 0:
                            tS = cp(DV, S[:, h, :], st)
                        else:
                            tS = stt(DV, S[:, h, :], S[:, h, :], lst[:, h, c:c + 1], st, MUL, ADD)
                    release(bs, tS, n=2)
            t = act(TMP, OG, ACT.Square, *done())
            for h in range(4):
                b, tok = colsum("o256", TMP[:, 2 * h:2 * h + 2, :], 2, T, t)
                t1 = rsq(small, PS[:, b, 0:T], 1e-6, tok)
                release(b, t1)
                for v in range(2):
                    k = 2 * h + v
                    stt(DV, OG[:, k, :], OG[:, k, :], par("n_gla")[:, k:k + 1], small, MUL, MUL)
                    tt(DV, OG[:, k, :], OG[:, k, :], RGo[:, k, :], MUL)
            linear("o_o", 8, OG, T, lambda e, ps, tok: tt(DV, X2[:, e, :], X2[:, e, :], ps, ADD, tok), *done())

        phases.append(odd)
        phases.append(lambda: conv_ffn(1))

        for i, ph in enumerate(phases):
            if i < stop:
                ph()

        def load(dst, src, s):
            SP(lambda e: e.dma_start(dst, src).then_inc(s, 16), inc=False, chain=False)

        load(at(0, 8, T0), x_d, s_in[0])
        load(con_t[:, :], con_d, s_in[2])
        load(par_t[:, :], par_d, s_in[1])
        nb = 0 if state["tile"] == 0 else (flat[state["tile"] - 1][1] + 1)
        off = 0
        for bi in range(nb):
            w = blocks[bi][1]
            dst = ring[:, bi % RING, 0:w]
            src = ws_d[off:off + 128 * w].rearrange("(p w) -> p w", p=128)
            off += 128 * w
            waits = [state["freed"][bi - RING]] if bi >= RING else []
            SP(lambda e, dst=dst, src=src, s=s_w[bi % RING]: e.dma_start(dst, src).then_inc(s, 16), *waits, inc=False, chain=False)
            if bi == 3:
                load(res_t[:, :], res_d, s_in[3])
                load(pos_t[:, :], pos_d, s_in[4])
        src = X2 if stop > len(phases) else None
        if src is not None:
            SP(lambda e: e.dma_start(out_d, src).then_inc(s_out, 16), *everything(), inc=False, chain=False)
            SP(None, (s_out, 16), inc=False, chain=False)

        block = ctx.enter_context(nc.Block())

        @block.sync
        def _(e):
            SP.emit(e)

        @block.tensor
        def _(e):
            PE.emit(e)

        @block.vector
        def _(e):
            DV.emit(e)

        @block.scalar
        def _(e):
            AC.emit(e)

        @block.gpsimd
        def _(e):
            PO.emit(e)


def host_inputs(inp):
    inp = {k: np.asarray(v) for k, v in inp.items()}
    h = np.concatenate([inp["meta"], inp["x"][0]], axis=0)
    return {
        "x_d": np.ascontiguousarray(h.T.reshape(8, 128, T0).transpose(1, 0, 2)),
        "ws_d": pack_stream(inp),
        "par_d": pack(params(), inp),
        "con_d": pack(consts(), inp),
        "res_d": pack(resident(), inp),
        "pos_d": np.ascontiguousarray(inp["positions_2"].reshape(2, 128).T),
    }


def kernel(**inputs):
    import concourse.bacc as bacc
    from concourse.bass_utils import run_bass_kernel_spmd as run
    arrays = host_inputs(inputs)
    nc = bacc.Bacc("TRN2", target_bir_lowering=False, num_devices=1)
    aps = {n: nc.dram_tensor(n, a.shape, mybir.dt.from_np(a.dtype), kind="ExternalInput").ap() for n, a in arrays.items()}
    out = nc.dram_tensor("out_d", (128, 8, T1), mybir.dt.float32, kind="ExternalOutput").ap()
    build(nc, out_d=out, **aps)
    r = run(nc, [arrays], core_ids=[0])
    got = r.results[0]["out_d"]
    return np.ascontiguousarray(got.transpose(1, 0, 2).reshape(D, T1).T).reshape(1, T1, D)
```

```python
import numpy as np
import concourse.bass as bass
from concourse import mybir
from contextlib import ExitStack

D, T0, T1, C = 1024, 272, 256, 96
TP = 288
FF, FE, NE = 2816, 3584, 8
ALPHA = float(4.0 ** 0.25)
LAM_INIT = 0.8 - 0.6 * float(np.exp(0.0))
BW = 3072
RING = 3
SLOTS = 2


def tiles_of(name, get, nk, cols, wide=0):
    return [(name, get, nk, c0, cw, max(cw, wide)) for c0, cw in cols]


def cuts(n, w, c0=0):
    return [(c0 + i, min(w, n - i)) for i in range(0, n, w)]


E_T = [(640, 314), (954, 314), (1268, 314), (1582, 314), (1896, 312)]


def stream_tiles():
    def g(name, *idx):
        return lambda inp: inp[name][idx] if idx else inp[name]

    def two(name):
        return lambda inp: np.concatenate([inp[name][0, 0], inp[name][0, 1]], axis=1)

    t = []
    t += tiles_of("attn_qk", g("attn_w_in", 0), 8, cuts(2048, 128))
    t += tiles_of("attn_v", g("attn_w_in", 0), 8, [(2048, 384), (2432, 384), (2816, 256)])
    t += tiles_of("attn_o", g("attn_w_o", 0), 8, cuts(D, 128))
    for f in range(22):
        t += tiles_of("ffn_gu", g("ffn_w_gate", 0), 8, [(128 * f, 128)])
        t += tiles_of("ffn_gu", g("ffn_w_up", 0), 8, [(128 * f, 128)])
    t += tiles_of("ffn_d", g("ffn_w_down", 0), 22, cuts(D, 128))
    for i in range(3):
        t += tiles_of(f"rkv{i}", g("rw_w_rkv", 0, i), 8, cuts(D, 128))
    t += tiles_of("lw", two("rw_w1"), 8, [(0, 128)])
    t += tiles_of("la", two("rw_a1"), 8, [(0, 128)])
    t += tiles_of("lg", g("rw_g1", 0), 8, [(0, 128), (128, 32)], 128)
    t += tiles_of("rw_o", g("rw_w_o", 0), 8, cuts(D, 128))
    t += tiles_of("router", g("moe_w_router", 0), 8, [(0, 8)])
    for e in range(NE):
        for f in range(FE // 128):
            t += tiles_of("moe", g("moe_w_gate", 0, e), 8, [(128 * f, 128)])
            t += tiles_of("moe", g("moe_w_up", 0, e), 8, [(128 * f, 128)])
            t += tiles_of("moe", lambda inp, e=e, f=f: inp["moe_w_down"][0, e, 128 * f:128 * f + 128], 1, [(0, D)])
    w = g("w_in_even_2", 0)
    t += tiles_of("e_c", w, 8, cuts(640, 128))
    t += tiles_of("e_t", w, 8, E_T)
    t += tiles_of("e_g", w, 8, cuts(512, 128, 2208))
    t += tiles_of("uq", g("mla_w_uq_2", 0), 3, [(0, 384), (384, 384)])
    t += tiles_of("ukv", g("mla_w_ukv_2", 0), 2, [(0, 512), (512, 512)])
    t += tiles_of("e_o", g("w_out_even_2", 0), 8, cuts(D, 128))

    def conv(i):
        r = []
        for f in range(22):
            r += tiles_of(f"cu{i}", g("ffn_w_up_2", i), 8, [(128 * f, 128)])
            r += tiles_of(f"cu{i}", g("ffn_w_up_2", i), 8, [(FF + 128 * f, 128)])
        return r + tiles_of(f"cd{i}", g("ffn_w_down_2", i), 22, cuts(D, 128))

    t += conv(0)
    w = g("w_in_odd_2", 0)
    t += tiles_of("o_qk", w, 8, cuts(1024, 128))
    t += tiles_of("o_v", w, 8, [(1024, 384), (1408, 384), (1792, 256)])
    t += tiles_of("o_a", w, 8, [(3072, 16), (3088, 16)], 128)
    t += tiles_of("gg", lambda inp: np.concatenate([inp["gla_w_gate_fwd_2"][0], inp["gla_w_gate_bwd_2"][0]], axis=1),
                  1, [(0, 1024)])
    t += tiles_of("o_g", w, 8, cuts(1024, 128, 2048))
    t += tiles_of("o_o", g("w_out_odd_2", 0), 8, cuts(D, 128))
    t += conv(1)
    return t


ALONE = ("moe", "router")


def stream_blocks():
    blocks, width = [], BW + 1
    for t in stream_tiles():
        w = t[2] * t[5]
        if width + w > BW or (t[0] in ALONE and blocks[-1][-1][0][0] != t[0]) or blocks[-1][-1][0][0] in ("lg", "router"):
            blocks.append([])
            width = 0
        blocks[-1].append((t, width))
        width += w
    return [(b, b[-1][1] + b[-1][0][2] * b[-1][0][5]) for b in blocks]


def pack_stream(inp):
    parts = []
    blocks = stream_blocks()
    out = np.zeros(sum(128 * w for _, w in blocks), np.float32)
    off = 0
    for b, w in blocks:
        dst = out[off:off + 128 * w].reshape(128, w)
        for (name, get, nk, c0, cw, pw), x in b:
            src = get(inp)[:, c0:c0 + cw]
            if nk == 1:
                dst[:src.shape[0], x:x + cw] = src
            else:
                dst[:, x:x + nk * pw].reshape(128, nk, pw)[:, :, 0:cw] = src.reshape(nk, 128, cw).transpose(1, 0, 2)
        off += 128 * w
    return out


def params():
    def fm(get):
        return lambda inp: np.reshape(get(inp), (-1, 128)).T

    def rep(get):
        return lambda inp: np.broadcast_to(np.reshape(get(inp), (1, -1)), (128, np.size(get(inp))))

    p = []
    for i in range(2):
        for j in range(2):
            p.append((f"ln_g{i}{j}", 8, fm(lambda inp, i=i, j=j: inp["ln_g"][i, j])))
            p.append((f"ln_b{i}{j}", 8, fm(lambda inp, i=i, j=j: inp["ln_b"][i, j])))
    p.append(("subln", 1, fm(lambda inp: inp["attn_subln_g"][0])))
    for n in ("q1", "q2", "k1", "k2"):
        p.append((f"lam_{n}", 64, rep(lambda inp, n=n: inp[f"attn_lam_{n}"][0])))
    for s in range(2):
        for m in range(6):
            p.append((f"mu{s}{m}", 8, fm(lambda inp, s=s, m=m: inp["rw_mu"][0, s, m])))
        p.append((f"w0{s}", 8, fm(lambda inp, s=s: inp["rw_w0"][0, s])))
        p.append((f"a0{s}", 8, fm(lambda inp, s=s: inp["rw_a0"][0, s])))
    for n in ("k_k", "k_a", "r_k", "lnx_g", "lnx_b"):
        p.append((n, 8, fm(lambda inp, n=n: inp[f"rw_{n}"][0])))
    p.append(("b_router", 8, rep(lambda inp: inp["moe_b_router"][0])))
    p.append(("n_even", 8, fm(lambda inp: inp["mix_norm_even_2"][0])))
    p.append(("n_q", 3, fm(lambda inp: inp["mla_q_norm_2"][0])))
    p.append(("n_kv", 2, fm(lambda inp: inp["mla_kv_norm_2"][0])))
    p.append(("n_qh", 96, rep(lambda inp: inp["mla_q_head_norm_2"][0])))
    p.append(("n_kh", 96, rep(lambda inp: inp["mla_k_head_norm_2"][0])))
    p.append(("th_f", 8, rep(lambda inp: inp["ret_theta_fwd_2"][0])))
    p.append(("th_b", 8, rep(lambda inp: inp["ret_theta_bwd_2"][0])))
    p.append(("n_ret", 4, fm(lambda inp: inp["ret_out_norm_2"][0])))
    p.append(("n_odd", 8, fm(lambda inp: inp["mix_norm_odd_2"][0])))
    p.append(("b_gf", 4, fm(lambda inp: inp["gla_b_gate_fwd_2"][0])))
    p.append(("b_gb", 4, fm(lambda inp: inp["gla_b_gate_bwd_2"][0])))
    p.append(("n_gla", 8, fm(lambda inp: inp["gla_out_norm_2"][0])))
    for i in range(2):
        p.append((f"n_ffn{i}", 8, fm(lambda inp, i=i: inp["ffn_norm_2"][i])))
        for j in range(3):
            p.append((f"cw{i}{j}", 22, fm(lambda inp, i=i, j=j: inp["ffn_conv_w_2"][i, j])))
        p.append((f"cb{i}", 22, fm(lambda inp, i=i: inp["ffn_conv_b_2"][i])))
    return p


def columns(items):
    at, out = 0, {}
    for name, n, _ in items:
        out[name] = (at, n)
        at += n
    return out, at


def pack(items, inp):
    at, n = columns(items)
    out = np.zeros((128, n), np.float32)
    for name, w, get in items:
        v = get(inp)
        out[:v.shape[0], at[name][0]:at[name][0] + w] = v
    return out


def consts():
    f = np.float32
    p = np.arange(128)
    e8 = np.arange(8)

    def full(n):
        return lambda _: np.full((128, 128), 1.0 / n, f)

    blk = ((p[:, None] // 64) == (p[None, :] // 64)).astype(f)
    i64, j64 = np.arange(64)[None, :], (p % 64)[:, None]
    c = [("ident", 128, lambda _: np.eye(128, dtype=f)),
         ("o1024", 128, full(1024)), ("o128", 128, full(128)), ("o256", 128, full(256)), ("o384", 128, full(384)),
         ("blk", 128, lambda _: blk), ("blk64", 128, lambda _: blk / f(64)),
         ("gm0", 64, lambda _: (j64 <= i64).astype(f)), ("gm1", 64, lambda _: (j64 > i64).astype(f))]
    for h in (16, 32):
        inv = (f(10000.0) ** (-np.arange(h, dtype=f) / f(h))).astype(f)
        c.append((f"inv{h}", h, lambda _, inv=inv: np.broadcast_to(inv[None], (128, len(inv)))))
    c.append(("before", 64, lambda _: np.broadcast_to((e8[None, :] < e8[:, None]).astype(f).reshape(1, 64), (128, 64))))
    return c


def distances():
    q = np.arange(384).reshape(3, 128).T
    negd = -np.abs(q[:, :, None] - np.arange(T0)[None, None, :]).astype(np.float32)
    return [("negd", 3 * T0, lambda _: negd.reshape(128, -1))]


def relatives():
    j2 = np.arange(256).reshape(2, 128).T
    rel = (np.arange(256)[None, None, :] - j2[:, :, None]).astype(np.float32)
    return [("relp", 512, lambda _: np.maximum(rel, 0).reshape(128, -1)),
            ("reln", 512, lambda _: np.maximum(-rel, 0).reshape(128, -1))]


def scan_consts():
    f = np.float32
    s, t = np.arange(C)[:, None], np.arange(C)[None, :]
    c = [("up", C, lambda _: (s < t).astype(f)), ("upi", C, lambda _: (s <= t).astype(f)),
         ("dn", C, lambda _: (s > t).astype(f)), ("dni", C, lambda _: (s >= t).astype(f)),
         ("nup", C, lambda _: -(s < t).astype(f)), ("ndn", C, lambda _: -(s > t).astype(f))]
    for lv in range(7):
        m = ((s >> (lv + 1)) == (t >> (lv + 1))) & (((s >> lv) & 1) == 0) & (((t >> lv) & 1) == 1)
        c.append((f"lu{lv}", C, lambda _, m=m: m.astype(f)))
        c.append((f"ld{lv}", C, lambda _, m=m: m.T.astype(f)))
    at0 = np.ones(T0, f)
    at0[::C] = 0
    at1 = np.ones(T0, f)
    at1[[0, T0 - 2 * C, T0 - C]] = 0
    for n, a in (("begin0", at0), ("begin1", at1)):
        c.append((n, T0, lambda _, a=a: np.broadcast_to(a[None], (128, T0))))
    c.append(("w2", D, lambda inp: np.reshape(inp["rw_w2"][0], (128, D))))
    c.append(("a2", D, lambda inp: np.reshape(inp["rw_a2"][0], (128, D))))
    return c


def out_weights():
    return [("g2", D, lambda inp: inp["rw_g2"][0, 0:128]),
            ("g2b", D, lambda inp: inp["rw_g2"][0, 128:160]),
            ("a2", D, lambda inp: np.reshape(inp["rw_a2"][0], (128, D)))]


SETS = {"dis_d": distances, "scn_d": scan_consts, "rel_d": relatives, "ow_d": out_weights}


class Eng:

    def __init__(self, sem):
        self.sem, self.n, self.queue = sem, 0, []

    def __call__(self, fn, *waits, inc=True, chain=True):
        w = [x for x in waits if x is not None]
        if chain and self.n:
            w.append((self.sem, self.n))
        self.n += 1 if inc else 0
        self.queue.append((fn, w, inc))
        return (self.sem, self.n)

    def last(self):
        return (self.sem, self.n) if self.n else None

    def emit(self, eng):
        seen = {}
        for fn, waits, inc in self.queue:
            for sem, v in waits:
                if seen.get(id(sem), 0) < v:
                    eng.wait_ge(sem, v)
                    seen[id(sem)] = v
            if fn is None:
                continue
            ins = fn(eng)
            if inc:
                ins.then_inc(self.sem, 1)


def build(nc, x_d, ws_d, par_d, con_d, dis_d, scn_d, rel_d, ow_d, pos_d, out_d, stop=99):
    fp32, i32, u32, f32r = mybir.dt.float32, mybir.dt.int32, mybir.dt.uint32, mybir.dt.float32r
    ALU, ACT, AX = mybir.AluOpType, mybir.ActivationFunctionType, mybir.AxisListType
    MUL, ADD, SUB, MAXO = ALU.mult, ALU.add, ALU.subtract, ALU.max
    ctx = ExitStack()
    with ctx:
        def sb(name, shape, dt=fp32, c=ctx):
            return c.enter_context(nc.sbuf_tensor(name, shape, dt))

        def sem(name):
            return ctx.enter_context(nc.semaphore(name))

        pc, np_ = columns(params())
        cc, nc_ = columns(consts())
        ring = sb("ring", [128, RING, BW])
        par_t, con_t, pos_t = sb("par", [128, np_]), sb("con", [128, nc_]), sb("pos", [128, 8], i32)
        xt = sb("xt", [128, 8 * T0])
        AB = 8 * T0
        XW = AB + 112
        NL = 2 * SLOTS * BW + 4 * XW
        NA = (208 * 1024 - 512 - 4 * (RING * BW + np_ + nc_ + 8 + AB + NL)) // 4 // 16 * 16

        with ExitStack() as c:
            sh = [sb(f"sh{i}", [128, BW], f32r, c) for i in range(SLOTS)]
            sl = [sb(f"sl{i}", [128, BW], f32r, c) for i in range(SLOTS)]
            xh = [sb(f"xh{i}", [128, XW], f32r, c) for i in range(2)]
            xl = [sb(f"xl{i}", [128, XW], f32r, c) for i in range(2)]
        scan_t = sb("scan_t", [128, NL])
        hid, arena_of = {}, {}
        for key, n in (("ffn", 22 * T0), ("moe", 3 * T1), ("conv0", 22 * T1), ("conv1", 22 * T1)):
            with ExitStack() as c:
                hid[key] = [sb(f"{key}_{x}", [128, n], f32r, c) for x in "hl"]
                if key == "moe":
                    sh.append(sb("sh2", [128, BW], f32r, c))
                    sl.append(sb("sl2", [128, BW], f32r, c))
                arena_of[key] = sb(f"arena_{key}", [128, NA - 2 * n - 2 * BW * (key == "moe")], fp32, c)
        arena = sb("arena", [128, NA])
        ps_t = ctx.enter_context(nc.psum_tensor("ps", [128, 8, 512], fp32))
        PS = ps_t[:, :, :]

        def par(n):
            return par_t[:, pc[n][0]:pc[n][0] + pc[n][1]]

        def con(n):
            return con_t[:, cc[n][0]:cc[n][0] + cc[n][1]]

        def cut(t, off, *shape):
            n = int(np.prod(shape))
            assert off + n <= t.shape[1], (off, shape, t.shape)
            v = t[:, off:off + n]
            if len(shape) == 2:
                v = v.rearrange("p (a b) -> p a b", a=shape[0])
            if len(shape) == 3:
                v = v.rearrange("p (a b c) -> p a b c", a=shape[0], b=shape[1])
            return v

        def at(off, *shape):
            return cut(arena, off, *shape)

        def bc(v, *shape):
            return v.broadcast_to([v.shape[0], *shape])

        PE, DV, AC, PO, SP = (Eng(sem(n)) for n in ("s_pe", "s_dve", "s_act", "s_pool", "s_sp"))
        s_in = {n: sem(f"s_in_{n}") for n in ("x", "par", "con", "pos", "dis", "scn", "rel", "ow")}
        s_w = [sem(f"s_w{i}") for i in range(RING)]
        s_out = sem("s_out")
        IN_X, IN_PAR, IN_CON, IN_POS, IN_DIS, IN_SCN, IN_REL, IN_OW = (
            (s_in[n], 16) for n in ("x", "par", "con", "pos", "dis", "scn", "rel", "ow"))

        def done():
            return [t for t in (PE.last(), DV.last(), AC.last(), PO.last()) if t]

        def load(E, dst, src, s, *waits):
            E(lambda e: e.dma_start(dst, src).then_inc(s, 16), *waits, inc=False, chain=False)

        def tt(E, out, a, b, op, *w, chain=True):
            return E(lambda e: e.tensor_tensor(out, a, b, op), *w, chain=chain)

        def ts(E, out, a, s1, s2, o0, o1, *w, chain=True):
            return E(lambda e: e.tensor_scalar(out, a, s1, s2, o0, o1) if o1 is not None
                     else e.tensor_scalar(out, a, s1, None, o0), *w, chain=chain)

        def stt(E, out, a, s, b, o0, o1, *w, chain=True):
            return E(lambda e: e.scalar_tensor_tensor(out=out, in0=a, scalar=s, in1=b, op0=o0, op1=o1), *w, chain=chain)

        def act(out, a, f, *w, bias=0.0, scale=1.0, accum=None, chain=True):
            return AC(lambda e: e.activation(out, a, f, bias=bias, scale=scale, accum_out=accum), *w, chain=chain)

        def cp(E, out, a, *w, chain=True):
            if E is AC:
                return act(out, a, ACT.Copy, *w, chain=chain)
            return E(lambda e: e.tensor_copy(out, a), *w, chain=chain)

        def mset(E, out, v, *w):
            return E(lambda e: e.memset(out, v), *w)

        def red(out, a, op, *w):
            return DV(lambda e: e.tensor_reduce(out, a, AX.X, op), *w)

        def rec(out, a, *w):
            return DV(lambda e: e.reciprocal(out, a), *w)

        def rsq(out, a, eps, *w):
            t = ts(DV, out, a, eps, None, ADD, None, *w)
            t = act(out, out, ACT.Sqrt, t)
            return rec(out, out, t)

        def f32(v):
            return v.bitcast(fp32)

        blocks = stream_blocks()
        flat = [(t, bi, x) for bi, (b, _) in enumerate(blocks) for t, x in b]
        state = {"tile": 0, "freed": {}, "split": {}, "read": {}, "next": 0, "ahead": True, "gate": []}
        slot_of, held = {}, [None] * 3

        def split_block(bi, slots=(0, 1)):
            w = blocks[bi][1]
            s = min(slots, key=lambda i: -1 if held[i] is None else held[i])
            fr = [] if held[s] is None else [state["read"][held[s]]]
            held[s], slot_of[bi] = bi, s
            src = ring[:, bi % RING, 0:w]
            t = cp(AC, sh[s][:, 0:w], src, (s_w[bi % RING], 16 * (bi // RING + 1)), *fr, *state["gate"])
            t = tt(DV, sl[s][:, 0:w], src, f32(sh[s][:, 0:w]), SUB, t, *fr, *state["gate"])
            state["split"][bi] = state["freed"][bi] = t
            state["next"] = bi + 1

        def weight(name, raw=False):
            t, bi, x = flat[state["tile"]]
            assert t[0] == name, (t[0], name)
            state["tile"] += 1
            n = state["tile"]
            w = t[2] * t[5]
            closes = n == len(flat) or flat[n][1] != bi
            if raw:
                state["next"] = bi + 1
                v = ring[:, bi % RING, x:x + w].rearrange("p (k c) -> p k c", k=t[2])
                return v, None, (s_w[bi % RING], 16 * (bi // RING + 1)), bi, t
            slots = (0, 1, 2) if name == "moe" else (0, 1)
            while state["next"] <= bi:
                split_block(state["next"], slots)
            b2 = bi + 1
            if state["ahead"] and state["next"] == b2 and b2 < len(blocks):
                n2 = blocks[b2][0][0][0][0]
                if n2 == name == "moe" or "moe" not in (n2, name) and n2 != "router":
                    split_block(b2, slots)
            h, l = (v[slot_of[bi]][:, x:x + w].rearrange("p (k c) -> p k c", k=t[2]) for v in (sh, sl))
            return h, l, state["split"][bi], (bi if closes else None), t

        def used(bi, tok):
            if bi is not None:
                state["read"][bi] = tok

        xfree = [[], []]

        def xset(s, n, T):
            h, l = (v[s][:, 0:n * T].rearrange("p (n t) -> p n t", n=n) for v in (xh, xl))
            return {"h": h, "l": l, "tok": {}, "s": s}

        def split_x(x, src, k0, k1, *waits):
            w = list(waits) + xfree[x["s"]]
            t = cp(AC, x["h"][:, k0:k1, :], src, *w)
            t = tt(DV, x["l"][:, k0:k1, :], src, f32(x["h"][:, k0:k1, :]), SUB, t, *w)
            for k in range(k0, k1):
                x["tok"][k] = t
            return t

        def split_all(s, src, n, T, *waits):
            x = xset(s, n, T)
            for k in range(0, n, 2):
                split_x(x, src[:, k:min(k + 2, n), :], k, min(k + 2, n), *waits)
            return x

        free = [[] for _ in range(8)]
        turn = [0]

        def bank(n=1):
            b = turn[0]
            if b % n or b + n > 8:
                b = -(-b // n) * n % 8
            turn[0] = (b + n) % 8
            return b, [t for i in range(n) for t in free[b + i]]

        def release(b, *toks, n=1):
            for i in range(n):
                free[b + i] = list(toks)

        def mm(out, lhsT, rhs, start, stop, *waits, inc=False):
            return PE(lambda e: e.matmul(out, lhsT, rhs, start=start, stop=stop), *waits, inc=inc, chain=False)

        def mm3(out, ah, al, bh, bl, start, stop, *waits, inc=False):
            mm(out, ah, bh, start, False, *waits)
            mm(out, ah, bl, False, False)
            return mm(out, al, bh, False, stop, inc=inc)

        def tr(out, in_, *waits, inc=False):
            k = in_.shape[0]
            return PE(lambda e: e.transpose(out, in_, con("ident")[0:k, 0:k]), *waits, IN_CON, inc=inc, chain=False)

        def linear(name, n, x, T, evac, *waits, rows=128):
            toks = []
            for e in range(n):
                wh, wl, wt, closes, t = weight(name)
                nk = t[2]
                b, fr = bank()
                for k in range(nk):
                    w = [x["tok"][k]] if e == 0 else []
                    tok = mm3(PS[:, b, 0:T], wh[0:rows, k, :], wl[0:rows, k, :], x["h"][0:rows, k, :], x["l"][0:rows, k, :],
                              k == 0, k == nk - 1, *(w + (fr + [wt] + list(waits) if k == 0 else [])), inc=k == nk - 1)
                used(closes, tok)
                tk = evac(e, PS[0:t[4], b, 0:T], tok)
                release(b, tk)
                toks.append(tk)
            if x["s"] is not None:
                xfree[x["s"]] = [tok]
            return toks

        def linear_t(name, n, x, spans, evac, *waits):
            out_t = []
            T = x["h"].shape[2]
            hf, lf = (v[x["s"]] for v in (xh, xl))
            for i in range(n):
                wh, wl, wt, closes, t = weight(name)
                nk, cw = t[2], t[4]
                for j, (t0, tn) in enumerate(spans):
                    b, fr = bank()
                    for k in range(nk):
                        c = slice(x.get("at", 0) + k * T + t0, x.get("at", 0) + k * T + t0 + 128)
                        w = [x["tok"][k]] if i + j == 0 else []
                        tok = mm3(PS[:, b, 0:cw], hf[:, c], lf[:, c], wh[:, k, :], wl[:, k, :], k == 0, k == nk - 1,
                                  *(w + (fr + [wt] + list(waits) if k == 0 else [])), inc=k == nk - 1)
                    tk = evac(i, j, PS[0:tn, b, 0:cw], tok)
                    release(b, tk)
                    out_t.append(tk)
                used(closes, tok)
            xfree[x["s"]] = [tok]
            return out_t

        def colsum(mat, src, n, T, *waits):
            b, fr = bank()
            for k in range(n):
                tok = mm(PS[:, b, 0:T], con(mat), src[:, k, :], k == 0, k == n - 1,
                         *(fr + [IN_CON] + list(waits) if k == 0 else []), inc=k == n - 1)
            return b, tok

        def layer_norm(src, dst, tmp, small, T, g, bb, s, *waits):
            b, tok = colsum("o1024", src, 8, T, *waits)
            bv, fr = bank()
            for k in range(8):
                t = tt(DV, src[:, k, :], src[:, k, :], PS[:, b, 0:T], SUB, tok)
                t1 = act(tmp[:, k, :], src[:, k, :], ACT.Square, t, *waits)
                tv = mm(PS[:, bv, 0:T], con("o1024"), tmp[:, k, :], k == 0, k == 7, t1, *fr, inc=k == 7)
            release(b, t)
            t = rsq(small, PS[:, bv, 0:T], 1e-5, tv)
            release(bv, t)
            x = xset(s, 8, T) if s is not None else None
            for k in range(8):
                t = stt(DV, src[:, k, :], src[:, k, :], par(g)[:, k:k + 1], small, MUL, MUL, IN_PAR)
                o = act(dst[:, k, :], src[:, k, :], ACT.Identity, t, *waits, bias=par(bb)[:, k:k + 1])
                if x and k % 2:
                    split_x(x, dst[:, k - 1:k + 1, :], k - 1, k + 1)
            return x if x else o

        def rms_norm(src, dst, tmp, small, n, T, g, mat, s, *waits, k0=0, x=None):
            bv, fr = bank()
            for k in range(n):
                t1 = act(tmp[:, k, :], src[:, k, :], ACT.Square, *waits)
                tv = mm(PS[:, bv, 0:T], con(mat), tmp[:, k, :], k == 0, k == n - 1, t1, IN_CON, *fr, inc=k == n - 1)
            t = rsq(small, PS[:, bv, 0:T], 1e-6, tv)
            release(bv, t)
            x = x or xset(s, n, T)
            for k in range(n):
                t = stt(DV, dst[:, k, :], src[:, k, :], par(g)[:, k:k + 1], small, MUL, MUL, IN_PAR, *waits)
                if k % 2 or k == n - 1:
                    a = k - k % 2
                    split_x(x, dst[:, a:k + 1, :], k0 + a, k0 + k + 1, t)
            return x

        phases = []
        X = cut(xt, 0, 8, T0)
        QT = [(0, 128), (128, 128), (256, 16)]
        THIRDS = [0, 384, 768]
        carry = {}

        def attention():
            Q, K, O = (at(i * AB, 8, T0) for i in range(3))
            VT = at(3 * AB, 3, 1024)
            o = 3 * AB + 3072
            negd = at(o, 3, T0)
            o += 3 * T0
            load(PO, negd.rearrange("p a t -> p (a t)"), dis_d, s_in["dis"])
            for s in range(2):
                for v in (xh, xl):
                    padded = mset(DV, f32(v[s][:, AB:XW]), 0.0)
            x = split_all(0, X, 8, T0, IN_X)
            linear("attn_qk", 16, x, T0, lambda e, ps, tok: cp(AC if e % 2 else DV, (Q if e < 8 else K)[:, e % 8, :], ps, tok))
            linear_t("attn_v", 3, x, QT, lambda i, j, ps, tok: cp(
                AC if j else DV, VT[0:ps.shape[0], j, THIRDS[i]:THIRDS[i] + ps.shape[1]], ps, tok), padded)
            lam = at(o, 8)
            pr = at(o + 8, 64)
            o += 72
            for i in (1, 2):
                tt(DV, pr, par(f"lam_q{i}"), par(f"lam_k{i}"), MUL, IN_PAR)
                red(lam[:, i - 1:i], pr, ADD)
            t = act(lam[:, 2:4], lam[:, 0:2], ACT.Exp, DV.last())
            tt(DV, lam[:, 4:5], lam[:, 3:4], lam[:, 2:3], SUB, t)
            ts(DV, lam[:, 5:6], lam[:, 4:5], -LAM_INIT, None, ADD, None)
            nlam = lam[:, 5:6]
            NB = 2
            st = [at(o + i * 2 * T0, 2, T0) for i in range(NB)]
            o += NB * 2 * T0
            ex = [at(o + i * 2 * T0, 2, T0) for i in range(NB)]
            o += NB * 2 * T0
            sm = [at(o + i * 16, 16) for i in range(NB)]
            o += NB * 16
            aT = [at(o + i * 3 * T0, 3, T0) for i in range(2)]
            o += 6 * T0
            small = at(o, T0)
            barrier = done()
            scale = 64.0 ** -0.5
            ready, freeS, freeT = {}, [[], []], [[], []]

            def scores(u):
                h, qi = u // 3, u % 3
                q0, qn = QT[qi]
                i = u % NB
                b, fr = bank(2)
                for c in range(2):
                    tok = mm(PS[0:qn, b + c, 0:T0], Q[64 * c:64 * c + 64, h, q0:q0 + qn], K[64 * c:64 * c + 64, h, :],
                             True, True, *(fr + barrier), inc=c == 1)
                slope = 2.0 ** -(h + 1)
                S, E, m = st[i][0:qn], ex[i][0:qn], sm[i][0:qn]
                t = stt(DV, S, bc(negd[0:qn, None, qi, :], 2, T0), slope / scale, PS[0:qn, b:b + 2, 0:T0],
                        MUL, ADD, tok, IN_DIS, *freeS[i])
                release(b, t, n=2)
                red(m[:, 0:2], S, MAXO)
                t = ts(DV, m[:, 2:4], m[:, 0:2], -scale, None, MUL, None)
                for c in range(2):
                    t = act(E[:, c, :], S[:, c, :], ACT.Exp, t, bias=m[:, 2 + c:3 + c], scale=scale, accum=m[:, 4 + c:5 + c])
                rec(m[:, 6:8], m[:, 4:6], t)
                tt(DV, m[:, 8:9], m[:, 7:8], nlam[0:qn], MUL)
                ts(DV, S[:, 0, :], E[:, 0, :], m[:, 6:7], None, MUL, None)
                ready[u] = stt(DV, S[:, 1, :], E[:, 1, :], m[:, 8:9], S[:, 0, :], MUL, ADD)

            def rest(u):
                h, qi = u // 3, u % 3
                q0, qn = QT[qi]
                i = u % NB
                b, fr = bank()
                pt = PS[:, b, 0:384].rearrange("p (k q) -> p k q", k=3)
                for kt, (k0, kn) in enumerate(QT):
                    tok = tr(pt[0:kn, kt, 0:qn], st[i][0:qn, 1, k0:k0 + kn], ready[u], *fr, inc=kt == 2)
                freeS[i] = [tok]
                w = freeT[h % 2] if qi == 0 else []
                cp(AC, aT[h % 2][:, 0:2, q0:q0 + qn], pt[:, 0:2, 0:qn], tok, *w)
                t = cp(AC, aT[h % 2][0:16, 2, q0:q0 + qn], pt[0:16, 2, 0:qn])
                release(b, t)
                if qi == 2:
                    b, fr = bank()
                    for kt, (k0, kn) in enumerate(QT):
                        tok = mm(PS[:, b, 0:T0], VT[0:kn, kt, 128 * h:128 * h + 128], aT[h % 2][0:kn, kt, :], kt == 0, kt == 2,
                                 t, *fr, inc=kt == 2)
                    freeT[h % 2] = [tok]
                    release(b, cp(AC, O[:, h, :], PS[:, b, 0:T0], tok))

            for u in range(25):
                if u < 24:
                    scores(u)
                if u:
                    rest(u - 1)
            ts(DV, lam[:, 6:7], par("subln"), 1.0 - LAM_INIT, None, MUL, None)
            x = xset(1, 8, T0)
            bar = done()
            for h in range(8):
                t = act(Q[:, h, :], O[:, h, :], ACT.Square, *bar)
                b, tok = colsum("o128", Q[:, h:h + 1, :], 1, T0, t)
                t = rsq(small, PS[:, b, 0:T0], 1e-5, tok)
                release(b, t)
                t = stt(DV, O[:, h, :], O[:, h, :], lam[:, 6:7], small, MUL, MUL)
                split_x(x, O[:, h:h + 1, :], h, h + 1, t)
            linear("attn_o", 8, x, T0, lambda e, ps, tok: stt(DV, K[:, e, :], X[:, e, :], ALPHA, ps, MUL, ADD, tok))
            carry["x"] = layer_norm(K, X, O, small, T0, "ln_g00", "ln_b00", 0, *done())

        phases.append(attention)

        def hidden(key, T):
            h, l = (v[:, :].rearrange("p (n t) -> p n t", t=T) for v in hid[key])
            return {"h": h, "l": l, "tok": {}, "s": None}

        def split_hidden(x, f, src, tok, *waits):
            t = cp(AC, x["h"][:, f, :], src, tok, *waits)
            t = tt(PO, x["l"][:, f, :], src, f32(x["h"][:, f, :]), SUB, t, *waits)
            x["tok"][f] = t
            return t

        def ffn():
            ar = arena_of["ffn"]
            R, tmp = cut(ar, 0, 8, T0), cut(ar, AB, 8, T0)
            small = cut(ar, 2 * AB, T0)
            o = 2 * AB + T0
            sg = [cut(ar, o + 2 * T0 * i, 2, T0) for i in range(2)]
            H = hidden("ffn", T0)
            bar = done()
            hold = {}

            def evac(e, ps, tok):
                f = e // 2
                s = sg[f % 2]
                if e % 2 == 0:
                    t = act(s[:, 0, :], ps, ACT.Sigmoid, tok, hold.get(f - 2), *bar)
                    return tt(DV, s[:, 1, :], ps, s[:, 0, :], MUL, t, hold.get(f - 2))
                t = tt(DV, s[:, 1, :], s[:, 1, :], ps, MUL, tok)
                hold[f] = split_hidden(H, f, s[:, 1, :], t, *bar)
                return t

            linear("ffn_gu", 44, carry["x"], T0, evac)
            linear("ffn_d", 8, H, T0, lambda e, ps, tok: stt(DV, R[:, e, :], X[:, e, :], ALPHA, ps, MUL, ADD, tok, *bar))
            layer_norm(R, X, tmp, small, T0, "ln_g01", "ln_b01", None, *done())

        phases.append(ffn)

        Rr, Kr, KK, Yb = (at(i * AB, 8, T0) for i in range(4))
        VW = 1024 + 32
        VC = at(4 * AB, 3, VW)
        hid_o = 4 * AB + 3 * VW
        HW, HA, HG, HG2 = (at(hid_o + i * T0, T0) for i in range(4))
        tail_o = hid_o + 4 * T0
        CH = [(0, C), (C, C), (2 * C, T0 - 2 * C)]

        def rwkv_project():
            Vr, DP = KK, Yb
            DN = at(tail_o, 8, T0)
            XS = at(tail_o + AB, 2, T0)
            bar = done()
            ts(DV, DP[:, :, 0:1], X[:, :, 0:1], -1.0, None, MUL, None, *bar)
            tt(DV, DP[:, :, 1:T0], X[:, :, 0:T0 - 1], X[:, :, 1:T0], SUB)
            ts(DV, DN[:, :, T0 - 1:T0], X[:, :, T0 - 1:T0], -1.0, None, MUL, None)
            tt(DV, DN[:, :, 0:T0 - 1], X[:, :, 1:T0], X[:, :, 0:T0 - 1], SUB)

            def mix(m):
                x = xset(m % 2, 8, T0)
                for k in range(8):
                    v = XS[:, k % 2, :]
                    stt(DV, v, DP[:, k, :], par(f"mu0{m}")[:, k:k + 1], X[:, k, :], MUL, ADD, *bar, AC.last())
                    t = stt(DV, v, DN[:, k, :], par(f"mu1{m}")[:, k:k + 1], v, MUL, ADD)
                    split_x(x, v[:, None, :], k, k + 1, t)
                return x

            xs = [mix(0), mix(1)]
            for m, dst in enumerate((Rr, Kr, Vr)):
                linear(f"rkv{m}", 8, xs[m], T0, lambda e, ps, tok: cp(AC, dst[:, e, :], ps, tok, *bar))
                xs.append(mix(m + 2))
            linear("lw", 1, xs[3], T0, lambda e, ps, tok: act(HW, ps, ACT.Tanh, tok, *bar))
            xs.append(mix(5))
            linear("la", 1, xs[4], T0, lambda e, ps, tok: cp(AC, HA, ps, tok))
            state["ahead"] = False
            linear("lg", 2, xs[5], T0, lambda e, ps, tok: act((HG, HG2[0:32])[e], ps, ACT.Sigmoid, tok))
            bar = done()
            mset(DV, VC[:, :, 1024:VW], 0.0, *bar)
            tz = mset(DV, VC[64:C, 2, 0:1024], 0.0)
            for c, (c0, cn) in enumerate(CH):
                for hf in range(2):
                    b, fr = bank()
                    for d in range(4):
                        tok = tr(PS[0:cn, b, 128 * d:128 * d + 128], Vr[:, 4 * hf + d, c0:c0 + cn], *(fr + bar), inc=d == 3)
                    release(b, cp(AC, VC[0:cn, c, 512 * hf:512 * hf + 512], PS[0:cn, b, :], tok, tz))
            bar = done()
            sq, nrm = at(tail_o, T0), at(tail_o + T0, T0)
            for k in range(8):
                t = ts(DV, KK[:, k, :], Kr[:, k, :], par("k_k")[:, k:k + 1], None, MUL, None, *bar)
                t = act(sq, KK[:, k, :], ACT.Square, t, PE.last())
                b, tok = colsum("blk", sq[:, None, :], 1, T0, t)
                t = act(nrm, PS[:, b, 0:T0], ACT.Sqrt, tok, DV.last())
                release(b, t)
                ts(DV, nrm, nrm, 1e-12, None, MAXO, None, t)
                rec(nrm, nrm)
                tt(DV, KK[:, k, :], KK[:, k, :], nrm, MUL)

        phases.append(rwkv_project)

        def rwkv_scan():
            sc, ns = columns(scan_consts())
            so = tail_o
            scn = at(so, ns)
            so += ns

            def sn(name):
                return scn[:, sc[name][0]:sc[name][0] + sc[name][1]]

            bar = done()
            load(PO, scn, scn_d, s_in["scn"], *bar)
            W = 8 * C
            per = []
            zo = 0
            for n in range(2):
                d = {}
                d["AR"] = cut(scan_t, zo, 2, 4, TP)
                d["B"], d["K"] = cut(scan_t, zo + 8 * TP, 4, TP), cut(scan_t, zo + 12 * TP, 4, TP)
                zo += 16 * TP
                for i, name in enumerate(("U", "X", "Y", "T", "GKA", "GKR", "GBR")):
                    d[name] = cut(scan_t, zo + i * W, 8, C)
                d["t1"], d["t2"] = cut(scan_t, zo, 4, T0), cut(scan_t, zo + 4 * T0, 4, T0)
                d["NS"], d["Z"] = cut(scan_t, zo, 544), cut(scan_t, zo + 3 * W, 544)
                d["Kt"] = cut(scan_t, zo + 2 * W, 4, 128)
                zo += 7 * W
                d["Bt"] = cut(scan_t, zo, 4, 128)
                zo += 512
                d["S"] = at(so, 288)
                so += 288
                d["PC"] = at(so, 4, 3)
                so += 12
                per.append(d)
            mset(DV, Yb, 0.0, *bar)
            for d in per:
                mset(DV, d["AR"].rearrange("p a b t -> p (a b) t")[:, :, T0:TP], 0.0)
                mset(DV, d["B"][:, :, T0:TP], 0.0)
                mset(DV, d["K"][:, :, T0:TP], 0.0)

            def prepare(n, hf):
                E = DV if n == 0 else PO
                d = per[n]
                t1, t2, B, K = d["t1"], d["t2"], d["B"][:, :, 0:T0], d["K"][:, :, 0:T0]
                A, R = d["AR"][:, 0, :, 0:T0], d["AR"][:, 1, :, 0:T0]
                d0 = 4 * hf
                bar = done()
                for i in range(4):
                    for w, src, dst, bias in (("w2", HW, t1, f"w0{n}"), ("a2", HA, t2, f"a0{n}")):
                        b, fr = bank()
                        tok = mm(PS[:, b, 0:T0], sn(w)[64 * n:64 * n + 64, 128 * (d0 + i):128 * (d0 + i) + 128],
                                 src[64 * n:64 * n + 64, :], True, True, *(fr + bar + [IN_SCN]), inc=True)
                        t = act(dst[:, i, :], PS[:, b, 0:T0], ACT.Sigmoid, tok, *bar, bias=par(bias)[:, d0 + i:d0 + i + 1])
                        release(b, t)
                kk, r, k = (v[:, d0:d0 + 4, :] for v in (KK, Rr, Kr))
                tb = tt(E, B, kk, t2, MUL, t, *bar)
                for i in range(4):
                    ts(E, t2[:, i, :], t2[:, i, :], -1.0, par("k_a")[:, d0 + i:d0 + i + 1], ADD, MUL)
                ts(E, t2, t2, 1.0, None, ADD, None)
                tk = tt(E, K, t2, k, MUL)
                tl = ts(E, t1, t1, -float(np.exp(-0.5)), None, MUL, None)
                for i in range(4):
                    cum, ld = A[:, i, :], t1[:, i, :]
                    if n == 1:
                        cum, ld = cum[:, ::-1], ld[:, ::-1]
                    t = DV(lambda e, cum=cum, ld=ld: e.tensor_tensor_scan(cum, sn(f"begin{n}"), ld, 0.0, MUL, ADD), tl, *bar)
                t3 = act(t2, A, ACT.Exp, t, tk)
                tt(E, R, r, t2, MUL, t3)
                for c, (c0, cn) in enumerate(CH):
                    last = c0 + cn - 1 if n == 0 else c0
                    t = cp(E, d["PC"][:, :, c:c + 1], t2[:, :, last:last + 1])
                t3 = act(t2, A, ACT.Exp, t, scale=-1.0)
                tt(E, B, B, t2, MUL, t3)
                tt(E, K, K, t2, MUL)
                t = tt(E, t1, A, t1, SUB)
                t3 = act(t1, t1, ACT.Exp, t)
                tt(E, A, kk, t1, MUL, t3)
                mset(E, d["S"], 0.0)

            def pairs(b, cols=C):
                return PS[0:C, b:b + 2, 0:4 * cols].rearrange("s p (i t) -> s p i t", i=4)

            def by4(v):
                return v.rearrange("s (p i) t -> s p i t", p=2)

            def chunks(n, hf):
                d = per[n]
                AR, B, K, U, X_, Y, T_, S, PC = (d[k] for k in ("AR", "B", "K", "U", "X", "Y", "T", "S", "PC"))
                strict, nstrict, incl = ("up", "nup", "upi") if n == 0 else ("dn", "ndn", "dni")
                lx = "lu" if n == 0 else "ld"
                begin = done()
                for ci, c in enumerate(range(3) if n == 0 else range(2, -1, -1)):
                    final = ci == 2
                    cn = CH[c][1]
                    cs = slice(C * c, C * c + C)
                    prev = [PE.last(), DV.last(), AC.last()] if ci else begin
                    for lh, m0, n0, m1, n1 in ((B, nstrict, "U", incl, "GBR"), (K, strict, "GKA", incl, "GKR")):
                        for m, name, rh in ((m0, n0, 0), (m1, n1, 1)):
                            b, fr = bank(2)
                            for p in range(2):
                                rows = slice(64 * p, 64 * p + 64)
                                for i in range(4):
                                    tok = mm(PS[0:C, b + p, C * i:C * i + C], lh[rows, i, cs], AR[rows, rh, i, cs], True, True,
                                             *(fr + prev if p + i == 0 else []), inc=p * i == 3)
                            tg = tt(DV, by4(d[name][0:C]), pairs(b), sn(m)[0:C, None, None, :].broadcast_to([C, 2, 4, C]), MUL, tok, IN_SCN, *prev)
                            release(b, tg, n=2)
                        yield
                    idb = con("ident")[0:C, None, 0:C].broadcast_to([C, 8, C])
                    cp(DV, X_[0:C], idb)
                    for lv in range(7):
                        msk = sn(f"{lx}{lv}")[0:C].bitcast(u32)
                        if lv == 0:
                            t = DV(lambda e, msk=msk: e.copy_predicated(X_[0:C], msk[:, None, :].broadcast_to([C, 8, C]), U[0:C]))
                        else:
                            b, fr = bank(2)
                            for h in range(8):
                                tok = mm(PS[0:C, b + h // 4, C * (h % 4):C * (h % 4) + C], U[0:C, h, :], Y[0:C, h, :], True, True,
                                         *(fr + [ty] if h == 0 else []), inc=h == 7)
                            tT = cp(AC, by4(T_[0:C]), pairs(b), tok)
                            release(b, tT, n=2)
                            yield
                            b, fr = bank(2)
                            for h in range(8):
                                tok = mm(PS[0:C, b + h // 4, C * (h % 4):C * (h % 4) + C], T_[0:C, h, :], X_[0:C, h, :], True, True,
                                         *(fr + [tT] if h == 0 else []), inc=h == 7)
                            t = DV(lambda e, b=b, msk=msk: e.copy_predicated(
                                by4(X_[0:C]), msk[:, None, None, :].broadcast_to([C, 2, 4, C]), pairs(b)), tok)
                            release(b, t, n=2)
                            yield
                        if lv < 6:
                            b, fr = bank(2)
                            for h in range(8):
                                tok = tr(PS[0:C, b + h // 4, C * (h % 4):C * (h % 4) + C], X_[0:C, h, :], *(fr + [t] if h == 0 else []), inc=h == 7)
                            ty = cp(AC, by4(Y[0:C]), pairs(b), tok)
                            release(b, ty, n=2)
                            yield
                    tX = t
                    if not final:
                        for src, dst in ((K, d["Kt"]), (B, d["Bt"])):
                            b, fr = bank()
                            for i in range(4):
                                tok = tr(PS[0:C, b, 128 * i:128 * i + 128], src[:, i, cs], *fr, inc=i == 3)
                            tkb = cp(AC, dst[0:C], PS[0:C, b, :].rearrange("s (i k) -> s i k", i=4), tok)
                            release(b, tkb)
                    tS = DV.last()
                    b, fr = bank(2)
                    for p in range(2):
                        rows = slice(64 * p, 64 * p + 64)
                        for i in range(4):
                            hh = 2 * (4 * hf + i) + p
                            out = PS[0:C, b + p, C * i:C * i + C]
                            if ci:
                                mm(out, AR[rows, 0, i, cs], S[rows, 64 * i:64 * i + C], True, False, tS, *fr)
                            tok = mm(out, d["GKA"][0:C, 4 * p + i, :], VC[0:C, c, 64 * hh:64 * hh + C], not ci, True, tS, *fr, inc=p * i == 3)
                    tz = mset(PO, d["Z"][0:C, 512:544], 0.0, tX)
                    tn = mset(PO, d["NS"][0:C, 512:544], 0.0, tX)
                    t = cp(AC, d["Z"][0:C, 0:512].rearrange("s (p i v) -> s p i v", p=2, i=4), pairs(b)[:, :, :, 0:64], tok, tX)
                    release(b, t, n=2)
                    yield
                    b, fr = bank(2)
                    for h in range(8):
                        tok = mm(PS[0:C, b + h // 4, C * (h % 4):C * (h % 4) + C], X_[0:C, h, :], d["Z"][0:C, 64 * h:64 * h + C], True, True,
                                 *(fr + [t, tz] if h == 0 else []), inc=h == 7)
                    tN = act(d["NS"][0:C, 0:512].rearrange("s (p i v) -> s p i v", p=2, i=4), pairs(b)[:, :, :, 0:64], ACT.Copy, tok, scale=-1.0)
                    release(b, tN, n=2)
                    yield
                    b, fr = bank(2)
                    for p in range(2):
                        rows = slice(64 * p, 64 * p + 64)
                        for i in range(4):
                            h, hh = 4 * p + i, 2 * (4 * hf + i) + p
                            out = PS[rows, b + p, C * i:C * i + C]
                            if ci:
                                mm(out, S[rows, 64 * i:64 * i + 64], AR[rows, 1, i, cs], True, False, tN, *fr)
                            mm(out, VC[0:C, c, 64 * hh:64 * hh + 64], d["GKR"][0:C, h, :], not ci, False, tN, *fr)
                            tok = mm(out, d["NS"][0:C, 64 * h:64 * h + 64], d["GBR"][0:C, h, :], False, True, inc=p * i == 3)
                    for p in range(2):
                        rows = slice(64 * p, 64 * p + 64)
                        y = Yb[rows, 4 * hf:4 * hf + 4, C * c:C * c + cn]
                        tY = tt(DV, y, y, PS[rows, b + p, 0:4 * C].rearrange("v (i t) -> v i t", i=4)[:, :, 0:cn], ADD, tok)
                    release(b, tY, n=2)
                    yield
                    if final:
                        continue
                    b, fr = bank()
                    for p in range(2):
                        rows = slice(64 * p, 64 * p + 64)
                        for i in range(4):
                            h, hh = 4 * p + i, 2 * (4 * hf + i) + p
                            out = PS[rows, b, C * i:C * i + C]
                            mm(out, d["Kt"][0:C, i, 64 * p:64 * p + 64], VC[0:C, c, 64 * hh:64 * hh + C], True, False, tkb, tn, *fr)
                            tok = mm(out, d["Bt"][0:C, i, 64 * p:64 * p + 64], d["NS"][0:C, 64 * h:64 * h + C], False, True, inc=p * i == 3)
                    S4 = S[:, 0:256].rearrange("k (i v) -> k i v", i=4)
                    t = tt(DV, S4, S4, PS[:, b, 0:4 * C].rearrange("k (i v) -> k i v", i=4)[:, :, 0:64], ADD, tok)
                    release(b, t)
                    tt(DV, S4, S4, bc(PC[:, :, c:c + 1], 4, 64), MUL)
                    yield

            for hf in range(2):
                for n in range(2):
                    prepare(n, hf)
                runs = [chunks(n, hf) for n in range(2)]
                while runs:
                    runs = [g for g in runs if next(g, "end") != "end"]

        phases.append(rwkv_scan)

        def rwkv_out():
            oc, nw = columns(out_weights())
            o = tail_o
            ow = at(o, nw)
            o += nw
            bar = done()
            load(PO, ow, ow_d, s_in["ow"], *bar)
            tmp = [at(o + i * T0, T0) for i in range(4)]

            def w(name, k):
                return ow[:, oc[name][0] + 128 * k:oc[name][0] + 128 * k + 128]

            state["ahead"], state["gate"] = True, bar
            x = xset(0, 8, T0)
            sm, va, vb, vv = tmp
            for k in range(8):
                y = Yb[:, k, :]
                b, tok = colsum("blk64", Yb[:, k:k + 1, :], 1, T0, *bar)
                t = tt(DV, y, y, PS[:, b, 0:T0], SUB, tok, *bar)
                release(b, t)
                t = act(sm, y, ACT.Square, t)
                b, tok = colsum("blk64", sm[:, None, :], 1, T0, t)
                t = rsq(sm, PS[:, b, 0:T0], 64e-5, tok)
                release(b, t)
                tt(DV, y, y, sm, MUL)
                ts(DV, y, y, par("lnx_g")[:, k:k + 1], par("lnx_b")[:, k:k + 1], MUL, ADD)
                for n, v in ((0, va), (1, vb)):
                    b, fr = bank()
                    tok = mm(PS[:, b, 0:T0], w("a2", k)[64 * n:64 * n + 64, :], HA[64 * n:64 * n + 64, :], True, True, IN_OW, *fr, inc=True)
                    t = act(v, PS[:, b, 0:T0], ACT.Sigmoid, tok, DV.last(), PE.last(), bias=par(f"a0{n}")[:, k:k + 1])
                    release(b, t)
                tt(DV, va, va, vb, ADD, t)
                ts(DV, va, va, -2.0, par("k_a")[:, k:k + 1], ADD, MUL)
                stt(DV, va, va, 2.0, Kr[:, k, :], ADD, MUL)
                t = stt(DV, va, va, par("r_k")[:, k:k + 1], Rr[:, k, :], MUL, MUL)
                bq, tq = colsum("blk", va[:, None, :], 1, T0, t)
                b, fr = bank()
                for c, (c0, cn) in enumerate(CH):
                    tok = tr(PS[:, b, c0:c0 + cn], VC[0:cn, c, 128 * k:128 * k + 128], *fr, inc=c == 2)
                t = cp(AC, vv, PS[:, b, 0:T0], tok, DV.last())
                release(b, t)
                t = tt(DV, vv, PS[:, bq, 0:T0], vv, MUL, tq, t)
                release(bq, t)
                tt(DV, y, y, vv, ADD)
                b, fr = bank()
                mm(PS[:, b, 0:T0], w("g2", k), HG, True, False, *fr)
                tok = mm(PS[:, b, 0:T0], w("g2b", k)[0:32, :], HG2[0:32, :], False, True, inc=True)
                t = tt(DV, y, y, PS[:, b, 0:T0], MUL, tok)
                release(b, t)
                split_x(x, Yb[:, k:k + 1, :], k, k + 1, t, *bar)
            linear("rw_o", 8, x, T0, lambda e, ps, tok: stt(DV, Rr[:, e, :], X[:, e, :], ALPHA, ps, MUL, ADD, tok))
            layer_norm(Rr, X, Kr, at(2 * AB, T0), T0, "ln_g10", "ln_b10", None, *done())

        phases.append(rwkv_out)

        T = T1
        XA = 8 * T
        Xm = X[:, :, 16:T0]
        SP2 = [(0, 128), (128, 128)]

        def moe():
            ar = arena_of["moe"]
            bar = done()
            state["gate"] = bar
            o = 0
            YA = cut(ar, o, 2, 1024)
            o += 2048
            lg, gt = cut(ar, o, 2, 8), cut(ar, o + 16, 2, 8)
            gq = cut(ar, o + 32, 2, 8, 8)
            g2 = cut(ar, o + 160, 2, 8, 8)
            s8 = cut(ar, o + 288, 2, 8)
            s1 = cut(ar, o + 304, 4)
            o += 320
            x = xset(0, 8, T)
            for k in range(0, 8, 2):
                split_x(x, Xm[:, k:k + 2, :], k, k + 2, *bar)
            wv, _, wt, bi, _ = weight("router", raw=True)
            for j in range(2):
                b, fr = bank()
                for k in range(8):
                    tok = mm(PS[:, b, 0:8], Xm[:, k, 128 * j:128 * j + 128], wv[:, k, :], k == 0, k == 7, wt, *(fr + bar), inc=k == 7)
                release(b, tt(DV, lg[:, j, :], PS[:, b, 0:8], par("b_router"), ADD, tok, *bar))
            state["freed"][bi] = state["read"][bi] = tok
            red(s1[:, 0:2], lg, MAXO)
            tt(DV, lg, lg, bc(s1[:, 0:2, None], 2, 8), SUB)
            t = act(lg, lg, ACT.Exp, DV.last())
            red(s1[:, 0:2], lg, ADD, t)
            rec(s1[:, 2:4], s1[:, 0:2])
            tt(DV, lg, lg, bc(s1[:, 2:4, None], 2, 8), MUL)
            for j in range(2):
                pe_ = bc(lg[:, j, :, None], 8, 8)
                pj = bc(lg[:, j, None, :], 8, 8)
                tt(DV, gq[:, j], pj, pe_, ALU.is_gt)
                tt(DV, g2[:, j], pj, pe_, ALU.is_equal)
                tt(DV, g2[:, j], g2[:, j], con("before").rearrange("p (e j) -> p e j", e=8), MUL)
                tt(DV, gq[:, j], gq[:, j], g2[:, j], ADD)
            red(s8, gq, ADD)
            ts(DV, s8, s8, 2.0, None, ALU.is_lt, None)
            tt(DV, gt, s8, lg, MUL)
            red(s1[:, 0:2], gt, ADD)
            rec(s1[:, 2:4], s1[:, 0:2])
            tt(DV, gt, gt, bc(s1[:, 2:4, None], 2, 8), MUL)
            bar = done()
            NH = 3
            H = hidden("moe", T)
            hf = [cut(ar, o + i * T, T) for i in range(NH)]
            o += NH * T
            sg = [cut(ar, o + i * 2 * T, 2, T) for i in range(2)]
            o += 4 * T
            gfree = [list(free[i]) for i in range(4)]
            dfree = [t for i in range(4, 8) for t in free[i]]
            NF = FE // 128
            hold, wd, hfree = {}, {}, {}

            def up(u):
                b = u % 4
                for g in range(2):
                    wh, wl, wt, _, _ = weight("moe")
                    for k in range(8):
                        tok = mm3(PS[:, b, T * g:T * g + T], wh[:, k, :], wl[:, k, :], x["h"][:, k, :], x["l"][:, k, :], k == 0, k == 7,
                                  *([x["tok"][k]] if u == 0 else []), *(gfree[b] + [wt] + bar if k == 0 else []), inc=k == 7)
                wh, wl, wt, bi, _ = weight("moe")
                wd[u] = (wh, wl, bi)
                s = sg[u % 2]
                t = act(s[:, 0, :], PS[:, b, 0:T], ACT.Sigmoid, tok, hold.get(u - 2))
                t = tt(DV, s[:, 1, :], PS[:, b, 0:T], s[:, 0, :], MUL, t)
                t = hold[u] = tt(DV, hf[u % NH], PS[:, b, T:2 * T], s[:, 1, :], MUL, hold.get(("split", u - NH)))
                gfree[b] = [t]
                hold["split", u] = split_hidden(H, u % NH, hf[u % NH], t, hfree.get(u - NH))

            def down(u):
                nonlocal dfree
                e, f = divmod(u, NF)
                wh, wl, bi = wd.pop(u)
                i = u % NH
                for j in range(2):
                    c = slice(128 * j, 128 * j + 128)
                    for n in range(2):
                        q = slice(512 * n, 512 * n + 512)
                        tok = mm3(PS[:, 4 + 2 * j + n, :], H["h"][:, i, c], H["l"][:, i, c], wh[:, 0, q], wl[:, 0, q],
                                  f == 0, f == NF - 1, hold["split", u], *(dfree if f == 0 else []), inc=j + n == 2)
                used(bi, tok)
                hfree[u] = tok
                if f == NF - 1:
                    for j in range(2):
                        y = YA[:, j, :].rearrange("p (n c) -> p n c", n=2)
                        src = PS[:, 4 + 2 * j:6 + 2 * j, :]
                        g = gt[:, j, e:e + 1]
                        if e == 0:
                            t = ts(DV, y, src, g, None, MUL, None, tok)
                        else:
                            t = stt(DV, y, src, g, y, MUL, ADD, tok)
                    dfree = [t]

            NU = NE * NF
            for u in range(NU + 1):
                if u < NU:
                    up(u)
                if u:
                    down(u - 1)
            xfree[0] = [PE.last()]
            for i in range(4):
                release(i, *gfree[i])
                release(4 + i, *dfree)
            R, tmp, small = cut(ar, o, 8, T), cut(ar, o + XA, 8, T), cut(ar, o + 2 * XA, T)
            bar = done()
            for d in range(8):
                b, fr = bank()
                for j in range(2):
                    tok = tr(PS[:, b, 128 * j:128 * j + 128], YA[:, j, 128 * d:128 * d + 128], *(fr + bar), inc=j == 1)
                t = stt(DV, R[:, d, :], Xm[:, d, :], ALPHA, PS[:, b, 0:T], MUL, ADD, tok, *bar)
                release(b, t)
            layer_norm(R, cut(xt, 0, 8, T), tmp, small, T, "ln_g11", "ln_b11", None, *done())

        phases.append(moe)

        X2 = cut(xt, 0, 8, T)

        def even():
            TMP, HN = at(0, 8, T), at(XA, 8, T)
            KQV = at(2 * XA, 2, 1568)
            o = 2 * XA + 3136
            CQ, CN = at(o, 5, T), at(o + 5 * T, 5, T)
            QF = at(o, 8, T)
            o += 10 * T
            RG = at(o, 4, T)
            o += 4 * T
            QM, KM = at(o, 2, 8, 96), at(o + 1536, 2, 8, 96)
            pool_o = o
            o += 3072
            VM = at(o, 2, 8, 64)
            o += 1024
            KF = at(o, 8, T)
            o += XA
            small = at(o, T)
            o += T
            posf = at(o, 8)
            o += 8
            tw = [at(o + 64 * i, 2, 32) for i in range(3)]
            o += 192
            tabs = {}
            bar = done()
            cp(DV, posf[:, 0:2], pos_t[:, 0:2], IN_POS, *bar)
            for hlf in (16, 32):
                for fn, ph in (("sin", 0.0), ("cos", 0.25)):
                    tab = at(o, 2, hlf)
                    o += 2 * hlf
                    a, n_, r = (v[:, :, 0:hlf] for v in tw)
                    for j in range(2):
                        ts(DV, a[:, j, :], con(f"inv{hlf}"), posf[:, j:j + 1], None, MUL, None, IN_CON, AC.last())
                    ts(DV, n_, a, 1.0 / (2 * np.pi), ph, MUL, ADD)
                    ts(DV, n_, n_, 12582912.0, None, ADD, None)
                    ts(DV, n_, n_, 12582912.0, None, SUB, None)
                    stt(DV, r, n_, -6.28125, a, MUL, ADD)
                    stt(DV, r, n_, -float(np.float32(2 * np.pi - 6.28125)), r, MUL, ADD)
                    ts(DV, r, r, 2 * np.pi * ph, None, ADD, None)
                    ts(DV, r, r, 3.1415925, -3.1415925, ALU.min, ALU.max)
                    act(tab, r, ACT.Sin, DV.last(), *bar)
                    tabs[fn, hlf] = tab
            lgm = at(o, 8, 8)
            o += 64
            for i, n in enumerate(("th_f", "th_b")):
                y, u, d, l = (lgm[:, 4 * i + k, :] for k in range(4))
                t = act(y, par(n), ACT.Exp, IN_PAR, *bar, scale=-float(np.log(2.0)))
                ts(DV, u, y, -1.0, 1.0, MUL, ADD, t)
                t = stt(DV, d, u, -1.0, y, ADD, ADD)
                t = act(l, u, ACT.Ln, t)
                rec(u, u, t)
                tt(DV, d, d, u, MUL)
                tt(DV, l, l, d, SUB)
            lgf, lgb = lgm[:, 3, :], lgm[:, 7, :]
            x = rms_norm(X2, HN, TMP, small, 8, T, "n_even", "o1024", 1, *bar)
            linear("e_c", 5, x, T, lambda e, ps, tok: cp(AC, CQ[:, e, :], ps, tok, *bar))
            linear_t("e_t", 5, x, SP2, lambda i, j, ps, tok: cp(
                AC if j else DV, KQV[:, j, E_T[i][0] - 640:E_T[i][0] - 640 + E_T[i][1]], ps, tok))
            KRO, RQK, RV = KQV[:, :, 0:32], KQV[:, :, 32:1056], KQV[:, :, 1056:1568]

            def rg(e, ps, tok):
                t = act(TMP[:, e, :], ps, ACT.Sigmoid, tok)
                return tt(DV, RG[:, e, :], ps, TMP[:, e, :], MUL, t)

            linear("e_g", 4, x, T, rg, *done())
            bar = done()
            xc = xset(0, 5, T)
            rms_norm(CQ[:, 0:3, :], CN[:, 0:3, :], TMP[:, 0:3, :], small, 3, T, "n_q", "o384", 0, *bar, x=xc)
            rms_norm(CQ[:, 3:5, :], CN[:, 3:5, :], TMP[:, 3:5, :], small, 2, T, "n_kv", "o256", 0, *done(), x=xc, k0=3)
            xq = {**xc, "h": xc["h"][:, 0:3, :], "l": xc["l"][:, 0:3, :]}
            linear_t("uq", 2, xq, SP2,
                     lambda i, j, ps, tok: cp(AC, QM[:, j, 4 * i:4 * i + 4, :], ps.rearrange("p (h c) -> p h c", h=4), tok), *done())
            xkv = {**xc, "h": xc["h"][:, 3:5, :], "tok": {0: xc["tok"][3], 1: xc["tok"][4]}, "at": 3 * T}

            def kv(i, j, ps, tok):
                v = ps.rearrange("p (h c) -> p h c", h=4)
                cp(AC, KM[:, j, 4 * i:4 * i + 4, 0:64], v[:, :, 0:64], tok)
                return cp(AC, VM[:, j, 4 * i:4 * i + 4, :], v[:, :, 64:128])

            linear_t("ukv", 2, xkv, SP2, kv)
            bar = done()
            for j in range(2):
                cp(DV, KM[:, j, :, 64:96], bc(KRO[:, j, None, :], 8, 32), *bar)
            rt = cut(arena, 0, 4, 8, 32)
            rt2 = cut(arena, 1024, 4, 8, 32)

            def rope(E, w4, v, h, hlf, j, *waits):
                c = bc(tabs["cos", hlf][:, j, None, :], h, hlf)
                s = bc(tabs["sin", hlf][:, j, None, :], h, hlf)
                x1, x2 = v[:, :, 0:hlf], v[:, :, hlf:2 * hlf]
                w = [w4[:, i, 0:h, 0:hlf] for i in range(4)]
                tt(E, w[0], x1, c, MUL, *waits)
                tt(E, w[1], x2, s, MUL)
                tt(E, w[2], x2, c, MUL)
                tt(E, w[3], x1, s, MUL)
                tt(E, x1, w[0], w[1], SUB)
                return tt(E, x2, w[2], w[3], ADD)

            for half in range(2):
                for j in range(2):
                    v = RQK[:, j, 512 * half:512 * half + 512].rearrange("p (h c) -> p h c", h=8)
                    rope(PO, rt2, v, 8, 32, j, *bar)
            ts(PO, RQK[:, :, 512:1024], RQK[:, :, 512:1024], 64.0 ** -0.5, None, MUL, None)
            sq = HN.rearrange("p a t -> p (a t)")[:, 0:768].rearrange("p (h c) -> p h c", h=8)
            ss = small[:, 0:16]
            for M, g in ((QM, "n_qh"), (KM, "n_kh")):
                for j in range(2):
                    v = M[:, j]
                    tt(DV, sq, v, v, MUL, *bar)
                    red(ss[:, 0:8], sq, ADD)
                    t = ts(DV, ss[:, 0:8], ss[:, 0:8], 1.0 / 96, 1e-6, MUL, ADD)
                    t = act(ss[:, 8:16], ss[:, 0:8], ACT.Sqrt, t)
                    rec(ss[:, 8:16], ss[:, 8:16], t)
                    tt(DV, v, v, bc(ss[:, 8:16, None], 8, 96), MUL)
                    tt(DV, v, v, bc(par(g)[:, None, :], 8, 96), MUL)
                    rope(DV, rt, v[:, :, 64:96], 8, 16, j)
            bar = done()
            RF = HN
            for M, F in ((QM, QF), (KM, KF)):
                for j in range(2):
                    for q in range(2):
                        b, fr = bank()
                        for h in range(4):
                            tok = tr(PS[0:96, b, 128 * h:128 * h + 128], M[:, j, 4 * q + h, :], *(fr + bar), inc=h == 3)
                        release(b, cp(AC, F[0:96, 4 * q:4 * q + 4, 128 * j:128 * j + 128],
                                      PS[0:96, b, :].rearrange("p (h t) -> p h t", h=4), tok))
            for j in range(2):
                for q in range(2):
                    b, fr = bank()
                    for h in range(4):
                        tok = tr(PS[:, b, 128 * h:128 * h + 128], RQK[:, j, 512 * q + 128 * h:512 * q + 128 * h + 128], *(fr + bar), inc=h == 3)
                    release(b, cp(DV, RF[:, 4 * q:4 * q + 4, 128 * j:128 * j + 128], PS[:, b, :].rearrange("p (h t) -> p h t", h=4), tok))
            bar = done()
            P = [at(pool_o + 512 * i, 2, T) for i in range(2)]
            PT = [at(pool_o + 1024 + 512 * i, 2, T) for i in range(2)]
            Dt = [at(pool_o + 2048 + 512 * i, 2, T) for i in range(2)]
            CA = at(2 * XA, 4, T)
            OR = TMP[:, 0:4, :]
            sm = [at(o + 16 * i, 16) for i in range(2)]
            o += 32
            scale = 96.0 ** -0.5
            freeP, freePT, ready = [[], []], [[], []], {}
            xo = xset(1, 8, T)

            def mscore(h):
                i = h % 2
                b, fr = bank()
                for j in range(2):
                    tok = mm(PS[:, b, T * j:T * j + T], QF[0:96, h, 128 * j:128 * j + 128], KF[0:96, h, :], True, True, *(fr + bar), inc=j == 1)
                v = PS[:, b, :].rearrange("p (j t) -> p j t", j=2)
                m = sm[i]
                red(m[:, 0:2], v, MAXO, tok)
                t = ts(DV, m[:, 2:4], m[:, 0:2], -scale, None, MUL, None)
                for j in range(2):
                    t = act(P[i][:, j, :], v[:, j, :], ACT.Exp, t, *freeP[i], bias=m[:, 2 + j:3 + j], scale=scale, accum=m[:, 4 + j:5 + j])
                release(b, t)
                rec(m[:, 6:8], m[:, 4:6], t)
                ready[h] = tt(DV, P[i], P[i], bc(m[:, 6:8, None], 2, T), MUL)

            def mrest(h):
                i = h % 2
                b, fr = bank()
                v = PS[:, b, :].rearrange("p (k t) -> p k t", k=2)
                for j in range(2):
                    for k in range(2):
                        tok = tr(v[:, k, 128 * j:128 * j + 128], P[i][:, j, 128 * k:128 * k + 128], ready[h], *fr, inc=j + k == 2)
                freeP[i] = [tok]
                t = cp(AC, PT[i], v, tok, *freePT[i])
                release(b, t)
                rows = slice(64 * (h % 2), 64 * (h % 2) + 64)
                b, fr = bank()
                for k in range(2):
                    tok = mm(PS[rows, b, 0:T], VM[:, k, h, :], PT[i][:, k, :], k == 0, k == 1, t, *fr, inc=k == 1)
                freePT[i] = [tok]
                t = cp(AC, CA[rows, h // 2, :], PS[rows, b, 0:T], tok)
                release(b, t)
                if h % 2:
                    split_x(xo, CA[:, h // 2:h // 2 + 1, :], h // 2, h // 2 + 1, t)

            for h in range(9):
                if h < 8:
                    mscore(h)
                if h:
                    mrest(h - 1)
            bar = done()
            rel = KF.rearrange("p a t -> p (a t)")[:, 0:1024]
            CR = QF[:, 0:4, :]
            load(PO, rel, rel_d, s_in["rel"], *bar)
            relp, reln = rel[:, 0:512].rearrange("p (j t) -> p j t", j=2), rel[:, 512:1024].rearrange("p (j t) -> p j t", j=2)
            fin = {}
            for h in range(8):
                i = h % 2
                rows = slice(64 * (h % 2), 64 * (h % 2) + 64)
                ts(DV, Dt[i], reln, lgb[:, h:h + 1], None, MUL, None, fin.get(h - 2), IN_REL, *bar)
                t = stt(DV, Dt[i], relp, lgf[:, h:h + 1], Dt[i], MUL, ADD)
                td = act(Dt[i], Dt[i], ACT.Exp, t)
                b, fr = bank()
                for j in range(2):
                    tok = mm(PS[:, b, T * j:T * j + T], RF[rows, 4 + h // 2, 128 * j:128 * j + 128], RF[rows, h // 2, :], True, True, *(fr + bar), inc=j == 1)
                t = tt(DV, Dt[i], Dt[i], PS[:, b, :].rearrange("p (j t) -> p j t", j=2), MUL, tok, td)
                release(b, t)
                b, fr = bank()
                for j in range(2):
                    tok = mm(PS[rows, b, 0:T], RV[:, j, 64 * h:64 * h + 64], Dt[i][:, j, :], j == 0, j == 1, t, *fr, inc=j == 1)
                fin[h] = tok
                release(b, cp(AC, OR[rows, h // 2, :], PS[rows, b, 0:T], tok))
            bar = done()
            for k in range(4):
                t = act(TMP[:, 4 + k, :], OR[:, k, :], ACT.Square, *bar)
                b, tok = colsum("blk64", TMP[:, 4 + k:5 + k, :], 1, T, t)
                t = rsq(small, PS[:, b, 0:T], 1e-6, tok)
                release(b, t)
                stt(DV, CR[:, k, :], OR[:, k, :], par("n_ret")[:, k:k + 1], small, MUL, MUL)
                t = tt(DV, CR[:, k, :], CR[:, k, :], RG[:, k, :], MUL)
                split_x(xo, CR[:, k:k + 1, :], 4 + k, 5 + k, t)
            linear("e_o", 8, xo, T, lambda e, ps, tok: tt(DV, X2[:, e, :], X2[:, e, :], ps, ADD, tok))

        phases.append(even)

        def conv_ffn(i):
            ar = arena_of[f"conv{i}"]
            TMP, HN = cut(ar, 0, 8, T), cut(ar, XA, 8, T)
            o = 2 * XA
            small = cut(ar, o, T)
            o += T
            gp = [cut(ar, o + 258 * j, 258) for j in range(2)]
            o += 516
            cv = [cut(ar, o + 256 * j, 256) for j in range(2)]
            o += 512
            sg = [cut(ar, o + 256 * j, 256) for j in range(2)]
            bar = done()
            x = rms_norm(X2, HN, TMP, small, 8, T, f"n_ffn{i}", "o1024", 0, *bar)
            for j in range(2):
                mset(DV, gp[j][:, 0:1], 0.0, *bar)
                tz = mset(DV, gp[j][:, 257:258], 0.0)
            H = hidden(f"conv{i}", T)
            hold, cvt = {}, {}

            def evac(e, ps, tok):
                f = e // 2
                s = f % 2
                if e % 2 == 0:
                    t = cp(AC, gp[s][:, 1:257], ps, tok, cvt.get(f - 2), tz)
                    ts(DV, cv[s], gp[s][:, 0:256], par(f"cw{i}0")[:, f:f + 1], None, MUL, None, t, hold.get(f - 2))
                    stt(DV, cv[s], gp[s][:, 1:257], par(f"cw{i}1")[:, f:f + 1], cv[s], MUL, ADD)
                    t2 = stt(DV, cv[s], gp[s][:, 2:258], par(f"cw{i}2")[:, f:f + 1], cv[s], MUL, ADD)
                    t3 = act(sg[s], cv[s], ACT.Sigmoid, t2, bias=par(f"cb{i}")[:, f:f + 1])
                    cvt[f] = stt(DV, cv[s], cv[s], par(f"cb{i}")[:, f:f + 1], sg[s], ADD, MUL, t3)
                    return t
                t = tt(DV, cv[s], cv[s], ps, MUL, tok)
                hold[f] = split_hidden(H, f, cv[s], t, *bar)
                return t

            linear(f"cu{i}", 44, x, T, evac)
            linear(f"cd{i}", 8, H, T, lambda e, ps, tok: tt(DV, X2[:, e, :], X2[:, e, :], ps, ADD, tok))

        phases.append(lambda: conv_ffn(0))

        def odd():
            HN, TMP = at(0, 8, T), at(XA, 8, T)
            o = 2 * XA
            small = at(o, T)
            o += T
            GQ, GK = at(o, 4, T), at(o + 4 * T, 4, T)
            o += 8 * T
            GV = at(o, 2, 1024)
            o += 2048
            LA = [at(o + 4 * T * i, 4, T) for i in range(2)]
            o += 8 * T
            RGo = at(o, 8, T)
            o += 8 * T
            QC, KC = at(o, 4, T), at(o + 4 * T, 4, T)
            KDT, S = at(o, 2, 512), at(o + 4 * T, 4, 256)
            QB, KE = at(o + 8 * T, 4, T), at(o + 12 * T, 4, T)
            o += 16 * T
            AT = at(o, 2, 4, 64)
            o += 512
            mid, lst = at(o, 16), at(o + 16, 4, 4)
            one = at(o + 32, T)
            o += 32 + T
            bar = done()
            x = rms_norm(X2, HN, TMP, small, 8, T, "n_odd", "o1024", 1, *bar)

            def qk(e, ps, tok):
                if e < 4:
                    return act(GQ[:, e, :], ps, ACT.Copy, tok, *bar, scale=128.0 ** -0.5)
                return cp(AC, GK[:, e - 4, :], ps, tok)

            linear("o_qk", 8, x, T, qk)
            linear_t("o_v", 3, x, SP2, lambda i, j, ps, tok: cp(
                AC if j else DV, GV[:, j, THIRDS[i]:THIRDS[i] + ps.shape[1]], ps, tok, *bar))
            xa = [xset(0, 2, T)]
            ga = at(o, 2, T)

            def lowrank(e, ps, tok):
                t = cp(AC, ga[0:16, e, :], ps, tok, *bar)
                cp(AC, xa[0]["h"][0:16, e, :], ga[0:16, e, :], *xfree[0])
                tt(DV, xa[0]["l"][0:16, e, :], ga[0:16, e, :], f32(xa[0]["h"][0:16, e, :]), SUB, AC.last(), *xfree[0])
                return t

            linear("o_a", 2, x, T, lowrank)
            ready = done()
            wh, wl, wt, closes, _ = weight("gg")
            tmp = TMP[:, 0:4, :]
            ab = TMP[:, 4:8, :]
            for n in range(2):
                for h in range(4):
                    b, fr = bank()
                    c = slice(512 * n + 128 * h, 512 * n + 128 * h + 128)
                    tok = mm3(PS[:, b, 0:T], wh[0:16, 0, c], wl[0:16, 0, c], xa[0]["h"][0:16, n, :], xa[0]["l"][0:16, n, :], True, True,
                              wt, *(fr + ready), inc=True)
                    t = ts(DV, LA[n][:, h, :], PS[:, b, 0:T], par(("b_gf", "b_gb")[n])[:, h:h + 1], None, ADD, None, tok, *bar)
                    release(b, t)
                act(ab, LA[n], ACT.Abs, t)
                act(ab, ab, ACT.Exp, scale=-1.0)
                t = act(ab, ab, ACT.Ln, bias=1.0)
                stt(DV, LA[n], LA[n], 0.0, ab, ALU.min, SUB, t)
                ts(DV, LA[n], LA[n], 1.0 / 16, None, MUL, None)
            used(closes, tok)
            xfree[0] = [tok]
            bar = done()

            def rg(e, ps, tok):
                t = act(TMP[:, e, :], ps, ACT.Sigmoid, tok, *bar)
                return tt(DV, RGo[:, e, :], ps, TMP[:, e, :], MUL, t, *bar)

            linear("o_g", 8, x, T, rg)
            bar = done()
            mset(DV, one, 1.0, *bar)
            mset(DV, one.rearrange("p (c t) -> p c t", c=4)[:, :, 0:1], 0.0)
            Bc = TMP[:, 0:4, :]
            Ex = TMP[:, 4:8, :]
            OG = HN

            def c4(v):
                return v.rearrange("p a (c t) -> p (a c) t", c=4)

            for n in range(2):
                bar = done()
                for h in range(4):
                    cum, la_ = Bc[:, h, :], LA[n][:, h, :]
                    if n == 1:
                        cum, la_ = cum[:, ::-1], la_[:, ::-1]
                    DV(lambda e, a=cum, l=la_: e.tensor_tensor_scan(a, one, l, 0.0, MUL, ADD), *bar)
                mi, la = (32, 63) if n == 0 else (31, 0)
                bm = c4(Bc)[:, :, mi:mi + 1]
                bl = c4(Bc)[:, :, la:la + 1]
                t = act(Ex, Bc, ACT.Exp, DV.last())
                tt(DV, QB, GQ, Ex, MUL, t)
                act(lst.rearrange("p a c -> p (a c)"), bl[:, :, 0], ACT.Exp, DV.last())
                t = tt(DV, c4(Ex), bc(bl, 16, 64), c4(Bc), SUB, t)
                t = act(Ex, Ex, ACT.Exp, t)
                tt(DV, KE, GK, Ex, MUL, t)
                cp(DV, mid, bm[:, :, 0])
                t = tt(DV, c4(Bc), c4(Bc), bc(mid[:, :, None], 16, 64), SUB, AC.last())
                t = act(Ex, Bc, ACT.Exp, t)
                tt(DV, QC, GQ, Ex, MUL, t)
                t = act(Ex, Bc, ACT.Exp, DV.last(), scale=-1.0)
                tt(DV, KC, GK, Ex, MUL, t)
                mset(DV, AT, 0.0)
                bar = done()
                b, fr = bank()
                for c in range(4):
                    rows = slice(64 * (c % 2), 64 * (c % 2) + 64)
                    for h in range(4):
                        k = 256 * (c // 2) + 64 * h
                        tok = mm(PS[rows, b, k:k + 64], KC[:, h, 64 * c:64 * c + 64], QC[:, h, 64 * c:64 * c + 64], True, True,
                                 *(fr + bar), inc=c * h == 9)
                ATf = AT.rearrange("p c h t -> p (c h) t")
                tA = DV(lambda e, b=b, n=n: e.copy_predicated(ATf, bc(con(f"gm{n}")[:, None, :], 8, 64).bitcast(u32),
                                                              PS[:, b, :].rearrange("p (k t) -> p k t", k=8)), tok)
                release(b, tA)
                for j in range(2):
                    b, fr = bank()
                    for h in range(4):
                        tok2 = tr(PS[:, b, 128 * h:128 * h + 128], KE[:, h, 128 * j:128 * j + 128], *(fr + bar), inc=h == 3)
                    tK = cp(AC, KDT[:, j, :], PS[:, b, :], tok2)
                    release(b, tK)
                tS = None
                for ci, c in enumerate(range(4) if n == 0 else range(3, -1, -1)):
                    rows = slice(64 * (c % 2), 64 * (c % 2) + 64)
                    j = c // 2
                    b, fr = bank()
                    for h in range(4):
                        for v in range(2):
                            out = PS[:, b, 128 * h + 64 * v:128 * h + 64 * v + 64]
                            mm(out, GV[rows, j, 256 * h + 128 * v:256 * h + 128 * v + 128], AT[rows, j, h, :], True, ci == 0, tA, *fr)
                            if ci:
                                mm(out, S[:, h, 128 * v:128 * v + 128], QB[:, h, 64 * c:64 * c + 64], False, True, tS)
                    bs, fs = bank(2)
                    for h in range(4):
                        tok = mm(PS[:, bs + h // 2, 256 * (h % 2):256 * (h % 2) + 256], KDT[rows, j, 128 * h:128 * h + 128],
                                 GV[rows, j, 256 * h:256 * h + 256], True, True, tK, *fs, inc=h == 3)
                    src = PS[:, b, :].rearrange("p (k t) -> p k t", k=8)
                    dst = OG[:, :, 64 * c:64 * c + 64]
                    t = cp(DV, dst, src, tok) if n == 0 else tt(DV, dst, dst, src, ADD, tok)
                    release(b, t)
                    for h in range(4):
                        st = PS[:, bs + h // 2, 256 * (h % 2):256 * (h % 2) + 256]
                        if ci == 0:
                            tS = cp(DV, S[:, h, :], st)
                        else:
                            tS = stt(DV, S[:, h, :], S[:, h, :], lst[:, h, c:c + 1], st, MUL, ADD)
                    release(bs, tS, n=2)
            bar = done()
            xo = xset(0, 8, T)
            for h in range(4):
                t = act(TMP[:, 2 * h:2 * h + 2, :], OG[:, 2 * h:2 * h + 2, :], ACT.Square, *bar)
                b, tok = colsum("o256", TMP[:, 2 * h:2 * h + 2, :], 2, T, t)
                t = rsq(small, PS[:, b, 0:T], 1e-6, tok)
                release(b, t)
                for v in range(2):
                    k = 2 * h + v
                    stt(DV, OG[:, k, :], OG[:, k, :], par("n_gla")[:, k:k + 1], small, MUL, MUL)
                    t = tt(DV, OG[:, k, :], OG[:, k, :], RGo[:, k, :], MUL)
                split_x(xo, OG[:, 2 * h:2 * h + 2, :], 2 * h, 2 * h + 2, t)
            linear("o_o", 8, xo, T, lambda e, ps, tok: tt(DV, X2[:, e, :], X2[:, e, :], ps, ADD, tok))

        phases.append(odd)
        phases.append(lambda: conv_ffn(1))

        for i, ph in enumerate(phases):
            if i < stop:
                ph()

        load(SP, xt[:, :].rearrange("p (n t) -> p n t", n=8), x_d, s_in["x"])
        nb = state["next"]
        off = 0
        for bi in range(nb):
            w = blocks[bi][1]
            src = ws_d[off:off + 128 * w].rearrange("(p w) -> p w", p=128)
            off += 128 * w
            load(SP, ring[:, bi % RING, 0:w], src, s_w[bi % RING], state["freed"][bi - RING] if bi >= RING else None)
            if bi == 1:
                load(SP, con_t[:, :], con_d, s_in["con"])
                load(SP, par_t[:, :], par_d, s_in["par"])
                load(SP, pos_t[:, 0:2], pos_d, s_in["pos"])
        if stop > len(phases):
            load(SP, out_d, X2, s_out, *done())
            SP(None, (s_out, 16), inc=False, chain=False)

        block = ctx.enter_context(nc.Block())

        @block.sync
        def _(e):
            SP.emit(e)

        @block.tensor
        def _(e):
            PE.emit(e)

        @block.vector
        def _(e):
            DV.emit(e)

        @block.scalar
        def _(e):
            AC.emit(e)

        @block.gpsimd
        def _(e):
            PO.emit(e)


def host_inputs(inp):
    inp = {k: np.asarray(v) for k, v in inp.items()}
    h = np.concatenate([inp["meta"], inp["x"][0]], axis=0)
    return {
        "x_d": np.ascontiguousarray(h.T.reshape(8, 128, T0).transpose(1, 0, 2)),
        "ws_d": pack_stream(inp),
        "par_d": pack(params(), inp),
        "con_d": pack(consts(), inp),
        **{n: pack(f(), inp) for n, f in SETS.items()},
        "pos_d": np.ascontiguousarray(inp["positions_2"].reshape(2, 128).T),
    }


def kernel(**inputs):
    import concourse.bacc as bacc
    from concourse.bass_utils import run_bass_kernel_spmd as run
    arrays = host_inputs(inputs)
    nc = bacc.Bacc("TRN2", target_bir_lowering=False, num_devices=1)
    aps = {n: nc.dram_tensor(n, a.shape, mybir.dt.from_np(a.dtype), kind="ExternalInput").ap() for n, a in arrays.items()}
    out = nc.dram_tensor("out_d", (128, 8, T1), mybir.dt.float32, kind="ExternalOutput").ap()
    build(nc, out_d=out, **aps)
    r = run(nc, [arrays], core_ids=[0])
    got = r.results[0]["out_d"]
    return np.ascontiguousarray(got.transpose(1, 0, 2).reshape(D, T1).T).reshape(1, T1, D)
```

```python
import numpy as np
import concourse.bass as bass
from concourse import mybir
from contextlib import ExitStack

D, T0, T1, C = 1024, 272, 256, 96
TP = 288
FF, FE, NE = 2816, 3584, 8
ALPHA = float(4.0 ** 0.25)
LAM_INIT = 0.8 - 0.6 * float(np.exp(0.0))
BW = 3072
RING = 3
SLOTS = 2
PIECE = 1024


def tiles_of(name, get, nk, cols, wide=0):
    return [(name, get, nk, c0, cw, max(cw, wide)) for c0, cw in cols]


def cuts(n, w, c0=0):
    return [(c0 + i, min(w, n - i)) for i in range(0, n, w)]


E_T = [(640, 314), (954, 314), (1268, 314), (1582, 314), (1896, 312)]


def stream_tiles():
    def g(name, *idx):
        return lambda inp: inp[name][idx] if idx else inp[name]

    def two(name):
        return lambda inp: np.concatenate([inp[name][0, 0], inp[name][0, 1]], axis=1)

    def gate_up(e, f):
        c = slice(128 * f, 128 * f + 128)
        return lambda inp: np.concatenate([inp["moe_w_gate"][0, e][:, c], inp["moe_w_up"][0, e][:, c]], axis=1)

    t = []
    t += tiles_of("attn_qk", g("attn_w_in", 0), 8, cuts(2048, 128))
    t += tiles_of("attn_v", g("attn_w_in", 0), 8, [(2048, 384), (2432, 384), (2816, 256)])
    t += tiles_of("attn_o", g("attn_w_o", 0), 8, cuts(D, 128))
    for f in range(22):
        t += tiles_of("ffn_gu", g("ffn_w_gate", 0), 8, [(128 * f, 128)])
        t += tiles_of("ffn_gu", g("ffn_w_up", 0), 8, [(128 * f, 128)])
    t += tiles_of("ffn_d", g("ffn_w_down", 0), 22, cuts(D, 128))
    for i in range(3):
        t += tiles_of(f"rkv{i}", g("rw_w_rkv", 0, i), 8, cuts(D, 128))
    t += tiles_of("lw", two("rw_w1"), 8, [(0, 128)])
    t += tiles_of("la", two("rw_a1"), 8, [(0, 128)])
    t += tiles_of("lg", g("rw_g1", 0), 8, [(0, 128), (128, 32)], 128)
    t += tiles_of("rw_o", g("rw_w_o", 0), 8, cuts(D, 128))
    t += tiles_of("router", g("moe_w_router", 0), 8, [(0, 8)])
    for e in range(NE):
        for f in range(FE // 128):
            t += tiles_of("moe", gate_up(e, f), 8, [(0, 256)])
            t += tiles_of("moe", lambda inp, e=e, f=f: inp["moe_w_down"][0, e, 128 * f:128 * f + 128], 1, [(0, D)])
    w = g("w_in_even_2", 0)
    t += tiles_of("e_c", w, 8, cuts(640, 128))
    t += tiles_of("e_t", w, 8, E_T)
    t += tiles_of("e_g", w, 8, cuts(512, 128, 2208))
    t += tiles_of("uq", g("mla_w_uq_2", 0), 3, [(0, 384), (384, 384)])
    t += tiles_of("ukv", g("mla_w_ukv_2", 0), 2, [(0, 512), (512, 512)])
    t += tiles_of("e_o", g("w_out_even_2", 0), 8, cuts(D, 128))

    def conv(i):
        r = []
        for f in range(22):
            r += tiles_of(f"cu{i}", g("ffn_w_up_2", i), 8, [(128 * f, 128)])
            r += tiles_of(f"cu{i}", g("ffn_w_up_2", i), 8, [(FF + 128 * f, 128)])
        return r + tiles_of(f"cd{i}", g("ffn_w_down_2", i), 22, cuts(D, 128))

    t += conv(0)
    w = g("w_in_odd_2", 0)
    t += tiles_of("o_qk", w, 8, cuts(1024, 128))
    t += tiles_of("o_v", w, 8, [(1024, 384), (1408, 384), (1792, 256)])
    t += tiles_of("o_a", w, 8, [(3072, 16), (3088, 16)], 128)
    t += tiles_of("gg", lambda inp: np.concatenate([inp["gla_w_gate_fwd_2"][0], inp["gla_w_gate_bwd_2"][0]], axis=1),
                  1, [(0, 1024)])
    t += tiles_of("o_g", w, 8, cuts(1024, 128, 2048))
    t += tiles_of("o_o", g("w_out_odd_2", 0), 8, cuts(D, 128))
    t += conv(1)
    return t


ALONE = ("moe", "router")


def stream_blocks():
    blocks, width = [], BW + 1
    for t in stream_tiles():
        w = t[2] * t[5]
        if width + w > BW or (t[0] in ALONE and blocks[-1][-1][0][0] != t[0]) or blocks[-1][-1][0][0] in ("lg", "router"):
            blocks.append([])
            width = 0
        blocks[-1].append((t, width))
        width += w
    return [(b, b[-1][1] + b[-1][0][2] * b[-1][0][5]) for b in blocks]


def pack_stream(inp):
    parts = []
    blocks = stream_blocks()
    out = np.zeros(sum(128 * w for _, w in blocks), np.float32)
    off = 0
    for b, w in blocks:
        dst = out[off:off + 128 * w].reshape(128, w)
        for (name, get, nk, c0, cw, pw), x in b:
            src = get(inp)[:, c0:c0 + cw]
            if nk == 1:
                dst[:src.shape[0], x:x + cw] = src
            else:
                dst[:, x:x + nk * pw].reshape(128, nk, pw)[:, :, 0:cw] = src.reshape(nk, 128, cw).transpose(1, 0, 2)
        off += 128 * w
    return out


def params():
    def fm(get):
        return lambda inp: np.reshape(get(inp), (-1, 128)).T

    def rep(get):
        return lambda inp: np.broadcast_to(np.reshape(get(inp), (1, -1)), (128, np.size(get(inp))))

    p = []
    for i in range(2):
        for j in range(2):
            p.append((f"ln_g{i}{j}", 8, fm(lambda inp, i=i, j=j: inp["ln_g"][i, j])))
            p.append((f"ln_b{i}{j}", 8, fm(lambda inp, i=i, j=j: inp["ln_b"][i, j])))
    p.append(("subln", 1, fm(lambda inp: inp["attn_subln_g"][0])))
    for n in ("q1", "q2", "k1", "k2"):
        p.append((f"lam_{n}", 64, rep(lambda inp, n=n: inp[f"attn_lam_{n}"][0])))
    for s in range(2):
        for m in range(6):
            p.append((f"mu{s}{m}", 8, fm(lambda inp, s=s, m=m: inp["rw_mu"][0, s, m])))
        p.append((f"w0{s}", 8, fm(lambda inp, s=s: inp["rw_w0"][0, s])))
        p.append((f"a0{s}", 8, fm(lambda inp, s=s: inp["rw_a0"][0, s])))
    for n in ("k_k", "k_a", "r_k", "lnx_g", "lnx_b"):
        p.append((n, 8, fm(lambda inp, n=n: inp[f"rw_{n}"][0])))
    p.append(("b_router", 8, rep(lambda inp: inp["moe_b_router"][0])))
    p.append(("n_even", 8, fm(lambda inp: inp["mix_norm_even_2"][0])))
    p.append(("n_q", 3, fm(lambda inp: inp["mla_q_norm_2"][0])))
    p.append(("n_kv", 2, fm(lambda inp: inp["mla_kv_norm_2"][0])))
    p.append(("n_qh", 96, rep(lambda inp: inp["mla_q_head_norm_2"][0])))
    p.append(("n_kh", 96, rep(lambda inp: inp["mla_k_head_norm_2"][0])))
    p.append(("th_f", 8, rep(lambda inp: inp["ret_theta_fwd_2"][0])))
    p.append(("th_b", 8, rep(lambda inp: inp["ret_theta_bwd_2"][0])))
    p.append(("n_ret", 4, fm(lambda inp: inp["ret_out_norm_2"][0])))
    p.append(("n_odd", 8, fm(lambda inp: inp["mix_norm_odd_2"][0])))
    p.append(("b_gf", 4, fm(lambda inp: inp["gla_b_gate_fwd_2"][0])))
    p.append(("b_gb", 4, fm(lambda inp: inp["gla_b_gate_bwd_2"][0])))
    p.append(("n_gla", 8, fm(lambda inp: inp["gla_out_norm_2"][0])))
    for i in range(2):
        p.append((f"n_ffn{i}", 8, fm(lambda inp, i=i: inp["ffn_norm_2"][i])))
        for j in range(3):
            p.append((f"cw{i}{j}", 22, fm(lambda inp, i=i, j=j: inp["ffn_conv_w_2"][i, j])))
        p.append((f"cb{i}", 22, fm(lambda inp, i=i: inp["ffn_conv_b_2"][i])))
    return p


def columns(items):
    at, out = 0, {}
    for name, n, _ in items:
        out[name] = (at, n)
        at += n
    return out, at


def pack(items, inp):
    at, n = columns(items)
    out = np.zeros((128, n), np.float32)
    for name, w, get in items:
        v = get(inp)
        out[:v.shape[0], at[name][0]:at[name][0] + w] = v
    return out


def consts():
    f = np.float32
    p = np.arange(128)
    e8 = np.arange(8)

    def full(n):
        return lambda _: np.full((128, 128), 1.0 / n, f)

    blk = ((p[:, None] // 64) == (p[None, :] // 64)).astype(f)
    i64, j64 = np.arange(64)[None, :], (p % 64)[:, None]
    c = [("ident", 128, lambda _: np.eye(128, dtype=f)),
         ("o1024", 128, full(1024)), ("o128", 128, full(128)), ("o256", 128, full(256)), ("o384", 128, full(384)),
         ("blk", 128, lambda _: blk), ("blk64", 128, lambda _: blk / f(64)),
         ("gm0", 64, lambda _: (j64 <= i64).astype(f)), ("gm1", 64, lambda _: (j64 > i64).astype(f))]
    for h in (16, 32):
        inv = (f(10000.0) ** (-np.arange(h, dtype=f) / f(h))).astype(f)
        c.append((f"inv{h}", h, lambda _, inv=inv: np.broadcast_to(inv[None], (128, len(inv)))))
    c.append(("before", 64, lambda _: np.broadcast_to((e8[None, :] < e8[:, None]).astype(f).reshape(1, 64), (128, 64))))
    return c


def distances():
    q = np.arange(384).reshape(3, 128).T
    negd = -np.abs(q[:, :, None] - np.arange(T0)[None, None, :]).astype(np.float32)
    return [("negd", 3 * T0, lambda _: negd.reshape(128, -1))]


def relatives():
    j2 = np.arange(256).reshape(2, 128).T
    rel = (np.arange(256)[None, None, :] - j2[:, :, None]).astype(np.float32)
    return [("relp", 512, lambda _: np.maximum(rel, 0).reshape(128, -1)),
            ("reln", 512, lambda _: np.maximum(-rel, 0).reshape(128, -1))]


def scan_consts():
    f = np.float32
    s, t = np.arange(C)[:, None], np.arange(C)[None, :]
    c = [("up", C, lambda _: (s < t).astype(f)), ("upi", C, lambda _: (s <= t).astype(f)),
         ("dn", C, lambda _: (s > t).astype(f)), ("dni", C, lambda _: (s >= t).astype(f)),
         ("nup", C, lambda _: -(s < t).astype(f)), ("ndn", C, lambda _: -(s > t).astype(f))]
    for lv in range(7):
        m = ((s >> (lv + 1)) == (t >> (lv + 1))) & (((s >> lv) & 1) == 0) & (((t >> lv) & 1) == 1)
        c.append((f"lu{lv}", C, lambda _, m=m: m.astype(f)))
        c.append((f"ld{lv}", C, lambda _, m=m: m.T.astype(f)))
    at0 = np.ones(T0, f)
    at0[::C] = 0
    at1 = np.ones(T0, f)
    at1[[0, T0 - 2 * C, T0 - C]] = 0
    for n, a in (("begin0", at0), ("begin1", at1)):
        c.append((n, T0, lambda _, a=a: np.broadcast_to(a[None], (128, T0))))
    c.append(("w2", D, lambda inp: np.reshape(inp["rw_w2"][0], (128, D))))
    c.append(("a2", D, lambda inp: np.reshape(inp["rw_a2"][0], (128, D))))
    return c


def moe_consts():
    p = np.arange(128)
    f = np.float32
    return [("iota", 128, lambda _: np.broadcast_to(p.astype(f)[None], (128, 128))),
            ("lt", 128, lambda _: (p[:, None] < p[None, :]).astype(f)),
            ("ones", 128, lambda _: np.ones((128, 128), f))]


def out_weights():
    return [("g2", D, lambda inp: inp["rw_g2"][0, 0:128]),
            ("g2b", D, lambda inp: inp["rw_g2"][0, 128:160]),
            ("a2", D, lambda inp: np.reshape(inp["rw_a2"][0], (128, D)))]


SETS = {"dis_d": distances, "scn_d": scan_consts, "rel_d": relatives, "ow_d": out_weights, "moe_d": moe_consts}


class Eng:

    def __init__(self, sem):
        self.sem, self.n, self.queue, self.way, self.ways, self.sems = sem, 0, [], None, [], []

    def __call__(self, fn, *waits, inc=True, chain=True):
        if self.way:
            return self.way(fn, *waits, inc=inc, chain=chain)
        w = [x for x in waits if x is not None]
        if chain and self.n:
            w.append((self.sem, self.n))
        self.n += 1 if inc else 0
        self.queue.append((fn, w, inc))
        return (self.sem, self.n)

    def last(self):
        if self.way:
            return self.way.last()
        return (self.sem, self.n) if self.n else None

    def way_begin(self, flag, *waits):
        own = [(self.sem, self.n)] if self.n else []
        self.ways = [Eng(s) for s in self.sems]
        self.queue.append((flag, [*waits, *own], self.ways))
        self.way = self.ways[0]

    def way_else(self):
        self.way = self.ways[1]

    def way_end(self):
        self.way = None
        self.n += 1

    def emit(self, eng, seen=None):
        seen = {} if seen is None else seen
        for fn, waits, inc in self.queue:
            for sem, v in waits:
                if seen.get(id(sem), 0) < v:
                    eng.wait_ge(sem, v)
                    seen[id(sem)] = v
            if isinstance(inc, list):
                few = eng.value_load(fn)
                with eng.If(few > 0):
                    inc[0].finish(eng, dict(seen), self.sem)
                with eng.Else():
                    inc[1].finish(eng, dict(seen), self.sem)
                continue
            if fn is None:
                continue
            ins = fn(eng)
            if inc:
                ins.then_inc(self.sem, 1)

    def finish(self, eng, seen, outer):
        self.emit(eng, seen)
        if self.n:
            eng.wait_ge(self.sem, self.n)
        eng.nop().then_inc(outer, 1)


def build(nc, x_d, ws_d, par_d, con_d, dis_d, scn_d, rel_d, ow_d, moe_d, pos_d, out_d, stop=99):
    fp32, i32, u32, f32r = mybir.dt.float32, mybir.dt.int32, mybir.dt.uint32, mybir.dt.float32r
    ALU, ACT, AX = mybir.AluOpType, mybir.ActivationFunctionType, mybir.AxisListType
    MUL, ADD, SUB, MAXO = ALU.mult, ALU.add, ALU.subtract, ALU.max
    ctx = ExitStack()
    with ctx:
        def sb(name, shape, dt=fp32, c=ctx):
            return c.enter_context(nc.sbuf_tensor(name, shape, dt))

        def sem(name):
            return ctx.enter_context(nc.semaphore(name))

        pc, np_ = columns(params())
        cc, nc_ = columns(consts())
        ring = sb("ring", [128, RING, BW])
        par_t, con_t, pos_t = sb("par", [128, np_]), sb("con", [128, nc_]), sb("pos", [128, 8], i32)
        flag_t = sb("flag", [128, 8], i32)[:, 0:1]
        xt = sb("xt", [128, 8 * T0])
        AB = 8 * T0
        XW = AB + 112
        NL = 2 * SLOTS * BW + 4 * XW
        NA = (208 * 1024 - 512 - 4 * (RING * BW + np_ + nc_ + 16 + AB + NL)) // 4 // 16 * 16

        with ExitStack() as c:
            sh = [sb(f"sh{i}", [128, BW], f32r, c) for i in range(SLOTS)]
            sl = [sb(f"sl{i}", [128, BW], f32r, c) for i in range(SLOTS)]
            xh = [sb(f"xh{i}", [128, XW], f32r, c) for i in range(2)]
            xl = [sb(f"xl{i}", [128, XW], f32r, c) for i in range(2)]
        scan_t = sb("scan_t", [128, NL])
        hid, arena_of = {}, {}
        for key, n in (("ffn", 22 * T0), ("moe", 3 * T1), ("conv0", 22 * T1), ("conv1", 22 * T1)):
            with ExitStack() as c:
                hid[key] = [sb(f"{key}_{x}", [128, n], f32r, c) for x in "hl"]
                if key == "moe":
                    sh.append(sb("sh2", [128, BW], f32r, c))
                    sl.append(sb("sl2", [128, BW], f32r, c))
                arena_of[key] = sb(f"arena_{key}", [128, NA - 2 * n - 2 * BW * (key == "moe")], fp32, c)
        arena = sb("arena", [128, NA])
        ps_t = ctx.enter_context(nc.psum_tensor("ps", [128, 8, 512], fp32))
        PS = ps_t[:, :, :]

        def par(n):
            return par_t[:, pc[n][0]:pc[n][0] + pc[n][1]]

        def con(n):
            return con_t[:, cc[n][0]:cc[n][0] + cc[n][1]]

        def cut(t, off, *shape):
            n = int(np.prod(shape))
            assert off + n <= t.shape[1], (off, shape, t.shape)
            v = t[:, off:off + n]
            if len(shape) == 2:
                v = v.rearrange("p (a b) -> p a b", a=shape[0])
            if len(shape) == 3:
                v = v.rearrange("p (a b c) -> p a b c", a=shape[0], b=shape[1])
            return v

        def at(off, *shape):
            return cut(arena, off, *shape)

        def bc(v, *shape):
            return v.broadcast_to([v.shape[0], *shape])

        PE, DV, AC, PO, SP = (Eng(sem(n)) for n in ("s_pe", "s_dve", "s_act", "s_pool", "s_sp"))
        s_in = {n: sem(f"s_in_{n}") for n in ("x", "par", "con", "pos", "dis", "scn", "rel", "ow", "moe")}
        s_w = [sem(f"s_w{i}") for i in range(RING)]
        s_out, s_fd, s_fp = sem("s_out"), sem("s_fd"), sem("s_fp")
        for n, E in (("pe", PE), ("dve", DV), ("act", AC), ("pool", PO)):
            E.sems = [sem(f"s_{n}_way{i}") for i in range(2)]
        IN_X, IN_PAR, IN_CON, IN_POS, IN_DIS, IN_SCN, IN_REL, IN_OW, IN_MOE = (
            (s_in[n], 16) for n in ("x", "par", "con", "pos", "dis", "scn", "rel", "ow", "moe"))

        def done(pool=True):
            return [t for t in (PE.last(), DV.last(), AC.last(), pool and PO.last()) if t]

        def load(E, dst, src, s, *waits):
            E(lambda e: e.dma_start(dst, src).then_inc(s, 16), *waits, inc=False, chain=False)

        def tt(E, out, a, b, op, *w, chain=True):
            return E(lambda e: e.tensor_tensor(out, a, b, op), *w, chain=chain)

        def ts(E, out, a, s1, s2, o0, o1, *w, chain=True):
            return E(lambda e: e.tensor_scalar(out, a, s1, s2, o0, o1) if o1 is not None
                     else e.tensor_scalar(out, a, s1, None, o0), *w, chain=chain)

        def stt(E, out, a, s, b, o0, o1, *w, chain=True):
            return E(lambda e: e.scalar_tensor_tensor(out=out, in0=a, scalar=s, in1=b, op0=o0, op1=o1), *w, chain=chain)

        def act(out, a, f, *w, bias=0.0, scale=1.0, accum=None, chain=True):
            return AC(lambda e: e.activation(out, a, f, bias=bias, scale=scale, accum_out=accum), *w, chain=chain)

        def cp(E, out, a, *w, chain=True):
            if E is AC:
                return act(out, a, ACT.Copy, *w, chain=chain)
            return E(lambda e: e.tensor_copy(out, a), *w, chain=chain)

        def mset(E, out, v, *w):
            return E(lambda e: e.memset(out, v), *w)

        def red(out, a, op, *w):
            return DV(lambda e: e.tensor_reduce(out, a, AX.X, op), *w)

        def rec(out, a, *w):
            return DV(lambda e: e.reciprocal(out, a), *w)

        def rsq(out, a, eps, *w):
            t = ts(DV, out, a, eps, None, ADD, None, *w)
            t = act(out, out, ACT.Sqrt, t)
            return rec(out, out, t)

        def f32(v):
            return v.bitcast(fp32)

        blocks = stream_blocks()
        flat = [(t, bi, x) for bi, (b, _) in enumerate(blocks) for t, x in b]
        state = {"tile": 0, "freed": {}, "split": {}, "read": {}, "next": 0, "piece": 0, "wait": [], "low": None, "ahead": True, "gate": []}
        slot_of, held = {}, [None] * 3

        def split_piece():
            bi, p = state["next"], state["piece"]
            w = blocks[bi][1]
            if p == 0:
                s = min(range(SLOTS), key=lambda i: -1 if held[i] is None else held[i])
                state["wait"] = [] if held[s] is None else [state["read"][held[s]]]
                held[s], slot_of[bi] = bi, s
            s = slot_of[bi]
            c = slice(PIECE * p, min(PIECE * p + PIECE, w))
            wait = [*state["wait"], *state["gate"]]
            src = ring[:, bi % RING, c]
            t = cp(AC, sh[s][:, c], src, (s_w[bi % RING], 16 * (bi // RING + 1)), *wait)
            low_part()
            state["low"] = (bi, p, sl[s][:, c], src, f32(sh[s][:, c]), t, wait)
            state["piece"] += 1
            if c.stop == w:
                state["next"], state["piece"] = bi + 1, 0

        def low_part():
            if state["low"]:
                bi, p, dst, src, high, t, wait = state["low"]
                t = tt(PO if p == 2 else DV, dst, src, high, SUB, t, *wait)
                state["split"].setdefault(bi, []).append(t)
                state["freed"].setdefault(bi, []).append(t)
                state["low"] = None

        def split_to(bi, end):
            while state["next"] < bi or state["next"] == bi and PIECE * state["piece"] < end:
                split_piece()

        def weight(name, raw=False):
            t, bi, x = flat[state["tile"]]
            assert t[0] == name, (t[0], name)
            state["tile"] += 1
            n = state["tile"]
            w = t[2] * t[5]
            closes = n == len(flat) or flat[n][1] != bi
            if raw:
                state["next"] = bi + 1
                v = ring[:, bi % RING, x:x + w].rearrange("p (k c) -> p k c", k=t[2])
                return v, None, (s_w[bi % RING], 16 * (bi // RING + 1)), bi, t
            split_to(bi, x + w)
            if len(state["split"].get(bi, [])) * PIECE < x + w:
                low_part()
            b2 = bi + 1
            if state["ahead"] and b2 < len(blocks) and blocks[b2][0][0][0][0] not in ALONE:
                if closes:
                    split_to(b2, blocks[b2][1])
                    low_part()
                elif state["next"] == b2:
                    split_to(b2, min(PIECE * (blocks[bi][0].index((t, x)) + 1), blocks[b2][1]))
            h, l = (v[slot_of[bi]][:, x:x + w].rearrange("p (k c) -> p k c", k=t[2]) for v in (sh, sl))
            return h, l, state["split"][bi][x // PIECE:-(-(x + w) // PIECE)], (bi if closes else None), t

        def split_ahead():
            split_to(state["next"], blocks[state["next"]][1])
            low_part()

        def used(bi, tok):
            if bi is not None:
                state["read"][bi] = tok

        xfree = [[], []]

        def xset(s, n, T):
            h, l = (v[s][:, 0:n * T].rearrange("p (n t) -> p n t", n=n) for v in (xh, xl))
            return {"h": h, "l": l, "tok": {}, "s": s}

        def split_x(x, src, k0, k1, *waits):
            w = list(waits) + xfree[x["s"]]
            t = cp(AC, x["h"][:, k0:k1, :], src, *w)
            t = tt(DV, x["l"][:, k0:k1, :], src, f32(x["h"][:, k0:k1, :]), SUB, t, *w)
            for k in range(k0, k1):
                x["tok"][k] = t
            return t

        def split_all(s, src, n, T, *waits):
            x = xset(s, n, T)
            for k in range(0, n, 2):
                split_x(x, src[:, k:min(k + 2, n), :], k, min(k + 2, n), *waits)
            return x

        free = [[] for _ in range(8)]
        turn = [0]

        def bank(n=1):
            b = turn[0]
            if b % n or b + n > 8:
                b = -(-b // n) * n % 8
            turn[0] = (b + n) % 8
            return b, [t for i in range(n) for t in free[b + i]]

        def release(b, *toks, n=1):
            for i in range(n):
                free[b + i] = list(toks)

        def mm(out, lhsT, rhs, start, stop, *waits, inc=False):
            return PE(lambda e: e.matmul(out, lhsT, rhs, start=start, stop=stop), *waits, inc=inc, chain=False)

        def mm3(out, ah, al, bh, bl, start, stop, *waits, inc=False):
            mm(out, ah, bh, start, False, *waits)
            mm(out, ah, bl, False, False)
            return mm(out, al, bh, False, stop, inc=inc)

        def tr(out, in_, *waits, inc=False):
            k = in_.shape[0]
            return PE(lambda e: e.transpose(out, in_, con("ident")[0:k, 0:k]), *waits, IN_CON, inc=inc, chain=False)

        def linear(name, n, x, T, evac, *waits, rows=128):
            toks = []
            for e in range(n):
                wh, wl, wt, closes, t = weight(name)
                nk = t[2]
                b, fr = bank()
                for k in range(nk):
                    w = [x["tok"][k]] if e == 0 else []
                    tok = mm3(PS[:, b, 0:T], wh[0:rows, k, :], wl[0:rows, k, :], x["h"][0:rows, k, :], x["l"][0:rows, k, :],
                              k == 0, k == nk - 1, *(w + (fr + wt + list(waits) if k == 0 else [])), inc=k == nk - 1)
                used(closes, tok)
                tk = evac(e, PS[0:t[4], b, 0:T], tok)
                release(b, tk)
                toks.append(tk)
            if x["s"] is not None:
                xfree[x["s"]] = [tok]
            return toks

        def linear_t(name, n, x, spans, evac, *waits):
            out_t = []
            T = x["h"].shape[2]
            hf, lf = (v[x["s"]] for v in (xh, xl))
            for i in range(n):
                wh, wl, wt, closes, t = weight(name)
                nk, cw = t[2], t[4]
                for j, (t0, tn) in enumerate(spans):
                    b, fr = bank()
                    for k in range(nk):
                        c = slice(x.get("at", 0) + k * T + t0, x.get("at", 0) + k * T + t0 + 128)
                        w = [x["tok"][k]] if i + j == 0 else []
                        tok = mm3(PS[:, b, 0:cw], hf[:, c], lf[:, c], wh[:, k, :], wl[:, k, :], k == 0, k == nk - 1,
                                  *(w + (fr + wt + list(waits) if k == 0 else [])), inc=k == nk - 1)
                    tk = evac(i, j, PS[0:tn, b, 0:cw], tok)
                    release(b, tk)
                    out_t.append(tk)
                used(closes, tok)
            xfree[x["s"]] = [tok]
            return out_t

        def colsum(mat, src, n, T, *waits):
            b, fr = bank()
            for k in range(n):
                tok = mm(PS[:, b, 0:T], con(mat), src[:, k, :], k == 0, k == n - 1,
                         *(fr + [IN_CON] + list(waits) if k == 0 else []), inc=k == n - 1)
            return b, tok

        def layer_norm(src, dst, tmp, small, T, g, bb, s, *waits):
            b, tok = colsum("o1024", src, 8, T, *waits)
            bv, fr = bank()
            for k in range(8):
                t = tt(DV, src[:, k, :], src[:, k, :], PS[:, b, 0:T], SUB, tok)
                t1 = act(tmp[:, k, :], src[:, k, :], ACT.Square, t, *waits)
                tv = mm(PS[:, bv, 0:T], con("o1024"), tmp[:, k, :], k == 0, k == 7, t1, *fr, inc=k == 7)
            release(b, t)
            t = rsq(small, PS[:, bv, 0:T], 1e-5, tv)
            release(bv, t)
            x = xset(s, 8, T) if s is not None else None
            for k in range(8):
                t = stt(DV, src[:, k, :], src[:, k, :], par(g)[:, k:k + 1], small, MUL, MUL, IN_PAR)
                o = act(dst[:, k, :], src[:, k, :], ACT.Identity, t, *waits, bias=par(bb)[:, k:k + 1])
                if x and k % 2:
                    split_x(x, dst[:, k - 1:k + 1, :], k - 1, k + 1)
            return x if x else o

        def rms_norm(src, dst, tmp, small, n, T, g, mat, s, *waits, k0=0, x=None):
            bv, fr = bank()
            for k in range(n):
                t1 = act(tmp[:, k, :], src[:, k, :], ACT.Square, *waits)
                tv = mm(PS[:, bv, 0:T], con(mat), tmp[:, k, :], k == 0, k == n - 1, t1, IN_CON, *fr, inc=k == n - 1)
            t = rsq(small, PS[:, bv, 0:T], 1e-6, tv)
            release(bv, t)
            x = x or xset(s, n, T)
            for k in range(n):
                t = stt(DV, dst[:, k, :], src[:, k, :], par(g)[:, k:k + 1], small, MUL, MUL, IN_PAR, *waits)
                if k % 2 or k == n - 1:
                    a = k - k % 2
                    split_x(x, dst[:, a:k + 1, :], k0 + a, k0 + k + 1, t)
            return x

        def staged(n, *stages):
            for step in range(n + len(stages) - 1):
                for j in range(len(stages) - 1, -1, -1):
                    if 0 <= step - j < n:
                        stages[j](step - j)

        phases = []
        X = cut(xt, 0, 8, T0)
        QT = [(0, 128), (128, 128), (256, 16)]
        THIRDS = [0, 384, 768]
        carry = {}

        def attention():
            Q, K, O = (at(i * AB, 8, T0) for i in range(3))
            VT = at(3 * AB, 3, 1024)
            o = 3 * AB + 3072
            negd = at(o, 3, T0)
            o += 3 * T0
            load(PO, negd.rearrange("p a t -> p (a t)"), dis_d, s_in["dis"])
            for s in range(2):
                for v in (xh, xl):
                    padded = mset(DV, f32(v[s][:, AB:XW]), 0.0)
            x = split_all(0, X, 8, T0, IN_X)
            linear("attn_qk", 16, x, T0, lambda e, ps, tok: cp(AC if e % 2 else DV, (Q if e < 8 else K)[:, e % 8, :], ps, tok))
            linear_t("attn_v", 3, x, QT, lambda i, j, ps, tok: cp(
                AC if j else DV, VT[0:ps.shape[0], j, THIRDS[i]:THIRDS[i] + ps.shape[1]], ps, tok), padded)
            lam = at(o, 8)
            pr = at(o + 8, 64)
            o += 72
            for i in (1, 2):
                tt(DV, pr, par(f"lam_q{i}"), par(f"lam_k{i}"), MUL, IN_PAR)
                red(lam[:, i - 1:i], pr, ADD)
            t = act(lam[:, 2:4], lam[:, 0:2], ACT.Exp, DV.last())
            tt(DV, lam[:, 4:5], lam[:, 3:4], lam[:, 2:3], SUB, t)
            ts(DV, lam[:, 5:6], lam[:, 4:5], -LAM_INIT, None, ADD, None)
            nlam = lam[:, 5:6]
            NB = 3
            st = [at(o + i * 2 * T0, 2, T0) for i in range(NB)]
            o += NB * 2 * T0
            ex = [at(o + i * 2 * T0, 2, T0) for i in range(NB)]
            o += NB * 2 * T0
            sm = [at(o + i * 16, 16) for i in range(NB)]
            o += NB * 16
            aT = [at(o + i * 3 * T0, 3, T0) for i in range(2)]
            o += 6 * T0
            small = at(o, T0)
            barrier = done()
            scale = 64.0 ** -0.5
            ready, got, freeS, freeT, tex, tT = {}, {}, [[] for _ in range(NB)], [[], []], {}, {}

            def scores(u):
                h, qi = u // 3, u % 3
                q0, qn = QT[qi]
                b, fr = bank(2)
                for c in range(2):
                    tok = mm(PS[0:qn, b + c, 0:T0], Q[64 * c:64 * c + 64, h, q0:q0 + qn], K[64 * c:64 * c + 64, h, :],
                             True, True, *(fr + barrier), inc=c == 1)
                got[u] = b, tok

            def soften(u):
                h, qi = u // 3, u % 3
                qn = QT[qi][1]
                i = u % NB
                b, tok = got[u]
                slope = 2.0 ** -(h + 1)
                S, E, m = st[i][0:qn], ex[i][0:qn], sm[i][0:qn]
                t = stt(DV, S, bc(negd[0:qn, None, qi, :], 2, T0), slope / scale, PS[0:qn, b:b + 2, 0:T0],
                        MUL, ADD, tok, IN_DIS, *freeS[i])
                release(b, t, n=2)
                red(m[:, 0:2], S, MAXO)
                t = ts(DV, m[:, 2:4], m[:, 0:2], -scale, None, MUL, None)
                for c in range(2):
                    t = act(E[:, c, :], S[:, c, :], ACT.Exp, t, bias=m[:, 2 + c:3 + c], scale=scale, accum=m[:, 4 + c:5 + c])
                tex[u] = t

            def weigh(u):
                qn = QT[u % 3][1]
                i = u % NB
                S, E, m = st[i][0:qn], ex[i][0:qn], sm[i][0:qn]
                rec(m[:, 6:8], m[:, 4:6], tex[u])
                tt(DV, m[:, 8:9], m[:, 7:8], nlam[0:qn], MUL)
                ts(DV, S[:, 0, :], E[:, 0, :], m[:, 6:7], None, MUL, None)
                ready[u] = stt(DV, S[:, 1, :], E[:, 1, :], m[:, 8:9], S[:, 0, :], MUL, ADD)

            def rest(u):
                h, qi = u // 3, u % 3
                q0, qn = QT[qi]
                i = u % NB
                b, fr = bank()
                pt = PS[:, b, 0:384].rearrange("p (k q) -> p k q", k=3)
                for kt, (k0, kn) in enumerate(QT):
                    tok = tr(pt[0:kn, kt, 0:qn], st[i][0:qn, 1, k0:k0 + kn], ready[u], *fr, inc=kt == 2)
                freeS[i] = [tok]
                w = freeT[h % 2] if qi == 0 else []
                cp(AC, aT[h % 2][:, 0:2, q0:q0 + qn], pt[:, 0:2, 0:qn], tok, *w)
                t = cp(AC, aT[h % 2][0:16, 2, q0:q0 + qn], pt[0:16, 2, 0:qn])
                release(b, t)
                tT[h] = t

            def values(h):
                b, fr = bank()
                for kt, (k0, kn) in enumerate(QT):
                    tok = mm(PS[:, b, 0:T0], VT[0:kn, kt, 128 * h:128 * h + 128], aT[h % 2][0:kn, kt, :], kt == 0, kt == 2,
                             tT[h], *fr, inc=kt == 2)
                freeT[h % 2] = [tok]
                release(b, cp(AC, O[:, h, :], PS[:, b, 0:T0], tok))

            scores(0)
            for u in range(26):
                if u < 23:
                    scores(u + 1)
                if u > 1:
                    rest(u - 2)
                if u < 24:
                    soften(u)
                if 1 <= u < 25:
                    weigh(u - 1)
                if u > 1 and (u - 2) % 3 == 2:
                    values((u - 2) // 3)
            ts(DV, lam[:, 6:7], par("subln"), 1.0 - LAM_INIT, None, MUL, None)
            x = xset(1, 8, T0)
            bar = done()
            sum_of, at_ = {}, {}

            def squares(h):
                t = act(Q[:, h, :], O[:, h, :], ACT.Square, *bar)
                sum_of[h] = colsum("o128", Q[:, h:h + 1, :], 1, T0, t)

            def roots(h):
                b, tok = sum_of[h]
                t = ts(DV, Q[:, h, :], PS[:, b, 0:T0], 1e-5, None, ADD, None, tok)
                release(b, t)
                at_[h] = act(Q[:, h, :], Q[:, h, :], ACT.Sqrt, t)

            def scaled(h):
                t = rec(Q[:, h, :], Q[:, h, :], at_[h])
                at_[h] = stt(DV, O[:, h, :], O[:, h, :], lam[:, 6:7], Q[:, h, :], MUL, MUL)

            staged(8, squares, roots, scaled, lambda h: split_x(x, O[:, h:h + 1, :], h, h + 1, at_[h]))
            linear("attn_o", 8, x, T0, lambda e, ps, tok: stt(DV, K[:, e, :], X[:, e, :], ALPHA, ps, MUL, ADD, tok))
            carry["x"] = layer_norm(K, X, O, small, T0, "ln_g00", "ln_b00", 0, *done())

        phases.append(attention)

        def hidden(key, T):
            h, l = (v[:, :].rearrange("p (n t) -> p n t", t=T) for v in hid[key])
            return {"h": h, "l": l, "tok": {}, "s": None}

        def split_hidden(x, f, src, tok, *waits):
            t = cp(AC, x["h"][:, f, :], src, tok, *waits)
            t = tt(PO, x["l"][:, f, :], src, f32(x["h"][:, f, :]), SUB, t, *waits)
            x["tok"][f] = t
            return t

        def ffn():
            ar = arena_of["ffn"]
            R, tmp = cut(ar, 0, 8, T0), cut(ar, AB, 8, T0)
            small = cut(ar, 2 * AB, T0)
            o = 2 * AB + T0
            sg = [cut(ar, o + 2 * T0 * i, 2, T0) for i in range(2)]
            H = hidden("ffn", T0)
            bar = done()
            hold = {}

            def evac(e, ps, tok):
                f = e // 2
                s = sg[f % 2]
                if e % 2 == 0:
                    t = act(s[:, 0, :], ps, ACT.Sigmoid, tok, hold.get(f - 2), *bar)
                    return tt(DV, s[:, 1, :], ps, s[:, 0, :], MUL, t, hold.get(f - 2))
                t = tt(DV, s[:, 1, :], s[:, 1, :], ps, MUL, tok)
                hold[f] = split_hidden(H, f, s[:, 1, :], t, *bar)
                return t

            linear("ffn_gu", 44, carry["x"], T0, evac)
            linear("ffn_d", 8, H, T0, lambda e, ps, tok: stt(DV, R[:, e, :], X[:, e, :], ALPHA, ps, MUL, ADD, tok, *bar))
            layer_norm(R, X, tmp, small, T0, "ln_g01", "ln_b01", None, *done())

        phases.append(ffn)

        Rr, Kr, KK, Yb = (at(i * AB, 8, T0) for i in range(4))
        VW = 1024 + 32
        VC = at(4 * AB, 3, VW)
        hid_o = 4 * AB + 3 * VW
        HW, HA, HG, HG2 = (at(hid_o + i * T0, T0) for i in range(4))
        tail_o = hid_o + 4 * T0
        CH = [(0, C), (C, C), (2 * C, T0 - 2 * C)]

        def rwkv_project():
            Vr, DP = KK, Yb
            DN = at(tail_o, 8, T0)
            XS = at(tail_o + AB, 4, T0)
            bar = done()
            ts(DV, DP[:, :, 0:1], X[:, :, 0:1], -1.0, None, MUL, None, *bar)
            tt(DV, DP[:, :, 1:T0], X[:, :, 0:T0 - 1], X[:, :, 1:T0], SUB)
            ts(PO, DN[:, :, T0 - 1:T0], X[:, :, T0 - 1:T0], -1.0, None, MUL, None, *bar)
            tn = tt(PO, DN[:, :, 0:T0 - 1], X[:, :, 1:T0], X[:, :, 0:T0 - 1], SUB)

            def mix(m):
                x = xset(m % 2, 8, T0)
                got = {}

                def mixed(k):
                    v = XS[:, k % 4, :]
                    stt(DV, v, DP[:, k, :], par(f"mu0{m}")[:, k:k + 1], X[:, k, :], MUL, ADD, *bar, hold.get(k % 4))
                    got[k] = stt(DV, v, DN[:, k, :], par(f"mu1{m}")[:, k:k + 1], v, MUL, ADD, tn)

                def parts(k):
                    split_x(x, XS[:, k % 4, None, :], k, k + 1, got[k])
                    hold[k % 4] = AC.last()

                def step(k):
                    if 0 < k:
                        parts(k - 1)
                    if k < 8:
                        mixed(k)

                return x, step

            hold = {}
            xs = []
            for m in range(2):
                x, step = mix(m)
                xs.append(x)
                for k in range(9):
                    step(k)
            step = None
            for m, dst in enumerate((Rr, Kr, Vr)):
                if m:
                    x, step = mix(m + 1)
                    xs.append(x)

                def evac(e, ps, tok):
                    t = cp(AC, dst[:, e, :], ps, tok, *bar)
                    if step:
                        step(e)
                    return t

                linear(f"rkv{m}", 8, xs[m], T0, evac)
                if step:
                    step(8)
            for m in (4, 5):
                x, step = mix(m)
                xs.append(x)
                if m == 5:
                    linear("lw", 1, xs[3], T0, lambda e, ps, tok: act(HW, ps, ACT.Tanh, tok, *bar))
                for k in range(9):
                    step(k)
            linear("la", 1, xs[4], T0, lambda e, ps, tok: cp(AC, HA, ps, tok))
            state["ahead"] = False
            linear("lg", 2, xs[5], T0, lambda e, ps, tok: act((HG, HG2[0:32])[e], ps, ACT.Sigmoid, tok))
            bar = done()
            mset(DV, VC[:, :, 1024:VW], 0.0, *bar)
            tz = mset(DV, VC[64:C, 2, 0:1024], 0.0)
            for c, (c0, cn) in enumerate(CH):
                for hf in range(2):
                    b, fr = bank()
                    for d in range(4):
                        tok = tr(PS[0:cn, b, 128 * d:128 * d + 128], Vr[:, 4 * hf + d, c0:c0 + cn], *(fr + bar), inc=d == 3)
                    release(b, cp(AC, VC[0:cn, c, 512 * hf:512 * hf + 512], PS[0:cn, b, :], tok, tz))
            bar = done()
            nrm = at(tail_o, 8, T0)
            sum_of, root = {}, {}

            def squares(k):
                t = ts(DV, KK[:, k, :], Kr[:, k, :], par("k_k")[:, k:k + 1], None, MUL, None, *bar)
                t = act(nrm[:, k, :], KK[:, k, :], ACT.Square, t, *bar)
                sum_of[k] = colsum("blk", nrm[:, k:k + 1, :], 1, T0, t)

            def roots(k):
                b, tok = sum_of[k]
                root[k] = act(nrm[:, k, :], PS[:, b, 0:T0], ACT.Sqrt, tok)
                release(b, root[k])

            def scaled(k):
                ts(DV, nrm[:, k, :], nrm[:, k, :], 1e-12, None, MAXO, None, root[k])
                rec(nrm[:, k, :], nrm[:, k, :])
                tt(DV, KK[:, k, :], KK[:, k, :], nrm[:, k, :], MUL)

            staged(8, squares, roots, scaled)

        phases.append(rwkv_project)

        def rwkv_scan():
            sc, ns = columns(scan_consts())
            so = tail_o
            scn = at(so, ns)
            so += ns

            def sn(name):
                return scn[:, sc[name][0]:sc[name][0] + sc[name][1]]

            bar = done()
            load(PO, scn, scn_d, s_in["scn"], *bar)
            W = 8 * C
            per = []
            zo = 0
            for n in range(2):
                d = {}
                d["AR"] = cut(scan_t, zo, 2, 4, TP)
                d["B"], d["K"] = cut(scan_t, zo + 8 * TP, 4, TP), cut(scan_t, zo + 12 * TP, 4, TP)
                zo += 16 * TP
                for i, name in enumerate(("U", "X", "Y", "T", "GKA", "GKR", "GBR")):
                    d[name] = cut(scan_t, zo + i * W, 8, C)
                d["t1"], d["t2"] = cut(scan_t, zo, 4, T0), cut(scan_t, zo + 4 * T0, 4, T0)
                d["NS"], d["Z"] = cut(scan_t, zo, 544), cut(scan_t, zo + 3 * W, 544)
                d["Kt"] = cut(scan_t, zo + 2 * W, 4, 128)
                zo += 7 * W
                d["Bt"] = cut(scan_t, zo, 4, 128)
                zo += 512
                d["S"] = at(so, 288)
                so += 288
                d["PC"] = at(so, 4, 3)
                so += 12
                per.append(d)
            mset(DV, Yb, 0.0, *bar)
            for d in per:
                mset(DV, d["AR"].rearrange("p a b t -> p (a b) t")[:, :, T0:TP], 0.0)
                mset(DV, d["B"][:, :, T0:TP], 0.0)
                mset(DV, d["K"][:, :, T0:TP], 0.0)

            def prepare(n, hf):
                E = DV if n == 0 else PO
                d = per[n]
                t1, t2, B, K = d["t1"], d["t2"], d["B"][:, :, 0:T0], d["K"][:, :, 0:T0]
                A, R = d["AR"][:, 0, :, 0:T0], d["AR"][:, 1, :, 0:T0]
                d0 = 4 * hf
                bar = done()
                for i in range(4):
                    for w, src, dst, bias in (("w2", HW, t1, f"w0{n}"), ("a2", HA, t2, f"a0{n}")):
                        b, fr = bank()
                        tok = mm(PS[:, b, 0:T0], sn(w)[64 * n:64 * n + 64, 128 * (d0 + i):128 * (d0 + i) + 128],
                                 src[64 * n:64 * n + 64, :], True, True, *(fr + bar + [IN_SCN]), inc=True)
                        t = t0 = act(dst[:, i, :], PS[:, b, 0:T0], ACT.Sigmoid, tok, *bar, bias=par(bias)[:, d0 + i:d0 + i + 1])
                        release(b, t)
                kk, r, k = (v[:, d0:d0 + 4, :] for v in (KK, Rr, Kr))
                tb = tt(E, B, kk, t2, MUL, t, *bar)
                for i in range(4):
                    ts(E, t2[:, i, :], t2[:, i, :], -1.0, par("k_a")[:, d0 + i:d0 + i + 1], ADD, MUL)
                if E is DV:
                    tk = stt(DV, K, t2, 1.0, k, ADD, MUL)
                else:
                    ts(E, t2, t2, 1.0, None, ADD, None)
                    tk = tt(E, K, t2, k, MUL)
                for i in range(4):
                    cum, ld = A[:, i, :], t1[:, i, :]
                    if n == 1:
                        cum, ld = cum[:, ::-1], ld[:, ::-1]
                    t = DV(lambda e, cum=cum, ld=ld: e.tensor_tensor_scan(cum, sn(f"begin{n}"), ld, 0.0, MUL, ADD), t0, *bar)
                lam = -float(np.exp(-0.5))
                t3 = act(t2, A, ACT.Exp, t, tk, scale=lam)
                ta = tt(DV, t1, A, t1, SUB)
                tt(DV, R, r, t2, MUL, t3)
                for c, (c0, cn) in enumerate(CH):
                    last = c0 + cn - 1 if n == 0 else c0
                    t = cp(DV, d["PC"][:, :, c:c + 1], t2[:, :, last:last + 1])
                t4 = act(t1, t1, ACT.Exp, ta, scale=lam)
                t3 = act(t2, A, ACT.Exp, t, scale=-lam)
                tt(DV, A, kk, t1, MUL, t3, t4)
                tt(DV, B, B, t2, MUL, tb)
                tt(DV, K, K, t2, MUL, tk)
                mset(DV, d["S"], 0.0)

            def pairs(b, cols=C):
                return PS[0:C, b:b + 2, 0:4 * cols].rearrange("s p (i t) -> s p i t", i=4)

            def by4(v):
                return v.rearrange("s (p i) t -> s p i t", p=2)

            def chunks(n, hf):
                d = per[n]
                AR, B, K, U, X_, Y, T_, S, PC = (d[k] for k in ("AR", "B", "K", "U", "X", "Y", "T", "S", "PC"))
                strict, nstrict, incl = ("up", "nup", "upi") if n == 0 else ("dn", "ndn", "dni")
                lx = "lu" if n == 0 else "ld"
                begin = done()
                for ci, c in enumerate(range(3) if n == 0 else range(2, -1, -1)):
                    final = ci == 2
                    cn = CH[c][1]
                    cs = slice(C * c, C * c + C)
                    prev = [PE.last(), DV.last(), AC.last()] if ci else begin
                    for lh, m0, n0, m1, n1 in ((B, nstrict, "U", incl, "GBR"), (K, strict, "GKA", incl, "GKR")):
                        for p in range(2):
                            rows = slice(64 * p, 64 * p + 64)
                            b, fr = bank(2)
                            for i in range(4):
                                out = PS[0:C, b + i // 2, 2 * C * (i % 2):2 * C * (i % 2) + 2 * C].rearrange("s (r t) -> s r t", r=2)
                                tok = mm(out, lh[rows, i, cs], AR[rows, :, i, cs], True, True, *(fr + prev), inc=i == 3)
                            v = PS[0:C, b:b + 2, 0:4 * C].rearrange("s q (i r t) -> s q i r t", i=2, r=2)
                            for r, (m, name) in enumerate(((m0, n0), (m1, n1))):
                                dst = d[name][0:C, 4 * p:4 * p + 4, :].rearrange("s (q i) t -> s q i t", q=2)
                                tg = tt(DV, dst, v[:, :, :, r, :], sn(m)[0:C, None, None, :].broadcast_to([C, 2, 2, C]), MUL, tok, IN_SCN, *prev)
                            release(b, tg, n=2)
                        yield
                    idb = con("ident")[0:C, None, 0:C].broadcast_to([C, 8, C])
                    cp(DV, X_[0:C], idb)
                    for lv in range(7):
                        msk = sn(f"{lx}{lv}")[0:C].bitcast(u32)
                        if lv == 0:
                            t = DV(lambda e, msk=msk: e.copy_predicated(X_[0:C], msk[:, None, :].broadcast_to([C, 8, C]), U[0:C]))
                        else:
                            b, fr = bank(2)
                            for h in range(8):
                                tok = mm(PS[0:C, b + h // 4, C * (h % 4):C * (h % 4) + C], U[0:C, h, :], Y[0:C, h, :], True, True,
                                         *(fr + [ty] if h == 0 else []), inc=h == 7)
                            tT = cp(AC, by4(T_[0:C]), pairs(b), tok)
                            release(b, tT, n=2)
                            yield
                            b, fr = bank(2)
                            for h in range(8):
                                tok = mm(PS[0:C, b + h // 4, C * (h % 4):C * (h % 4) + C], T_[0:C, h, :], X_[0:C, h, :], True, True,
                                         *(fr + [tT] if h == 0 else []), inc=h == 7)
                            t = DV(lambda e, b=b, msk=msk: e.copy_predicated(
                                by4(X_[0:C]), msk[:, None, None, :].broadcast_to([C, 2, 4, C]), pairs(b)), tok)
                            release(b, t, n=2)
                            yield
                        if lv < 6:
                            b, fr = bank(2)
                            for h in range(8):
                                tok = tr(PS[0:C, b + h // 4, C * (h % 4):C * (h % 4) + C], X_[0:C, h, :], *(fr + [t] if h == 0 else []), inc=h == 7)
                            ty = cp(AC, by4(Y[0:C]), pairs(b), tok)
                            release(b, ty, n=2)
                            yield
                    tX = t
                    if not final:
                        for src, dst in ((K, d["Kt"]), (B, d["Bt"])):
                            b, fr = bank()
                            for i in range(4):
                                tok = tr(PS[0:C, b, 128 * i:128 * i + 128], src[:, i, cs], *fr, inc=i == 3)
                            tkb = cp(AC, dst[0:C], PS[0:C, b, :].rearrange("s (i k) -> s i k", i=4), tok)
                            release(b, tkb)
                    tS = DV.last()
                    b, fr = bank(2)
                    for p in range(2):
                        rows = slice(64 * p, 64 * p + 64)
                        for i in range(4):
                            hh = 2 * (4 * hf + i) + p
                            out = PS[0:C, b + p, C * i:C * i + C]
                            if ci:
                                mm(out, AR[rows, 0, i, cs], S[rows, 64 * i:64 * i + C], True, False, tS, *fr)
                            tok = mm(out, d["GKA"][0:C, 4 * p + i, :], VC[0:C, c, 64 * hh:64 * hh + C], not ci, True, tS, *fr, inc=p * i == 3)
                    tz = mset(PO, d["Z"][0:C, 512:544], 0.0, tX)
                    tn = mset(PO, d["NS"][0:C, 512:544], 0.0, tX)
                    t = cp(AC, d["Z"][0:C, 0:512].rearrange("s (p i v) -> s p i v", p=2, i=4), pairs(b)[:, :, :, 0:64], tok, tX)
                    release(b, t, n=2)
                    yield
                    b, fr = bank(2)
                    for h in range(8):
                        tok = mm(PS[0:C, b + h // 4, C * (h % 4):C * (h % 4) + C], X_[0:C, h, :], d["Z"][0:C, 64 * h:64 * h + C], True, True,
                                 *(fr + [t, tz] if h == 0 else []), inc=h == 7)
                    tN = act(d["NS"][0:C, 0:512].rearrange("s (p i v) -> s p i v", p=2, i=4), pairs(b)[:, :, :, 0:64], ACT.Copy, tok, scale=-1.0)
                    release(b, tN, n=2)
                    yield
                    b, fr = bank(2)
                    for p in range(2):
                        rows = slice(64 * p, 64 * p + 64)
                        for i in range(4):
                            h, hh = 4 * p + i, 2 * (4 * hf + i) + p
                            out = PS[rows, b + p, C * i:C * i + C]
                            if ci:
                                mm(out, S[rows, 64 * i:64 * i + 64], AR[rows, 1, i, cs], True, False, tN, *fr)
                            mm(out, VC[0:C, c, 64 * hh:64 * hh + 64], d["GKR"][0:C, h, :], not ci, False, tN, *fr)
                            tok = mm(out, d["NS"][0:C, 64 * h:64 * h + 64], d["GBR"][0:C, h, :], False, True, inc=p * i == 3)
                    for p in range(2):
                        rows = slice(64 * p, 64 * p + 64)
                        y = Yb[rows, 4 * hf:4 * hf + 4, C * c:C * c + cn]
                        tY = tt(DV, y, y, PS[rows, b + p, 0:4 * C].rearrange("v (i t) -> v i t", i=4)[:, :, 0:cn], ADD, tok)
                    release(b, tY, n=2)
                    yield
                    if final:
                        continue
                    b, fr = bank()
                    for p in range(2):
                        rows = slice(64 * p, 64 * p + 64)
                        for i in range(4):
                            h, hh = 4 * p + i, 2 * (4 * hf + i) + p
                            out = PS[rows, b, C * i:C * i + C]
                            mm(out, d["Kt"][0:C, i, 64 * p:64 * p + 64], VC[0:C, c, 64 * hh:64 * hh + C], True, False, tkb, tn, *fr)
                            tok = mm(out, d["Bt"][0:C, i, 64 * p:64 * p + 64], d["NS"][0:C, 64 * h:64 * h + C], False, True, inc=p * i == 3)
                    S4 = S[:, 0:256].rearrange("k (i v) -> k i v", i=4)
                    t = tt(DV, S4, S4, PS[:, b, 0:4 * C].rearrange("k (i v) -> k i v", i=4)[:, :, 0:64], ADD, tok)
                    release(b, t)
                    tt(DV, S4, S4, bc(PC[:, :, c:c + 1], 4, 64), MUL)
                    yield

            for hf in range(2):
                for n in range(2):
                    prepare(n, hf)
                runs = [chunks(n, hf) for n in range(2)]
                while runs:
                    runs = [g for g in runs if next(g, "end") != "end"]

        phases.append(rwkv_scan)

        def rwkv_out():
            oc, nw = columns(out_weights())
            o = tail_o
            ow = at(o, nw)
            o += nw
            bar = done()
            load(PO, ow, ow_d, s_in["ow"], *bar)
            VB, VV = at(o, 3, T0), at(o + 3 * T0, 3, T0)
            SM, VA = (cut(scan_t, 2 * SLOTS * BW + i * XW, 8, T0) for i in (1, 3))

            def w(name, k):
                return ow[:, oc[name][0] + 128 * k:oc[name][0] + 128 * k + 128]

            state["ahead"], state["gate"] = True, bar
            split_ahead()
            x = xset(0, 8, T0)
            mean, var, v_, quad, root, last = {}, {}, {}, {}, {}, {}

            def first(k):
                mean[k] = colsum("blk64", Yb[:, k:k + 1, :], 1, T0, *bar)
                for n, v in ((0, VA[:, k, :]), (1, VB[:, k % 3, :])):
                    b, fr = bank()
                    tok = mm(PS[:, b, 0:T0], w("a2", k)[64 * n:64 * n + 64, :], HA[64 * n:64 * n + 64, :], True, True, IN_OW, *(fr + bar), inc=True)
                    t = act(v, PS[:, b, 0:T0], ACT.Sigmoid, tok, v_.get(("b", k - 3)), *bar, bias=par(f"a0{n}")[:, k:k + 1])
                    release(b, t)
                v_["a", k] = t
                b, fr = bank()
                for c, (c0, cn) in enumerate(CH):
                    tok = tr(PS[:, b, c0:c0 + cn], VC[0:cn, c, 128 * k:128 * k + 128], *(fr + bar), inc=c == 2)
                v_["v", k] = cp(AC, VV[:, k % 3, :], PS[:, b, 0:T0], tok, v_.get(("f", k - 3)), *bar)
                release(b, v_["v", k])

            def second(k):
                y, va = Yb[:, k, :], VA[:, k, :]
                b, tok = mean[k]
                t = tt(DV, y, y, PS[:, b, 0:T0], SUB, tok)
                release(b, t)
                t = act(SM[:, k, :], y, ACT.Square, t)
                var[k] = colsum("blk64", SM[:, k:k + 1, :], 1, T0, t)
                v_["b", k] = tt(PO, va, va, VB[:, k % 3, :], ADD, v_["a", k])
                t = ts(PO, va, va, -2.0, par("k_a")[:, k:k + 1], ADD, MUL)
                stt(DV, va, va, 2.0, Kr[:, k, :], ADD, MUL, t)
                t = stt(DV, va, va, par("r_k")[:, k:k + 1], Rr[:, k, :], MUL, MUL)
                quad[k] = colsum("blk", VA[:, k:k + 1, :], 1, T0, t)

            def third(k):
                b, tok = var[k]
                t = ts(DV, SM[:, k, :], PS[:, b, 0:T0], 64e-5, None, ADD, None, tok)
                release(b, t)
                root[k] = act(SM[:, k, :], SM[:, k, :], ACT.Sqrt, t)
                b, tok = quad[k]
                t = tt(DV, VV[:, k % 3, :], PS[:, b, 0:T0], VV[:, k % 3, :], MUL, tok, v_["v", k])
                release(b, t)

            def fourth(k):
                y = Yb[:, k, :]
                b, fr = bank()
                mm(PS[:, b, 0:T0], w("g2", k), HG, True, False, *(fr + bar))
                tok = mm(PS[:, b, 0:T0], w("g2b", k)[0:32, :], HG2[0:32, :], False, True, inc=True)
                rec(SM[:, k, :], SM[:, k, :], root[k])
                tt(DV, y, y, SM[:, k, :], MUL)
                ts(DV, y, y, par("lnx_g")[:, k:k + 1], par("lnx_b")[:, k:k + 1], MUL, ADD)
                v_["f", k] = tt(DV, y, y, VV[:, k % 3, :], ADD)
                last[k] = tt(DV, y, y, PS[:, b, 0:T0], MUL, tok)
                release(b, last[k])

            staged(8, first, second, third, fourth, lambda k: split_x(x, Yb[:, k:k + 1, :], k, k + 1, last[k], *bar))
            xfree[1] = done()
            linear("rw_o", 8, x, T0, lambda e, ps, tok: stt(DV, Rr[:, e, :], X[:, e, :], ALPHA, ps, MUL, ADD, tok))
            layer_norm(Rr, X, Kr, at(2 * AB, T0), T0, "ln_g10", "ln_b10", None, *done())

        phases.append(rwkv_out)

        T = T1
        XA = 8 * T
        Xm = X[:, :, 16:T0]
        SP2 = [(0, 128), (128, 128)]

        def moe():
            ar = arena_of["moe"]
            bar = done()
            state["gate"] = bar
            NF = FE // 128
            NU = NE * NF
            mc, nm = columns(moe_consts())
            o = 0

            def take(*shape):
                nonlocal o
                v = cut(ar, o, *shape)
                o += int(np.prod(shape))
                return v

            cons = take(nm)
            load(PO, cons, moe_d, s_in["moe"], *bar)
            iota, before, ones = (cons[:, mc[n][0]:mc[n][0] + 128] for n in ("iota", "lt", "ones"))
            YA = take(2, 1024)
            lg, gt, s8 = take(2, 8), take(2, 8), take(2, 8)
            gq, g2 = take(2, 8, 8), take(2, 8, 8)
            s1 = take(8)
            pos = take(24)
            rest_o = o
            wv, _, wt, bi, _ = weight("router", raw=True)
            for j in range(2):
                b, fr = bank()
                for k in range(8):
                    tok = mm(PS[:, b, 0:8], Xm[:, k, 128 * j:128 * j + 128], wv[:, k, :], k == 0, k == 7, wt, *(fr + bar), inc=k == 7)
                release(b, tt(DV, lg[:, j, :], PS[:, b, 0:8], par("b_router"), ADD, tok, *bar))
            state["freed"][bi] = [tok]
            red(s1[:, 0:2], lg, MAXO)
            tt(DV, lg, lg, bc(s1[:, 0:2, None], 2, 8), SUB)
            t = act(lg, lg, ACT.Exp, DV.last())
            red(s1[:, 0:2], lg, ADD, t)
            rec(s1[:, 2:4], s1[:, 0:2])
            tt(DV, lg, lg, bc(s1[:, 2:4, None], 2, 8), MUL)
            for j in range(2):
                pe_ = bc(lg[:, j, :, None], 8, 8)
                pj = bc(lg[:, j, None, :], 8, 8)
                tt(DV, gq[:, j], pj, pe_, ALU.is_gt)
                tt(DV, g2[:, j], pj, pe_, ALU.is_equal)
                tt(DV, g2[:, j], g2[:, j], con("before").rearrange("p (e j) -> p e j", e=8), MUL)
                tt(DV, gq[:, j], gq[:, j], g2[:, j], ADD)
            red(s8, gq, ADD)
            ts(DV, s8, s8, 2.0, None, ALU.is_lt, None)
            tt(DV, gt, s8, lg, MUL)
            red(s1[:, 0:2], gt, ADD)
            rec(s1[:, 2:4], s1[:, 0:2])
            t = tt(DV, gt, gt, bc(s1[:, 2:4, None], 2, 8), MUL)
            b, fr = bank()
            mm(PS[:, b, 0:8], before, s8[:, 0, :], True, True, t, IN_MOE, *fr)
            mm(PS[:, b, 8:16], ones, s8[:, 0, :], True, False)
            mm(PS[:, b, 8:16], before, s8[:, 1, :], False, True)
            mm(PS[:, b, 16:24], ones, s8[:, 0, :], True, False)
            tok = mm(PS[:, b, 16:24], ones, s8[:, 1, :], False, True, inc=True)
            t = cp(DV, pos, PS[:, b, 0:24], tok)
            release(b, t)
            red(s1[:, 4:5], pos[:, 16:24], MAXO)
            ts(DV, flag_t[:, :], s1[:, 4:5], 128.0, None, ALU.is_le, None)
            bar = done()

            SLICES = ((0, 1024), (1024, 2048), (2048, 3072))
            blk0 = state["next"]

            def raw(u):
                bi = blk0 + u
                return ring[:, bi % RING, :], (s_w[bi % RING], 16 * (bi // RING + 1))

            class Way:

                def __init__(self):
                    self.hi, self.lo, self.down = {}, {}, {}

                def high(self, u, i):
                    if u < NU:
                        src, w = raw(u)
                        a, z = SLICES[i]
                        self.hi[u, i] = cp(AC, sh[u % 3][:, a:z], src[:, a:z], w, self.down.get(u - 3), *bar)

                def low(self, u, i):
                    if u < NU:
                        src, _ = raw(u)
                        a, z = SLICES[i]
                        w = [self.hi[u, i], self.down.get(u - 3), *bar]
                        s = u % 3
                        if i == 0:
                            self.lo[u, i] = tt(DV, sl[s][:, a:z], src[:, a:z], f32(sh[s][:, a:z]), SUB, *w)
                            return
                        E, sm_ = (DV, s_fd) if i == 1 else (PO, s_fp)
                        E(lambda e: e.tensor_tensor(sl[s][:, a:z], src[:, a:z], f32(sh[s][:, a:z]), SUB).then_inc(sm_, 1), *w, inc=False)
                        self.lo[u, i] = (sm_, u + 1)

                def block(self, u):
                    for i in range(3):
                        self.high(u, i)
                        self.low(u, i)

            def gate_up(u):
                return [v[u % 3][:, 0:2048].rearrange("p (k c) -> p k c", k=8) for v in (sh, sl)]

            def down_of(u):
                return [v[u % 3][:, 2048:3072] for v in (sh, sl)]

            def few():
                nonlocal o
                o = rest_o
                XT = take(2, 1024)
                sel, gsel = [take(2, 128) for _ in range(2)], take(2, 128)
                GT = [take(2 * 128) for _ in range(2)]
                OE = take(1024)
                sg = [take(3, 128) for _ in range(2)]
                w = Way()
                xg, gt_tok = {}, {}
                misc, t3, dfree, gfree, tfree = list(bar), list(bar), list(bar), [list(bar), list(bar)], [list(bar), list(bar)]
                H = hidden("moe", T)
                hr, hs, hd, fin = {}, {}, {}, {}
                for j in range(2):
                    for q in range(2):
                        b = 2 * j + q
                        for d in range(4):
                            tok = tr(PS[:, b, 128 * d:128 * d + 128], Xm[:, 4 * q + d, 128 * j:128 * j + 128], *bar, inc=d == 3)
                        tx = cp(AC if q else DV, XT[:, j, 512 * q:512 * q + 512], PS[:, b, :], tok)
                        if b < 2:
                            gfree[b] = [tx]
                        elif b == 2:
                            tfree = [[tx], [tx]]
                        else:
                            t3 = [tx]
                xt_ready = [DV.last(), AC.last()]

                def choose(e):
                    nonlocal t3
                    for j in range(2):
                        ts(DV, sel[e % 2][:, j, :], iota, pos[:, 8 * j + e:8 * j + e + 1], s8[:, j, e:e + 1], ALU.is_equal, MUL, xg.get(("read", e - 2)))
                    for j in range(2):
                        t = ts(DV, gsel[:, j, :], sel[e % 2][:, j, :], gt[:, j, e:e + 1], None, MUL, None, gt_tok.get(("read", e - 1)))
                    for j in range(2):
                        tok = tr(PS[:, 3, 128 * j:128 * j + 128], gsel[:, j, :], t, *t3, inc=j == 1)
                    gt_tok["read", e] = tok
                    gt_tok[e] = cp(AC, GT[e % 2], PS[:, 3, 0:256], tok, fin.get(e - 2))
                    t3 = [gt_tok[e]]
                    gt_tok["sel", e] = t

                def gather(e):
                    nonlocal misc
                    for d in range(8):
                        for j in range(2):
                            tok = mm(PS[:, 6 + d // 4, 128 * (d % 4):128 * (d % 4) + 128], XT[:, j, 128 * d:128 * d + 128], sel[e % 2][:, j, :],
                                     j == 0, j == 1, *(misc + xt_ready + [gt_tok["sel", e]]), inc=d + j == 8)
                    xg["read", e] = tok
                    src = PS[:, 6:8, :]
                    h, l = (v[e % 2][:, 0:1024].rearrange("p (a b) -> p a b", a=2) for v in (xh, xl))
                    fr = [xg.get(("used", e - 2)), *xfree[e % 2]]
                    t = cp(AC, h, src, tok, *fr)
                    xg[e] = tt(DV, l, src, f32(h), SUB, t, *fr)
                    misc = [xg[e]]

                def up(u, half):
                    e = u // NF
                    wh, wl = gate_up(u)
                    b = u % 2
                    h, l = (v[e % 2][:, 0:1024].rearrange("p (k t) -> p k t", k=8) for v in (xh, xl))
                    for k in range(4 * half, 4 * half + 4):
                        tok = mm3(PS[:, b, 0:256], h[:, k, :], l[:, k, :], wh[:, k, :], wl[:, k, :], k == 0, k == 7,
                                  w.lo[u, half], xg[e], *gfree[b], inc=k % 4 == 3)
                    xg["used", e] = hr[u] = tok

                def glu(u):
                    s = sg[u % 2]
                    b = u % 2
                    t = act(s[:, 0, :], PS[:, b, 0:128], ACT.Sigmoid, hr[u], hs.get(u - 2))
                    return t

                def glu2(u, t):
                    s, b = sg[u % 2], u % 2
                    tt(DV, s[:, 1, :], PS[:, b, 0:128], s[:, 0, :], MUL, t)
                    hs[u] = tt(DV, s[:, 2, :], PS[:, b, 128:256], s[:, 1, :], MUL, hd.get(("t", u - 2)))
                    gfree[b] = [hs[u]]

                def turn_h(u):
                    c = slice(128 * (u % 2), 128 * (u % 2) + 128)
                    tok = hd["t", u] = tr(PS[:, 2, c], sg[u % 2][:, 2, :], hs[u], *tfree[u % 2], inc=True)
                    hd["hi", u] = cp(AC, H["h"][:, u % 3, 0:128], PS[:, 2, c], tok, w.down.get(u - 3))

                def low_h(u):
                    c = slice(128 * (u % 2), 128 * (u % 2) + 128)
                    hd[u] = tt(DV, H["l"][:, u % 3, 0:128], PS[:, 2, c], f32(H["h"][:, u % 3, 0:128]), SUB, hd["hi", u], w.down.get(u - 3))
                    tfree[u % 2] = [hd[u]]

                def down(u):
                    e, f = divmod(u, NF)
                    wh, wl = down_of(u)
                    for n in range(2):
                        q = slice(512 * n, 512 * n + 512)
                        tok = mm3(PS[:, 4 + n, :], H["h"][:, u % 3, 0:128], H["l"][:, u % 3, 0:128], wh[:, q], wl[:, q], f == 0, f == NF - 1,
                                  hd[u], w.lo[u, 1], w.lo[u, 2], *(dfree if f == 0 else []), inc=n == 1)
                    w.down[u] = tok

                def keep(e):
                    nonlocal dfree
                    t = cp(AC, OE.rearrange("p (n c) -> p n c", n=2), PS[:, 4:6, :], w.down[e * NF + NF - 1], fin.get(e - 1))
                    dfree = [t]
                    hd["out", e] = t

                def scatter(e, j):
                    nonlocal misc
                    for n in range(2):
                        tok = mm(PS[:, 6 + n, :], GT[e % 2][:, 128 * j:128 * j + 128], OE[:, 512 * n:512 * n + 512], True, True,
                                 hd["out", e], gt_tok[e], *misc, inc=n == 1)
                    if j:
                        fin[e] = tok
                    y = YA[:, j, :].rearrange("p (n c) -> p n c", n=2)
                    t = cp(DV, y, PS[:, 6:8, :], tok) if e == 0 else tt(DV, y, y, PS[:, 6:8, :], ADD, tok)
                    misc = [t]

                choose(0)
                gather(0)
                w.block(0)
                for u in range(NU + 1):
                    e, f = divmod(u, NF)
                    w.high(u + 1, 0)
                    w.low(u + 1, 0)
                    if u < NU:
                        up(u, 0)
                    if u:
                        turn_h(u - 1)
                    w.high(u + 1, 1)
                    if u:
                        low_h(u - 1)
                    w.low(u + 1, 1)
                    if u < NU:
                        up(u, 1)
                    if u:
                        down(u - 1)
                    if u < NU:
                        t = glu(u)
                    w.high(u + 1, 2)
                    w.low(u + 1, 2)
                    if u < NU:
                        glu2(u, t)
                    if u and f == 0:
                        keep(e - 1)
                    if e and e <= NE and f in (1, 4):
                        scatter(e - 1, int(f == 4))
                    if e + 1 < NE and f == 8:
                        choose(e + 1)
                    if e + 1 < NE and f == 12:
                        gather(e + 1)
                scatter(NE - 1, 0)
                scatter(NE - 1, 1)

            def many():
                nonlocal o
                o = rest_o
                NH = 3
                w = Way()
                H = hidden("moe", T)
                hf = [take(T) for _ in range(NH)]
                sg = [take(2, T) for _ in range(2)]
                x = xset(0, 8, T)
                for k in range(0, 8, 2):
                    split_x(x, Xm[:, k:k + 2, :], k, k + 2, *bar)
                gfree = [list(bar) for i in range(4)]
                dfree = list(bar)
                hold = {}

                def up(u):
                    b = u % 4
                    wh, wl = gate_up(u)
                    for g in range(2):
                        c = slice(128 * g, 128 * g + 128)
                        for k in range(8):
                            tok = mm3(PS[:, b, T * g:T * g + T], wh[:, k, c], wl[:, k, c], x["h"][:, k, :], x["l"][:, k, :], k == 0, k == 7,
                                      w.lo[u, 0], w.lo[u, 1], *([x["tok"][k]] if u == 0 else []), *gfree[b], inc=k == 7)
                    s = sg[u % 2]
                    t = act(s[:, 0, :], PS[:, b, 0:T], ACT.Sigmoid, tok, hold.get(u - 2))
                    t = tt(DV, s[:, 1, :], PS[:, b, 0:T], s[:, 0, :], MUL, t)
                    t = hold[u] = tt(DV, hf[u % NH], PS[:, b, T:2 * T], s[:, 1, :], MUL, hold.get(("split", u - NH)))
                    gfree[b] = [t]
                    hold["split", u] = split_hidden(H, u % NH, hf[u % NH], t, w.down.get(u - NH))

                def down(u):
                    nonlocal dfree
                    e, f = divmod(u, NF)
                    wh, wl = down_of(u)
                    i = u % NH
                    for j in range(2):
                        c = slice(128 * j, 128 * j + 128)
                        for n in range(2):
                            q = slice(512 * n, 512 * n + 512)
                            tok = mm3(PS[:, 4 + 2 * j + n, :], H["h"][:, i, c], H["l"][:, i, c], wh[:, q], wl[:, q],
                                      f == 0, f == NF - 1, hold["split", u], w.lo[u, 2], *(dfree if f == 0 else []), inc=j + n == 2)
                    w.down[u] = tok
                    if f == NF - 1:
                        for j in range(2):
                            y = YA[:, j, :].rearrange("p (n c) -> p n c", n=2)
                            src = PS[:, 4 + 2 * j:6 + 2 * j, :]
                            g = gt[:, j, e:e + 1]
                            if e == 0:
                                t = ts(DV, y, src, g, None, MUL, None, tok)
                            else:
                                t = stt(DV, y, src, g, y, MUL, ADD, tok)
                        dfree = [t]

                w.block(0)
                for u in range(NU + 1):
                    w.block(u + 1)
                    if u < NU:
                        up(u)
                    if u:
                        down(u - 1)

            ENG = (PE, DV, AC, PO)
            for E in ENG:
                E.way_begin(flag_t[0:1, 0:1], *bar)
            few()
            for E in ENG:
                E.way_else()
            many()
            for E in ENG:
                E.way_end()
            for u in range(NU):
                state["freed"][blk0 + u] = [(s_fd, u + 1), (s_fp, u + 1)]
            state["tile"] += 2 * NU
            state["next"] = blk0 + NU
            bar = done()
            state["gate"] = bar
            held[:] = [None] * 3
            xfree[0] = xfree[1] = bar
            for i in range(8):
                release(i, *bar)
            o = rest_o
            split_ahead()
            R, tmp, small = take(8, T), take(8, T), take(T)
            for d in range(8):
                b, fr = bank()
                for j in range(2):
                    tok = tr(PS[:, b, 128 * j:128 * j + 128], YA[:, j, 128 * d:128 * d + 128], *(fr + bar), inc=j == 1)
                t = stt(DV, R[:, d, :], Xm[:, d, :], ALPHA, PS[:, b, 0:T], MUL, ADD, tok, *bar)
                release(b, t)
            layer_norm(R, cut(xt, 0, 8, T), tmp, small, T, "ln_g11", "ln_b11", None, *done())

        phases.append(moe)

        X2 = cut(xt, 0, 8, T)

        def even():
            TMP, HN = at(0, 8, T), at(XA, 8, T)
            KQV = at(2 * XA, 2, 1568)
            o = 2 * XA + 3136
            CQ, CN = at(o, 5, T), at(o + 5 * T, 5, T)
            QF = at(o, 8, T)
            o += 10 * T
            RG = at(o, 4, T)
            o += 4 * T
            QM, KM = at(o, 2, 8, 96), at(o + 1536, 2, 8, 96)
            pool_o = o
            o += 3072
            VM = at(o, 2, 8, 64)
            o += 1024
            KF = at(o, 8, T)
            o += XA
            small = at(o, T)
            o += T
            posf = at(o, 8)
            o += 8
            tw = [at(o + 64 * i, 2, 32) for i in range(3)]
            o += 192
            tabs = {}
            bar = done()
            cp(DV, posf[:, 0:2], pos_t[:, 0:2], IN_POS, *bar)
            for hlf in (16, 32):
                for fn, ph in (("sin", 0.0), ("cos", 0.25)):
                    tab = at(o, 2, hlf)
                    o += 2 * hlf
                    a, n_, r = (v[:, :, 0:hlf] for v in tw)
                    for j in range(2):
                        ts(DV, a[:, j, :], con(f"inv{hlf}"), posf[:, j:j + 1], None, MUL, None, IN_CON, AC.last())
                    ts(DV, n_, a, 1.0 / (2 * np.pi), ph, MUL, ADD)
                    ts(DV, n_, n_, 12582912.0, None, ADD, None)
                    ts(DV, n_, n_, 12582912.0, None, SUB, None)
                    stt(DV, r, n_, -6.28125, a, MUL, ADD)
                    stt(DV, r, n_, -float(np.float32(2 * np.pi - 6.28125)), r, MUL, ADD)
                    ts(DV, r, r, 2 * np.pi * ph, None, ADD, None)
                    ts(DV, r, r, 3.1415925, -3.1415925, ALU.min, ALU.max)
                    act(tab, r, ACT.Sin, DV.last(), *bar)
                    tabs[fn, hlf] = tab
            lgm = at(o, 8, 8)
            o += 64
            for i, n in enumerate(("th_f", "th_b")):
                y, u, d, l = (lgm[:, 4 * i + k, :] for k in range(4))
                t = act(y, par(n), ACT.Exp, IN_PAR, *bar, scale=-float(np.log(2.0)))
                ts(DV, u, y, -1.0, 1.0, MUL, ADD, t)
                t = stt(DV, d, u, -1.0, y, ADD, ADD)
                t = act(l, u, ACT.Ln, t)
                rec(u, u, t)
                tt(DV, d, d, u, MUL)
                tt(DV, l, l, d, SUB)
            lgf, lgb = lgm[:, 3, :], lgm[:, 7, :]
            x = rms_norm(X2, HN, TMP, small, 8, T, "n_even", "o1024", 1, *bar)
            linear("e_c", 5, x, T, lambda e, ps, tok: cp(AC, CQ[:, e, :], ps, tok, *bar))
            linear_t("e_t", 5, x, SP2, lambda i, j, ps, tok: cp(
                AC if j else DV, KQV[:, j, E_T[i][0] - 640:E_T[i][0] - 640 + E_T[i][1]], ps, tok))
            KRO, RQK, RV = KQV[:, :, 0:32], KQV[:, :, 32:1056], KQV[:, :, 1056:1568]

            rt = cut(arena, 0, 4, 8, 32)
            rt2 = cut(arena, 1280, 4, 8, 32)

            def rope(E, w4, v, h, hlf, j, *waits):
                c = bc(tabs["cos", hlf][:, j, None, :], h, hlf)
                s = bc(tabs["sin", hlf][:, j, None, :], h, hlf)
                x1, x2 = v[:, :, 0:hlf], v[:, :, hlf:2 * hlf]
                w = [w4[:, i, 0:h, 0:hlf] for i in range(4)]
                tt(E, w[0], x1, c, MUL, *waits)
                tt(E, w[1], x2, s, MUL)
                tt(E, w[2], x2, c, MUL)
                tt(E, w[3], x1, s, MUL)
                tt(E, x1, w[0], w[1], SUB)
                return tt(E, x2, w[2], w[3], ADD)

            bar = done()
            for half in range(2):
                for j in range(2):
                    v = RQK[:, j, 512 * half:512 * half + 512].rearrange("p (h c) -> p h c", h=8)
                    rope(PO, rt2, v, 8, 32, j, *bar)
            ts(PO, RQK[:, :, 512:1024], RQK[:, :, 512:1024], 64.0 ** -0.5, None, MUL, None)

            def rg(e, ps, tok):
                t = act(TMP[:, e, :], ps, ACT.Sigmoid, tok, *bar)
                return tt(DV, RG[:, e, :], ps, TMP[:, e, :], MUL, t, *bar)

            linear("e_g", 4, x, T, rg)
            bar = done(pool=False)
            xc = xset(0, 5, T)
            rms_norm(CQ[:, 0:3, :], CN[:, 0:3, :], TMP[:, 0:3, :], small, 3, T, "n_q", "o384", 0, *bar, x=xc)
            rms_norm(CQ[:, 3:5, :], CN[:, 3:5, :], TMP[:, 3:5, :], small, 2, T, "n_kv", "o256", 0, *done(pool=False), x=xc, k0=3)
            xq = {**xc, "h": xc["h"][:, 0:3, :], "l": xc["l"][:, 0:3, :]}
            linear_t("uq", 2, xq, SP2,
                     lambda i, j, ps, tok: cp(AC, QM[:, j, 4 * i:4 * i + 4, :], ps.rearrange("p (h c) -> p h c", h=4), tok), *done(pool=False))
            xkv = {**xc, "h": xc["h"][:, 3:5, :], "tok": {0: xc["tok"][3], 1: xc["tok"][4]}, "at": 3 * T}

            def kv(i, j, ps, tok):
                v = ps.rearrange("p (h c) -> p h c", h=4)
                cp(AC, KM[:, j, 4 * i:4 * i + 4, 0:64], v[:, :, 0:64], tok)
                return cp(AC, VM[:, j, 4 * i:4 * i + 4, :], v[:, :, 64:128])

            linear_t("ukv", 2, xkv, SP2, kv)
            bar = done(pool=False)
            for j in range(2):
                cp(DV, KM[:, j, :, 64:96], bc(KRO[:, j, None, :], 8, 32), *bar)
            sq = HN.rearrange("p a t -> p (a t)")[:, 512:1280].rearrange("p (h c) -> p h c", h=8)
            ss = small[:, 0:64].rearrange("p (r m h) -> p r m h", r=2, m=4)
            heads = [(M, j, g) for M, g in ((KM, "n_kh"), (QM, "n_qh")) for j in range(2)]
            for i, (M, j, g) in enumerate(heads):
                tt(DV, sq, M[:, j], M[:, j], MUL, *bar)
                red(ss[:, 0, i, :], sq, ADD)
            t = ts(DV, ss[:, 0], ss[:, 0], 1.0 / 96, 1e-6, MUL, ADD)
            t = act(ss[:, 1], ss[:, 0], ACT.Sqrt, t)
            t = rec(ss[:, 1], ss[:, 1], t)
            for i, (M, j, g) in enumerate(heads):
                E, w4 = (PO, rt2) if i == 0 else (DV, rt)
                v = M[:, j]
                tt(E, v, v, bc(ss[:, 1, i, :, None], 8, 96), MUL, t)
                tt(E, v, v, bc(par(g)[:, None, :], 8, 96), MUL)
                rope(E, w4, v[:, :, 64:96], 8, 16, j)
            bar = done()
            RF = HN
            for M, F in ((QM, QF), (KM, KF)):
                for j in range(2):
                    for q in range(2):
                        b, fr = bank()
                        for h in range(4):
                            tok = tr(PS[0:96, b, 128 * h:128 * h + 128], M[:, j, 4 * q + h, :], *(fr + bar), inc=h == 3)
                        release(b, cp(AC, F[0:96, 4 * q:4 * q + 4, 128 * j:128 * j + 128],
                                      PS[0:96, b, :].rearrange("p (h t) -> p h t", h=4), tok))
            for j in range(2):
                for q in range(2):
                    b, fr = bank()
                    for h in range(4):
                        tok = tr(PS[:, b, 128 * h:128 * h + 128], RQK[:, j, 512 * q + 128 * h:512 * q + 128 * h + 128], *(fr + bar), inc=h == 3)
                    release(b, cp(DV, RF[:, 4 * q:4 * q + 4, 128 * j:128 * j + 128], PS[:, b, :].rearrange("p (h t) -> p h t", h=4), tok))
            bar = done()
            P = [at(pool_o + 512 * i, 2, T) for i in range(3)]
            PT = [at(pool_o + 1536 + 512 * i, 2, T) for i in range(2)]
            Dt = [at(pool_o + 512 * i, 2, T) for i in range(3)]
            CA = at(2 * XA, 4, T)
            OR = TMP[:, 0:4, :]
            sm = [at(o + 16 * i, 16) for i in range(3)]
            o += 48
            scale = 96.0 ** -0.5
            got, freeP, freePT, ready, tex = {}, [[], [], []], [[], []], {}, {}
            xo = xset(1, 8, T)

            def mscore(h):
                b, fr = bank()
                for j in range(2):
                    tok = mm(PS[:, b, T * j:T * j + T], QF[0:96, h, 128 * j:128 * j + 128], KF[0:96, h, :], True, True, *(fr + bar), inc=j == 1)
                got[h] = b, tok

            def msoften(h):
                i = h % 3
                b, tok = got[h]
                v = PS[:, b, :].rearrange("p (j t) -> p j t", j=2)
                m = sm[i]
                red(m[:, 0:2], v, MAXO, tok)
                t = ts(DV, m[:, 2:4], m[:, 0:2], -scale, None, MUL, None)
                for j in range(2):
                    t = act(P[i][:, j, :], v[:, j, :], ACT.Exp, t, *freeP[i], bias=m[:, 2 + j:3 + j], scale=scale, accum=m[:, 4 + j:5 + j])
                release(b, t)
                tex[h] = t

            def mweigh(h):
                i = h % 3
                m = sm[i]
                rec(m[:, 6:8], m[:, 4:6], tex[h])
                ready[h] = tt(DV, P[i], P[i], bc(m[:, 6:8, None], 2, T), MUL)

            def mrest(h):
                i, g = h % 3, h % 2
                b, fr = bank()
                v = PS[:, b, :].rearrange("p (k t) -> p k t", k=2)
                for j in range(2):
                    for k in range(2):
                        tok = tr(v[:, k, 128 * j:128 * j + 128], P[i][:, j, 128 * k:128 * k + 128], ready[h], *fr, inc=j + k == 2)
                freeP[i] = [tok]
                t = cp(AC, PT[g], v, tok, *freePT[g])
                release(b, t)
                rows = slice(64 * (h % 2), 64 * (h % 2) + 64)
                b, fr = bank()
                for k in range(2):
                    tok = mm(PS[rows, b, 0:T], VM[:, k, h, :], PT[g][:, k, :], k == 0, k == 1, t, *fr, inc=k == 1)
                freePT[g] = [tok]
                t = cp(AC, CA[rows, h // 2, :], PS[rows, b, 0:T], tok)
                release(b, t)
                if h % 2:
                    split_x(xo, CA[:, h // 2:h // 2 + 1, :], h // 2, h // 2 + 1, t)

            mscore(0)
            for h in range(10):
                if h < 7:
                    mscore(h + 1)
                if h > 1:
                    mrest(h - 2)
                if h < 8:
                    msoften(h)
                if 1 <= h < 9:
                    mweigh(h - 1)
            bar = done()
            rel = KF.rearrange("p a t -> p (a t)")[:, 0:1024]
            CR = QF[:, 0:4, :]
            load(PO, rel, rel_d, s_in["rel"], *bar)
            relp, reln = rel[:, 0:512].rearrange("p (j t) -> p j t", j=2), rel[:, 512:1024].rearrange("p (j t) -> p j t", j=2)
            fin, td, pre, rb = {}, {}, {}, {}

            def decays(h):
                i = h % 3
                ts(DV, Dt[i], reln, lgb[:, h:h + 1], None, MUL, None, fin.get(h - 3), IN_REL, *bar)
                t = stt(DV, Dt[i], relp, lgf[:, h:h + 1], Dt[i], MUL, ADD)
                td[h] = act(Dt[i], Dt[i], ACT.Exp, t)

            def rscore(h):
                rows = slice(64 * (h % 2), 64 * (h % 2) + 64)
                b, fr = bank()
                for j in range(2):
                    tok = mm(PS[:, b, T * j:T * j + T], RF[rows, 4 + h // 2, 128 * j:128 * j + 128], RF[rows, h // 2, :], True, True, *(fr + bar), inc=j == 1)
                rb[h] = b, tok

            def decayed(h):
                b, tok = rb[h]
                t = pre[h] = tt(DV, Dt[h % 3], Dt[h % 3], PS[:, b, :].rearrange("p (j t) -> p j t", j=2), MUL, tok, td[h])
                release(b, t)

            def rvalues(h):
                rows = slice(64 * (h % 2), 64 * (h % 2) + 64)
                b, fr = bank()
                for j in range(2):
                    tok = mm(PS[rows, b, 0:T], RV[:, j, 64 * h:64 * h + 64], Dt[h % 3][:, j, :], j == 0, j == 1, pre[h], *fr, inc=j == 1)
                fin[h] = tok
                release(b, cp(AC, OR[rows, h // 2, :], PS[rows, b, 0:T], tok))

            for h in range(10):
                if h < 8:
                    decays(h)
                if h < 8:
                    rscore(h)
                if 1 <= h < 9:
                    decayed(h - 1)
                if h > 1:
                    rvalues(h - 2)
            bar = done()
            sum_of, last = {}, {}

            def squares(k):
                t = act(TMP[:, 4 + k, :], OR[:, k, :], ACT.Square, *bar)
                sum_of[k] = colsum("blk64", TMP[:, 4 + k:5 + k, :], 1, T, t)

            def roots(k):
                b, tok = sum_of[k]
                t = ts(DV, TMP[:, 4 + k, :], PS[:, b, 0:T], 1e-6, None, ADD, None, tok)
                release(b, t)
                last[k] = act(TMP[:, 4 + k, :], TMP[:, 4 + k, :], ACT.Sqrt, t)

            def scaled(k):
                r = TMP[:, 4 + k, :]
                rec(r, r, last[k])
                stt(DV, CR[:, k, :], OR[:, k, :], par("n_ret")[:, k:k + 1], r, MUL, MUL)
                last[k] = tt(DV, CR[:, k, :], CR[:, k, :], RG[:, k, :], MUL)

            staged(4, squares, roots, scaled, lambda k: split_x(xo, CR[:, k:k + 1, :], 4 + k, 5 + k, last[k]))
            linear("e_o", 8, xo, T, lambda e, ps, tok: tt(DV, X2[:, e, :], X2[:, e, :], ps, ADD, tok))

        phases.append(even)

        def conv_ffn(i):
            ar = arena_of[f"conv{i}"]
            TMP, HN = cut(ar, 0, 8, T), cut(ar, XA, 8, T)
            o = 2 * XA
            small = cut(ar, o, T)
            o += T
            gp = [cut(ar, o + 258 * j, 258) for j in range(2)]
            o += 516
            cv = [cut(ar, o + 256 * j, 256) for j in range(2)]
            o += 512
            sg = [cut(ar, o + 256 * j, 256) for j in range(2)]
            bar = done()
            x = rms_norm(X2, HN, TMP, small, 8, T, f"n_ffn{i}", "o1024", 0, *bar)
            for j in range(2):
                mset(DV, gp[j][:, 0:1], 0.0, *bar)
                tz = mset(DV, gp[j][:, 257:258], 0.0)
            H = hidden(f"conv{i}", T)
            ub = [cut(ar, o + 256 * (2 + j), 256) for j in range(2)]
            hold, cvt, sgt = {}, {}, {}

            def finish(f):
                s = f % 2
                stt(DV, cv[s], cv[s], par(f"cb{i}")[:, f:f + 1], sg[s], ADD, MUL, sgt[f])
                t = tt(DV, cv[s], cv[s], ub[s], MUL)
                hold[f] = split_hidden(H, f, cv[s], t, *bar)

            def evac(e, ps, tok):
                f = e // 2
                s = f % 2
                if e % 2 == 0:
                    t = cp(AC, gp[s][:, 1:257], ps, tok, cvt.get(f - 2), tz)
                    if f:
                        finish(f - 1)
                    return t
                t = cp(AC, ub[s], ps, tok, hold.get(f - 2), *bar)
                ts(DV, cv[s], gp[s][:, 0:256], par(f"cw{i}0")[:, f:f + 1], None, MUL, None, t, hold.get(f - 2))
                stt(DV, cv[s], gp[s][:, 1:257], par(f"cw{i}1")[:, f:f + 1], cv[s], MUL, ADD)
                cvt[f] = stt(DV, cv[s], gp[s][:, 2:258], par(f"cw{i}2")[:, f:f + 1], cv[s], MUL, ADD)
                sgt[f] = act(sg[s], cv[s], ACT.Sigmoid, cvt[f], bias=par(f"cb{i}")[:, f:f + 1])
                return t

            linear(f"cu{i}", 44, x, T, evac)
            finish(21)
            linear(f"cd{i}", 8, H, T, lambda e, ps, tok: tt(DV, X2[:, e, :], X2[:, e, :], ps, ADD, tok))

        phases.append(lambda: conv_ffn(0))

        def odd():
            HN, TMP = at(0, 8, T), at(XA, 8, T)
            o = 2 * XA
            small = at(o, T)
            o += T
            GQ, GK = at(o, 4, T), at(o + 4 * T, 4, T)
            o += 8 * T
            GV = at(o, 2, 1024)
            o += 2048
            LA = [at(o + 4 * T * i, 4, T) for i in range(2)]
            o += 8 * T
            RGo = at(o, 8, T)
            o += 8 * T
            KE = at(o, 4, T)
            QBs = [at(o + 4 * T * (i + 1), 4, T) for i in range(2)]
            o += 12 * T
            KDTs = [v.rearrange("p (j a) t -> p j (a t)", j=2) for v in LA]
            Ss = [v.rearrange("p a t -> p (a t)").rearrange("p (h v) -> p h v", h=4) for v in (GQ, GK)]
            q = 2 * SLOTS * BW + XW
            QC = cut(scan_t, q, 4, T)
            ATs = [cut(scan_t, q + 4 * T + 512 * i, 2, 4, 64) for i in range(2)]
            mid, lsts = at(o, 16), [at(o + 16 + 16 * i, 4, 4) for i in range(2)]
            one = at(o + 48, T)
            o += 48 + T
            bar = done()
            x = rms_norm(X2, HN, TMP, small, 8, T, "n_odd", "o1024", 1, *bar)

            def qk(e, ps, tok):
                if e < 4:
                    return act(GQ[:, e, :], ps, ACT.Copy, tok, *bar, scale=128.0 ** -0.5)
                return cp(AC, GK[:, e - 4, :], ps, tok)

            linear("o_qk", 8, x, T, qk)
            linear_t("o_v", 3, x, SP2, lambda i, j, ps, tok: cp(
                AC if j else DV, GV[:, j, THIRDS[i]:THIRDS[i] + ps.shape[1]], ps, tok, *bar))
            xa = [xset(0, 2, T)]
            ga = at(o, 2, T)

            def lowrank(e, ps, tok):
                t = cp(AC, ga[0:16, e, :], ps, tok, *bar)
                cp(AC, xa[0]["h"][0:16, e, :], ga[0:16, e, :], *xfree[0])
                tt(DV, xa[0]["l"][0:16, e, :], ga[0:16, e, :], f32(xa[0]["h"][0:16, e, :]), SUB, AC.last(), *xfree[0])
                return t

            linear("o_a", 2, x, T, lowrank)
            ready = done()
            wh, wl, wt, closes, _ = weight("gg")
            tmp = TMP[:, 0:4, :]
            ab = TMP[:, 4:8, :]
            for n in range(2):
                for h in range(4):
                    b, fr = bank()
                    c = slice(512 * n + 128 * h, 512 * n + 128 * h + 128)
                    tok = mm3(PS[:, b, 0:T], wh[0:16, 0, c], wl[0:16, 0, c], xa[0]["h"][0:16, n, :], xa[0]["l"][0:16, n, :], True, True,
                              *(fr + wt + ready), inc=True)
                    t = ts(DV, LA[n][:, h, :], PS[:, b, 0:T], par(("b_gf", "b_gb")[n])[:, h:h + 1], None, ADD, None, tok, *bar)
                    release(b, t)
                act(ab, LA[n], ACT.Abs, t)
                act(ab, ab, ACT.Exp, scale=-1.0)
                t = act(ab, ab, ACT.Ln, bias=1.0)
                stt(DV, LA[n], LA[n], 0.0, ab, ALU.min, SUB, t)
                ts(DV, LA[n], LA[n], 1.0 / 16, None, MUL, None)
            used(closes, tok)
            xfree[0] = [tok]
            bar = done()

            def rg(e, ps, tok):
                t = act(TMP[:, e, :], ps, ACT.Sigmoid, tok, *bar)
                return tt(DV, RGo[:, e, :], ps, TMP[:, e, :], MUL, t, *bar)

            linear("o_g", 8, x, T, rg)
            bar = done()
            mset(DV, one, 1.0, *bar)
            mset(DV, one.rearrange("p (c t) -> p c t", c=4)[:, :, 0:1], 0.0)
            Bc = KC = TMP[:, 0:4, :]
            Ex = TMP[:, 4:8, :]
            OG = HN

            def c4(v):
                return v.rearrange("p a (c t) -> p (a c) t", c=4)

            tKs, tAs = {}, {}
            for n in range(2):
                bar = done()
                QB, KDT, AT, lst = QBs[n], KDTs[n], ATs[n], lsts[n]
                for h in range(4):
                    cum, la_ = Bc[:, h, :], LA[n][:, h, :]
                    if n == 1:
                        cum, la_ = cum[:, ::-1], la_[:, ::-1]
                    DV(lambda e, a=cum, l=la_: e.tensor_tensor_scan(a, one, l, 0.0, MUL, ADD), *bar)
                mi, la = (32, 63) if n == 0 else (31, 0)
                bm = c4(Bc)[:, :, mi:mi + 1]
                bl = c4(Bc)[:, :, la:la + 1]
                t = act(Ex, Bc, ACT.Exp, DV.last())
                tt(DV, QB, GQ, Ex, MUL, t)
                act(lst.rearrange("p a c -> p (a c)"), bl[:, :, 0], ACT.Exp, DV.last())
                t = tt(DV, c4(Ex), bc(bl, 16, 64), c4(Bc), SUB, t)
                t = act(Ex, Ex, ACT.Exp, t)
                tt(DV, KE, GK, Ex, MUL, t)
                cp(DV, mid, bm[:, :, 0])
                t = tt(DV, c4(Bc), c4(Bc), bc(mid[:, :, None], 16, 64), SUB, AC.last())
                t = act(Ex, Bc, ACT.Exp, t)
                tt(DV, QC, GQ, Ex, MUL, t)
                t = act(Ex, Bc, ACT.Exp, DV.last(), scale=-1.0)
                tt(DV, KC, GK, Ex, MUL, t)
                mset(DV, AT, 0.0)
                bar = done()
                b, fr = bank()
                for c in range(4):
                    rows = slice(64 * (c % 2), 64 * (c % 2) + 64)
                    for h in range(4):
                        k = 256 * (c // 2) + 64 * h
                        tok = mm(PS[rows, b, k:k + 64], KC[:, h, 64 * c:64 * c + 64], QC[:, h, 64 * c:64 * c + 64], True, True,
                                 *(fr + bar), inc=c * h == 9)
                ATf = AT.rearrange("p c h t -> p (c h) t")
                tA = tAs[n] = DV(lambda e, b=b, n=n, ATf=ATf: e.copy_predicated(ATf, bc(con(f"gm{n}")[:, None, :], 8, 64).bitcast(u32),
                                                              PS[:, b, :].rearrange("p (k t) -> p k t", k=8)), tok)
                release(b, tA)
                for j in range(2):
                    b, fr = bank()
                    for h in range(4):
                        tok2 = tr(PS[:, b, 128 * h:128 * h + 128], KE[:, h, 128 * j:128 * j + 128], *(fr + bar), inc=h == 3)
                    tKs[n] = cp(AC, KDT[:, j, :], PS[:, b, :], tok2)
                    release(b, tKs[n])
            bar = done()
            tS = [None, None]
            for ci in range(4):
                for n in range(2):
                    c = ci if n == 0 else 3 - ci
                    QB, KDT, AT, lst, S = QBs[n], KDTs[n], ATs[n], lsts[n], Ss[n]
                    rows = slice(64 * (c % 2), 64 * (c % 2) + 64)
                    j = c // 2
                    b, fr = bank()
                    for h in range(4):
                        for v in range(2):
                            out = PS[:, b, 128 * h + 64 * v:128 * h + 64 * v + 64]
                            mm(out, GV[rows, j, 256 * h + 128 * v:256 * h + 128 * v + 128], AT[rows, j, h, :], True, ci == 0, tAs[n], *fr)
                            if ci:
                                mm(out, S[:, h, 128 * v:128 * v + 128], QB[:, h, 64 * c:64 * c + 64], False, True, tS[n])
                    bs, fs = bank(2)
                    for h in range(4):
                        tok = mm(PS[:, bs + h // 2, 256 * (h % 2):256 * (h % 2) + 256], KDT[rows, j, 128 * h:128 * h + 128],
                                 GV[rows, j, 256 * h:256 * h + 256], True, True, tKs[n], *fs, inc=h == 3)
                    src = PS[:, b, :].rearrange("p (k t) -> p k t", k=8)
                    dst = OG[:, :, 64 * c:64 * c + 64]
                    t = cp(DV, dst, src, tok) if ci < 2 else tt(DV, dst, dst, src, ADD, tok)
                    release(b, t)
                    for h in range(4):
                        st = PS[:, bs + h // 2, 256 * (h % 2):256 * (h % 2) + 256]
                        if ci == 0:
                            tS[n] = cp(DV, S[:, h, :], st, *bar)
                        else:
                            tS[n] = stt(DV, S[:, h, :], S[:, h, :], lst[:, h, c:c + 1], st, MUL, ADD)
                    release(bs, tS[n], n=2)
            bar = done()
            xo = xset(0, 8, T)
            sum_of, last = {}, {}

            def squares(h):
                t = act(TMP[:, 2 * h:2 * h + 2, :], OG[:, 2 * h:2 * h + 2, :], ACT.Square, *bar)
                sum_of[h] = colsum("o256", TMP[:, 2 * h:2 * h + 2, :], 2, T, t)

            def roots(h):
                b, tok = sum_of[h]
                t = ts(DV, TMP[:, 2 * h, :], PS[:, b, 0:T], 1e-6, None, ADD, None, tok)
                release(b, t)
                last[h] = act(TMP[:, 2 * h, :], TMP[:, 2 * h, :], ACT.Sqrt, t)

            def scaled(h):
                r = TMP[:, 2 * h, :]
                rec(r, r, last[h])
                for k in (2 * h, 2 * h + 1):
                    stt(DV, OG[:, k, :], OG[:, k, :], par("n_gla")[:, k:k + 1], r, MUL, MUL)
                    last[h] = tt(DV, OG[:, k, :], OG[:, k, :], RGo[:, k, :], MUL)

            staged(4, squares, roots, scaled, lambda h: split_x(xo, OG[:, 2 * h:2 * h + 2, :], 2 * h, 2 * h + 2, last[h]))
            linear("o_o", 8, xo, T, lambda e, ps, tok: tt(DV, X2[:, e, :], X2[:, e, :], ps, ADD, tok))

        phases.append(odd)
        phases.append(lambda: conv_ffn(1))

        for i, ph in enumerate(phases):
            if i < stop:
                ph()

        load(SP, xt[:, :].rearrange("p (n t) -> p n t", n=8), x_d, s_in["x"])
        nb = state["next"]
        off = 0
        for bi in range(nb):
            w = blocks[bi][1]
            src = ws_d[off:off + 128 * w].rearrange("(p w) -> p w", p=128)
            off += 128 * w
            load(SP, ring[:, bi % RING, 0:w], src, s_w[bi % RING], *(state["freed"][bi - RING] if bi >= RING else []))
            if bi == 1:
                load(SP, con_t[:, :], con_d, s_in["con"])
                load(SP, par_t[:, :], par_d, s_in["par"])
                load(SP, pos_t[:, 0:2], pos_d, s_in["pos"])
        if stop > len(phases):
            load(SP, out_d, X2, s_out, *done())
            SP(None, (s_out, 16), inc=False, chain=False)

        block = ctx.enter_context(nc.Block())

        @block.sync
        def _(e):
            SP.emit(e)

        @block.tensor
        def _(e):
            PE.emit(e)

        @block.vector
        def _(e):
            DV.emit(e)

        @block.scalar
        def _(e):
            AC.emit(e)

        @block.gpsimd
        def _(e):
            PO.emit(e)


def host_inputs(inp):
    inp = {k: np.asarray(v) for k, v in inp.items()}
    h = np.concatenate([inp["meta"], inp["x"][0]], axis=0)
    return {
        "x_d": np.ascontiguousarray(h.T.reshape(8, 128, T0).transpose(1, 0, 2)),
        "ws_d": pack_stream(inp),
        "par_d": pack(params(), inp),
        "con_d": pack(consts(), inp),
        **{n: pack(f(), inp) for n, f in SETS.items()},
        "pos_d": np.ascontiguousarray(inp["positions_2"].reshape(2, 128).T),
    }


def kernel(**inputs):
    import concourse.bacc as bacc
    from concourse.bass_utils import run_bass_kernel_spmd as run
    arrays = host_inputs(inputs)
    nc = bacc.Bacc("TRN2", target_bir_lowering=False, num_devices=1)
    aps = {n: nc.dram_tensor(n, a.shape, mybir.dt.from_np(a.dtype), kind="ExternalInput").ap() for n, a in arrays.items()}
    out = nc.dram_tensor("out_d", (128, 8, T1), mybir.dt.float32, kind="ExternalOutput").ap()
    build(nc, out_d=out, **aps)
    r = run(nc, [arrays], core_ids=[0])
    got = r.results[0]["out_d"]
    return np.ascontiguousarray(got.transpose(1, 0, 2).reshape(D, T1).T).reshape(1, T1, D)
```
